# Optimizing a Trainium2 kernel written in Bass

```python
import jax, jax.numpy as jnp
from jax import lax
import numpy as np

D_MODEL = 1024
BATCH = 1
SEQ = 256
DEPTH = 2

MEM_LEN = 256
GROUP_WIDTH = D_MODEL // 2
D_MIX = 3 * GROUP_WIDTH
MOBA_HEAD_DIM = 64
MOBA_HEADS = GROUP_WIDTH // MOBA_HEAD_DIM
MOBA_BLOCK = 256
MOBA_TOPK = 3
MOBA_Q_CHUNK = 16
HGRN_HEAD_DIM = 128
HGRN_HEADS = GROUP_WIDTH // HGRN_HEAD_DIM
HGRN_CHUNK = 64
MEM_HEAD_DIM = 128
MEM_HEADS = GROUP_WIDTH // MEM_HEAD_DIM
ROPE_THETA = 500000.0
ROPE_DIM = MOBA_HEAD_DIM // 4
NORM_EPS = 1e-6
IN_COLS = 3 * GROUP_WIDTH + 3 * GROUP_WIDTH + GROUP_WIDTH + D_MIX


def rms_norm(x, g):
    xf = x.astype(jnp.float32)
    y = xf * lax.rsqrt(jnp.mean(xf * xf, axis=-1, keepdims=True) + NORM_EPS)
    return (y * g.astype(jnp.float32)).astype(x.dtype)

def partial_rope(x, positions):
    half = ROPE_DIM // 2
    inv_freq = ROPE_THETA ** (-jnp.arange(half, dtype=jnp.float32) / half)
    ang = positions.astype(jnp.float32)[..., None] * inv_freq
    cos = jnp.cos(ang)[:, :, None, :]
    sin = jnp.sin(ang)[:, :, None, :]
    xr = x[..., :ROPE_DIM].astype(jnp.float32)
    x1, x2 = xr[..., :half], xr[..., half:]
    rot = jnp.concatenate([x1 * cos - x2 * sin, x2 * cos + x1 * sin], axis=-1).astype(x.dtype)
    return jnp.concatenate([rot, x[..., ROPE_DIM:]], axis=-1)

def moba_attention(q, k, v):
    B, S, H, D = q.shape
    BLK, QC = MOBA_BLOCK, MOBA_Q_CHUNK
    nb = -(-S // BLK)
    pad = nb * BLK - S
    topk = min(MOBA_TOPK, nb)
    kbh = jnp.pad(k, ((0, 0), (0, pad), (0, 0), (0, 0))).reshape(B, nb, BLK, H, D).transpose(0, 3, 1, 2, 4)
    vbh = jnp.pad(v, ((0, 0), (0, pad), (0, 0), (0, 0))).reshape(B, nb, BLK, H, D).transpose(0, 3, 1, 2, 4)
    kmean = jnp.mean(kbh.astype(jnp.float32), axis=3)
    scale = D ** -0.5
    nqc = S // QC
    qch = q.reshape(B, nqc, QC, H, D).transpose(1, 0, 3, 2, 4)
    bi = jnp.arange(B)[:, None, None, None]
    hi = jnp.arange(H)[None, :, None, None]
    blk_ids = jnp.arange(nb)

    def one_chunk(args):
        ci, qi = args
        start = ci * QC
        own = start // BLK
        qpos = start + jnp.arange(QC)
        gate = jnp.einsum('bhqd,bhnd->bhqn', qi.astype(jnp.float32), kmean)
        gate = jnp.where(blk_ids < own, gate, -jnp.inf)
        _, sel = lax.top_k(gate, topk)
        sel_ok = sel < own
        k_sel = kbh[bi, hi, sel]
        v_sel = vbh[bi, hi, sel]
        s_sel = jnp.einsum('bhqd,bhqkld->bhqkl', qi, k_sel).astype(jnp.float32) * scale
        s_sel = jnp.where(sel_ok[..., None], s_sel, -jnp.inf).reshape(B, H, QC, topk * BLK)
        k_own = lax.dynamic_index_in_dim(kbh, own, axis=2, keepdims=False)
        v_own = lax.dynamic_index_in_dim(vbh, own, axis=2, keepdims=False)
        kpos = own * BLK + jnp.arange(BLK)
        s_own = jnp.einsum('bhqd,bhld->bhql', qi, k_own).astype(jnp.float32) * scale
        s_own = jnp.where(kpos[None, :] <= qpos[:, None], s_own, -jnp.inf)
        p = jax.nn.softmax(jnp.concatenate([s_sel, s_own], axis=-1), axis=-1).astype(v.dtype)
        p_sel = p[..., :topk * BLK].reshape(B, H, QC, topk, BLK)
        p_own = p[..., topk * BLK:]
        return (jnp.einsum('bhqkl,bhqkld->bhqd', p_sel, v_sel)
                + jnp.einsum('bhql,bhld->bhqd', p_own, v_own))

    o = lax.map(one_chunk, (jnp.arange(nqc), qch))
    return o.transpose(1, 0, 3, 2, 4).reshape(B, S, H, D)

def hgrn2_chunkwise(q, f_logit, i, lb):
    B, S, H, DK = q.shape
    DV = i.shape[-1]
    C = HGRN_CHUNK
    NC = S // C
    fl = f_logit.astype(jnp.float32)
    qf = jax.nn.silu(q.astype(jnp.float32))
    log_f = jnp.logaddexp(jnp.log(lb), jnp.log1p(-lb) + jax.nn.log_sigmoid(fl))
    kf = (1.0 - lb) * jax.nn.sigmoid(-fl)
    vf = i.astype(jnp.float32)

    def to_chunks(t):
        return t.reshape(B, NC, C, H, t.shape[-1]).transpose(1, 0, 3, 2, 4)

    causal = jnp.tril(jnp.ones((C, C), dtype=bool))

    def step(state, inp):
        qc, lfc, kc, vc = inp
        A = jnp.cumsum(lfc, axis=2)
        diff = A[:, :, :, None, :] - A[:, :, None, :, :]
        decay = jnp.exp(jnp.where(causal[:, :, None], diff, -jnp.inf))
        scores = jnp.einsum('bhtd,bhtsd,bhsd->bhts', qc, decay, kc)
        o = (jnp.einsum('bhts,bhsv->bhtv', scores, vc)
             + jnp.einsum('bhtd,bhdv->bhtv', qc * jnp.exp(A), state))
        A_end = A[:, :, -1:, :]
        state = (jnp.exp(A_end[:, :, 0, :])[..., None] * state
                 + jnp.einsum('bhsd,bhsv->bhdv', kc * jnp.exp(A_end - A), vc))
        return state, o

    s0 = jnp.zeros((B, H, DK, DV), jnp.float32)
    _, o = lax.scan(step, s0, (to_chunks(qf), to_chunks(log_f), to_chunks(kf), to_chunks(vf)))
    return o.transpose(1, 0, 3, 2, 4).reshape(B, S, H, DV)

def memory_attention(q, k, v):
    scale = q.shape[-1] ** -0.5
    s = jnp.einsum('bshd,bmhd->bhsm', q, k).astype(jnp.float32) * scale
    p = jax.nn.softmax(s, axis=-1).astype(v.dtype)
    return jnp.einsum('bhsm,bmhd->bshd', p, v)

def first_inputs(seed: int = 0) -> dict:
    key = jax.random.key(seed)
    ks = jax.random.split(key, 14)
    f32 = jnp.float32

    def gain(k, shape):
        return 1.0 + 0.02 * jax.random.normal(k, shape, f32)

    return {
        "x": jax.random.normal(ks[0], (BATCH, SEQ, D_MODEL), f32),
        "mem": jax.random.normal(ks[1], (BATCH, MEM_LEN, D_MODEL), f32),
        "positions": jnp.tile(jnp.arange(SEQ, dtype=jnp.int32)[None, :], (BATCH, 1)),
        "norm_g": gain(ks[2], (DEPTH, D_MODEL)),
        "w_in": jax.random.normal(ks[3], (DEPTH, D_MODEL, IN_COLS), f32) * D_MODEL ** -0.5,
        "w_out": jax.random.normal(ks[4], (DEPTH, D_MIX, D_MODEL), f32) * D_MIX ** -0.5,
        "moba_q_norm": gain(ks[5], (DEPTH, MOBA_HEAD_DIM)),
        "moba_k_norm": gain(ks[6], (DEPTH, MOBA_HEAD_DIM)),
        "hgrn_lb_logits": 0.5 * jax.random.normal(ks[7], (DEPTH, GROUP_WIDTH), f32),
        "hgrn_o_norm": gain(ks[8], (DEPTH, HGRN_HEAD_DIM)),
        "mem_norm_g": gain(ks[9], (DEPTH, D_MODEL)),
        "w_mem_kv": jax.random.normal(ks[10], (DEPTH, D_MODEL, 2 * GROUP_WIDTH), f32) * D_MODEL ** -0.5,
        "mem_q_norm": gain(ks[11], (DEPTH, MEM_HEAD_DIM)),
        "mem_k_norm": gain(ks[12], (DEPTH, MEM_HEAD_DIM)),
    }

def first_block(x, mem, positions, norm_g, w_in, w_out, moba_q_norm, moba_k_norm, hgrn_lb_logits,
              hgrn_o_norm, mem_norm_g, w_mem_kv, mem_q_norm, mem_k_norm):
    B, S, _ = x.shape
    M = mem.shape[1]
    G = GROUP_WIDTH
    lb_all = jnp.cumsum(jax.nn.softmax(hgrn_lb_logits.astype(jnp.float32), axis=0), axis=0)
    lb_all = lb_all - lb_all[0:1]
    split_points = [G * n for n in range(1, 8)]
    for l in range(DEPTH):
        h = rms_norm(x, norm_g[l])
        proj = h @ w_in[l]
        q_a, k_a, v_a, q_h, f_h, i_h, q_m, z = jnp.split(proj, split_points, axis=-1)

        qa = partial_rope(rms_norm(q_a.reshape(B, S, MOBA_HEADS, MOBA_HEAD_DIM), moba_q_norm[l]), positions)
        ka = partial_rope(rms_norm(k_a.reshape(B, S, MOBA_HEADS, MOBA_HEAD_DIM), moba_k_norm[l]), positions)
        va = v_a.reshape(B, S, MOBA_HEADS, MOBA_HEAD_DIM)
        o_a = moba_attention(qa, ka, va).reshape(B, S, G)

        o_h = hgrn2_chunkwise(q_h.reshape(B, S, HGRN_HEADS, HGRN_HEAD_DIM),
                              f_h.reshape(B, S, HGRN_HEADS, HGRN_HEAD_DIM),
                              i_h.reshape(B, S, HGRN_HEADS, HGRN_HEAD_DIM),
                              lb_all[l].reshape(HGRN_HEADS, HGRN_HEAD_DIM))
        o_h = rms_norm(o_h, hgrn_o_norm[l]).astype(x.dtype).reshape(B, S, G)

        kv_m = rms_norm(mem, mem_norm_g[l]) @ w_mem_kv[l]
        k_m, v_m = jnp.split(kv_m, 2, axis=-1)
        km = rms_norm(k_m.reshape(B, M, MEM_HEADS, MEM_HEAD_DIM), mem_k_norm[l])
        vm = v_m.reshape(B, M, MEM_HEADS, MEM_HEAD_DIM)
        qm = rms_norm(q_m.reshape(B, S, MEM_HEADS, MEM_HEAD_DIM), mem_q_norm[l])
        o_m = memory_attention(qm, km, vm).reshape(B, S, G)

        y = jnp.concatenate([o_a, o_h, o_m], axis=-1) * jax.nn.silu(z)
        x = x + y @ w_out[l]
    return x


CHUNK = 64
RMS_EPS = 1e-6
DN_HEADS = 4
DN_DK = 128
DN_DV = 128
DN_CONV = 4
DN_QKV = 2 * DN_HEADS * DN_DK + DN_HEADS * DN_DV
DN_VAL = DN_HEADS * DN_DV
RET_HEADS = 4
RET_DK = 128
RET_DV = 128
RET_QK = RET_HEADS * RET_DK
RET_VAL = RET_HEADS * RET_DV
ROPE_BASE = 10000.0
GN_EPS = 1e-5
POOL_WINDOWS = (2, 4, 8, 16)
POOL_GROUPS = 4
POOL_GROUP = 128
POOL_WIDTH = POOL_GROUPS * POOL_GROUP
N_BRANCH = 3
D_FF = -(-8 * D_MODEL // (3 * 256)) * 256
IN_SIZES = (DN_QKV, DN_VAL, DN_HEADS, DN_HEADS, RET_QK, RET_QK, RET_VAL, RET_VAL, POOL_WIDTH, N_BRANCH * D_MODEL)
D_IN = sum(IN_SIZES)


def _split_points(sizes):
    pts, acc = [], 0
    for s in sizes[:-1]:
        acc += s
        pts.append(acc)
    return pts

def rms_norm_2(x, w):
    xf = x.astype(jnp.float32)
    y = xf * lax.rsqrt(jnp.mean(xf * xf, axis=-1, keepdims=True) + RMS_EPS) * w.astype(jnp.float32)
    return y.astype(x.dtype)

def l2_normalize(x):
    return x * lax.rsqrt(jnp.sum(x * x, axis=-1, keepdims=True) + 1e-6)

def causal_depthwise_conv(x, w):
    k = w.shape[0]
    return lax.conv_general_dilated(
        x, w[:, None, :].astype(x.dtype), window_strides=(1,), padding=((k - 1, 0),),
        dimension_numbers=("NWC", "WIO", "NWC"), feature_group_count=x.shape[-1])

def to_chunks(x):
    b, s, h, d = x.shape
    return x.reshape(b, s // CHUNK, CHUNK, h, d).transpose(0, 3, 1, 2, 4)

def from_chunks(x):
    b, h, n, c, d = x.shape
    return x.transpose(0, 2, 3, 1, 4).reshape(b, n * c, h * d)

def gated_delta_rule(q, k, v, beta, g):
    b, s, h, dk = q.shape
    dv = v.shape[-1]
    n = s // CHUNK
    q = to_chunks(q) * (dk ** -0.5)
    k = to_chunks(k)
    v = to_chunks(v)
    beta = beta.reshape(b, n, CHUNK, h).transpose(0, 3, 1, 2)
    g = g.reshape(b, n, CHUNK, h).transpose(0, 3, 1, 2)
    G = jnp.cumsum(g, axis=-1)
    causal = jnp.tril(jnp.ones((CHUNK, CHUNK), dtype=bool))
    strict = jnp.tril(jnp.ones((CHUNK, CHUNK), dtype=bool), k=-1)
    diff = G[..., :, None] - G[..., None, :]
    decay = jnp.where(causal, jnp.exp(jnp.where(causal, diff, 0.0)), 0.0)
    k_beta = k * beta[..., None]
    m = jnp.where(strict, jnp.einsum('bhnid,bhnjd->bhnij', k_beta, k) * decay, 0.0)
    a = m + jnp.eye(CHUNK, dtype=m.dtype)
    rhs = jnp.concatenate([v * beta[..., None], k_beta * jnp.exp(G)[..., None]], axis=-1)
    sol = lax.linalg.triangular_solve(a, rhs, left_side=True, lower=True, unit_diagonal=True)
    u, w = sol[..., :dv], sol[..., dv:]
    attn = jnp.einsum('bhnid,bhnjd->bhnij', q, k) * decay
    g_last = G[..., -1]
    q_dec = q * jnp.exp(G)[..., None]
    k_tail = k * jnp.exp(g_last[..., None] - G)[..., None]
    xs = tuple(jnp.moveaxis(t, 2, 0) for t in (u, w, attn, q_dec, k_tail, jnp.exp(g_last)))

    def step(state, inp):
        u_c, w_c, a_c, qd_c, kt_c, dl_c = inp
        v_new = u_c - jnp.einsum('bhck,bhkv->bhcv', w_c, state)
        o = jnp.einsum('bhck,bhkv->bhcv', qd_c, state) + jnp.einsum('bhcj,bhjv->bhcv', a_c, v_new)
        state = state * dl_c[..., None, None] + jnp.einsum('bhck,bhcv->bhkv', kt_c, v_new)
        return state, o

    s0 = jnp.zeros((b, h, dk, dv), dtype=q.dtype)
    _, o = lax.scan(step, s0, xs)
    return from_chunks(jnp.moveaxis(o, 0, 2))

def rotary(x):
    s, d = x.shape[1], x.shape[-1]
    half = d // 2
    inv = ROPE_BASE ** (-jnp.arange(half, dtype=jnp.float32) / half)
    ang = jnp.arange(s, dtype=jnp.float32)[:, None] * inv[None, :]
    cos = jnp.cos(ang)[None, :, None, :]
    sin = jnp.sin(ang)[None, :, None, :]
    x1, x2 = x[..., :half], x[..., half:]
    return jnp.concatenate([x1 * cos - x2 * sin, x2 * cos + x1 * sin], axis=-1)

def chunkwise_retention(q, k, v, log_gamma):
    b, s, h, dk = q.shape
    dv = v.shape[-1]
    q = to_chunks(q)
    k = to_chunks(k) * (dk ** -0.5)
    v = to_chunks(v)
    idx = jnp.arange(CHUNK, dtype=jnp.float32)
    lg = log_gamma[:, None]
    dmask = jnp.exp(jnp.abs(idx[:, None] - idx[None, :])[None] * log_gamma[:, None, None])
    scores = jnp.einsum('bhnid,bhnjd->bhnij', q, k) * dmask[:, None]
    o_inner = jnp.einsum('bhnij,bhnjv->bhniv', scores, v)
    xi = jnp.exp((idx + 1.0)[None] * lg)
    zeta = jnp.exp((CHUNK - 1.0 - idx)[None] * lg)
    kv = jnp.einsum('bhnjd,bhnjv->bhndv', k * zeta[:, None, :, None], v)
    chunk_decay = jnp.exp(CHUNK * log_gamma)

    def step(r, kv_c):
        return r * chunk_decay[:, None, None] + kv_c, r

    _, r_prev = lax.scan(step, jnp.zeros((b, h, dk, dv), dtype=kv.dtype), jnp.moveaxis(kv, 2, 0))
    r_prev = jnp.moveaxis(r_prev, 0, 2)
    o_cross = jnp.einsum('bhnid,bhndv->bhniv', q * xi[:, None, :, None], r_prev)
    o = from_chunks(o_inner + o_cross)
    return o.reshape(b, s, h, dv)

def multiscale_pool(u, w_lin, scale):
    b, s, _ = u.shape
    groups = u.reshape(b, s, POOL_GROUPS, POOL_GROUP)
    cs = jnp.cumsum(groups, axis=1)
    t = jnp.arange(1, s + 1, dtype=jnp.float32)
    pooled = []
    for gi, win in enumerate(POOL_WINDOWS):
        c = cs[:, :, gi]
        prev = jnp.pad(c, ((0, 0), (win, 0), (0, 0)))[:, :s]
        cnt = jnp.minimum(t, float(win))[None, :, None]
        pooled.append((c - prev) / cnt)
    mixed = jnp.stack(pooled, axis=2) - groups
    y = jnp.einsum('bsgc,gcd->bsgd', mixed, w_lin.astype(jnp.float32)).reshape(b, s, POOL_WIDTH)
    return y * scale.astype(jnp.float32)

def hybrid_mixer(h, w_in, dn_conv, dn_A_log, dn_dt_bias, dn_out_norm, ret_out_norm,
                 pool_w, pool_scale, w_branch_dn, w_branch_ret, w_branch_pool, w_out):
    b, s, _ = h.shape
    f32 = jnp.float32
    proj = h @ w_in
    (dn_qkv, dn_z, dn_b, dn_a, ret_q, ret_k, ret_v, ret_g, pool_u, gates) = jnp.split(
        proj, _split_points(IN_SIZES), axis=-1)

    qkv = jax.nn.silu(causal_depthwise_conv(dn_qkv, dn_conv)).astype(f32)
    q, k, v = jnp.split(qkv, [DN_HEADS * DN_DK, 2 * DN_HEADS * DN_DK], axis=-1)
    q = l2_normalize(q.reshape(b, s, DN_HEADS, DN_DK))
    k = l2_normalize(k.reshape(b, s, DN_HEADS, DN_DK))
    v = v.reshape(b, s, DN_HEADS, DN_DV)
    beta = jax.nn.sigmoid(dn_b.astype(f32))
    g = -jnp.exp(dn_A_log.astype(f32)) * jax.nn.softplus(dn_a.astype(f32) + dn_dt_bias.astype(f32))
    o_dn = gated_delta_rule(q, k, v, beta, g).reshape(b, s, DN_HEADS, DN_DV)
    o_dn = o_dn * lax.rsqrt(jnp.mean(o_dn * o_dn, axis=-1, keepdims=True) + RMS_EPS) * dn_out_norm.astype(f32)
    o_dn = o_dn.reshape(b, s, DN_VAL) * jax.nn.silu(dn_z.astype(f32))

    o_pool = multiscale_pool(pool_u.astype(f32), pool_w, pool_scale)

    log_gamma = jnp.log1p(-jnp.exp2(-5.0 - jnp.arange(RET_HEADS, dtype=f32)))
    rq = rotary(ret_q.astype(f32).reshape(b, s, RET_HEADS, RET_DK))
    rk = rotary(ret_k.astype(f32).reshape(b, s, RET_HEADS, RET_DK))
    rv = ret_v.astype(f32).reshape(b, s, RET_HEADS, RET_DV)
    o_ret = chunkwise_retention(rq, rk, rv, log_gamma)
    mu = jnp.mean(o_ret, axis=-1, keepdims=True)
    var = jnp.mean(jnp.square(o_ret - mu), axis=-1, keepdims=True)
    o_ret = ((o_ret - mu) * lax.rsqrt(var + GN_EPS)).reshape(b, s, RET_VAL) * ret_out_norm.astype(f32)
    o_ret = o_ret * jax.nn.silu(ret_g.astype(f32))

    gt = jax.nn.sigmoid(gates.astype(f32)).reshape(b, s, N_BRANCH, D_MODEL)
    y = (gt[:, :, 0] * (o_dn.astype(h.dtype) @ w_branch_dn)
         + gt[:, :, 1] * (o_pool.astype(h.dtype) @ w_branch_pool)
         + gt[:, :, 2] * (o_ret.astype(h.dtype) @ w_branch_ret))
    return y.astype(h.dtype) @ w_out

def swiglu(h, w_gate, w_up, w_down):
    return (jax.nn.silu(h @ w_gate) * (h @ w_up)) @ w_down

def second_inputs(seed: int = 0) -> dict:
    key = jax.random.key(seed)
    ks = jax.random.split(key, 24)
    f32 = jnp.float32
    L = DEPTH

    def nrm(k, shape, fan_in):
        return jax.random.normal(k, shape, f32) * (fan_in ** -0.5)

    def gain(k, shape):
        return 1.0 + 0.1 * jax.random.normal(k, shape, f32)

    dt = jnp.exp(jax.random.uniform(ks[6], (L, DN_HEADS), f32, minval=float(np.log(1e-3)), maxval=float(np.log(1e-1))))
    return {
        "x": jax.random.normal(ks[0], (BATCH, SEQ, D_MODEL), f32),
        "mix_pre_norm": gain(ks[1], (L, D_MODEL)),
        "mix_post_norm": gain(ks[2], (L, D_MODEL)),
        "w_in": nrm(ks[3], (L, D_MODEL, D_IN), D_MODEL),
        "dn_conv": nrm(ks[4], (L, DN_CONV, DN_QKV), DN_CONV),
        "dn_A_log": jnp.log(jax.random.uniform(ks[5], (L, DN_HEADS), f32, minval=1.0, maxval=16.0)),
        "dn_dt_bias": dt + jnp.log(-jnp.expm1(-dt)),
        "dn_out_norm": gain(ks[7], (L, DN_DV)),
        "ret_out_norm": gain(ks[8], (L, RET_VAL)),
        "pool_w": nrm(ks[9], (L, POOL_GROUPS, POOL_GROUP, POOL_GROUP), POOL_GROUP),
        "pool_scale": gain(ks[10], (L, POOL_WIDTH)),
        "w_branch_dn": nrm(ks[11], (L, DN_VAL, D_MODEL), DN_VAL),
        "w_branch_ret": nrm(ks[12], (L, RET_VAL, D_MODEL), RET_VAL),
        "w_branch_pool": nrm(ks[13], (L, POOL_WIDTH, D_MODEL), POOL_WIDTH),
        "w_out": nrm(ks[14], (L, D_MODEL, D_MODEL), D_MODEL),
        "ffn_pre_norm": gain(ks[15], (L, D_MODEL)),
        "ffn_post_norm": gain(ks[16], (L, D_MODEL)),
        "ffn_gate": nrm(ks[17], (L, D_MODEL, D_FF), D_MODEL),
        "ffn_up": nrm(ks[18], (L, D_MODEL, D_FF), D_MODEL),
        "ffn_down": nrm(ks[19], (L, D_FF, D_MODEL), D_FF),
    }

def second_block(x, mix_pre_norm, mix_post_norm, w_in, dn_conv, dn_A_log, dn_dt_bias, dn_out_norm,
              ret_out_norm, pool_w, pool_scale, w_branch_dn, w_branch_ret, w_branch_pool, w_out,
              ffn_pre_norm, ffn_post_norm, ffn_gate, ffn_up, ffn_down):
    for l in range(DEPTH):
        h = rms_norm_2(x, mix_pre_norm[l])
        m = hybrid_mixer(h, w_in[l], dn_conv[l], dn_A_log[l], dn_dt_bias[l], dn_out_norm[l],
                         ret_out_norm[l], pool_w[l], pool_scale[l], w_branch_dn[l], w_branch_ret[l],
                         w_branch_pool[l], w_out[l])
        x = x + rms_norm_2(m, mix_post_norm[l])
        h = rms_norm_2(x, ffn_pre_norm[l])
        x = x + rms_norm_2(swiglu(h, ffn_gate[l], ffn_up[l], ffn_down[l]), ffn_post_norm[l])
    return x


def setup_inputs(seed=0):
    out = dict(first_inputs(seed))
    for name, value in second_inputs(seed + 1).items():
        if name != "x":
            out[name + "_2"] = value
    return out


def reference(
    x, mem, positions, norm_g, w_in, w_out, moba_q_norm, moba_k_norm, hgrn_lb_logits,
    hgrn_o_norm, mem_norm_g, w_mem_kv, mem_q_norm, mem_k_norm, mix_pre_norm_2, mix_post_norm_2,
    w_in_2, dn_conv_2, dn_A_log_2, dn_dt_bias_2, dn_out_norm_2, ret_out_norm_2, pool_w_2,
    pool_scale_2, w_branch_dn_2, w_branch_ret_2, w_branch_pool_2, w_out_2, ffn_pre_norm_2,
    ffn_post_norm_2, ffn_gate_2, ffn_up_2, ffn_down_2,
):
    x = first_block(
        x, mem, positions, norm_g, w_in, w_out, moba_q_norm, moba_k_norm, hgrn_lb_logits,
        hgrn_o_norm, mem_norm_g, w_mem_kv, mem_q_norm, mem_k_norm,
    )
    return second_block(
        x, mix_pre_norm_2, mix_post_norm_2, w_in_2, dn_conv_2, dn_A_log_2, dn_dt_bias_2,
        dn_out_norm_2, ret_out_norm_2, pool_w_2, pool_scale_2, w_branch_dn_2, w_branch_ret_2,
        w_branch_pool_2, w_out_2, ffn_pre_norm_2, ffn_post_norm_2, ffn_gate_2, ffn_up_2,
        ffn_down_2,
    )


_drawn_inputs = setup_inputs


def setup_inputs(seed=0):
    import zlib

    import numpy as np

    out = dict(_drawn_inputs(seed))
    spreads = {}
    factors = {'moba_q_norm': 8.0,
     'moba_k_norm': 8.0,
     'hgrn_o_norm': 3.495,
     'mem_norm_g': 8.0,
     'mem_q_norm': 8.0,
     'mem_k_norm': 8.0,
     'hgrn_lb_logits': 3.122,
     'dn_out_norm_2': 3.759,
     'ret_out_norm_2': 3.28}
    for name, (base, spread) in spreads.items():
        noise = np.random.default_rng([zlib.crc32(name.encode()), seed]).standard_normal(out[name].shape)
        drawn = base * np.exp(spread * noise) if base else spread * noise
        out[name] = __import__('jax').numpy.asarray(drawn.astype(out[name].dtype))
    for name, factor in factors.items():
        out[name] = (out[name] * factor).astype(out[name].dtype)
    return out
```

```python
import numpy as np
import concourse.bass as bass
from concourse import mybir
from contextlib import ExitStack

P = 128
S = 256
TT = S // P
D = 1024
KD = D // P
DEPTH = 2
G = D // 2
MEM = 256
F32_COLS = 512
NH_A, DH_A = 8, 64
NH = 4
ROT = 8
D_FF = 2816
FF_G = D_FF // 256
KF = D_FF // P
UNIT_K = 4
SLOTS = 4
POOL_WINDOWS = (2, 4, 8, 16)
LEVELS = (1, 2, 4, 8, 16, 32, 64)
NEG = -1.0e30
TWO_PI_PARTS = (6.28125, 0.0019350051879882812, 3.0199157663446385e-07)
ROUND_MAGIC = 12582912.0

CONST_WIDTHS = [("ident", P), ("upper", P), ("ones", P), ("causal", 3 * P), ("inv_freq", ROT),
                ("cos", 4 * 64), ("sin", 4 * 64), ("band", 4 * 3 * P), ("ret_decay", 2 * NH * P),
                ("level", len(LEVELS) * P)]
CONST_AT = {}
_at = 0
for _n, _w in CONST_WIDTHS:
    CONST_AT[_n] = (_at, _w)
    _at += _w
CONST_COLS = _at


def shape_constants():
    c = np.zeros((P, CONST_COLS), np.float32)

    def put(name, a):
        at, w = CONST_AT[name]
        c[:, at:at + w] = np.asarray(a, np.float64).reshape(P, w).astype(np.float32)

    i = np.arange(P)
    upper = (i[:, None] <= i[None, :])
    put("ident", np.eye(P))
    put("upper", upper)
    put("ones", np.ones((P, P)))
    late = np.where(upper.T, 0.0, NEG)
    put("causal", np.concatenate([late, np.zeros((P, P)), late], axis=1))
    inv = np.float32(500000.0) ** (-np.arange(ROT, dtype=np.float32) / np.float32(ROT))
    put("inv_freq", np.broadcast_to(inv, (P, ROT)))
    inv = np.float32(10000.0) ** (-np.arange(64, dtype=np.float32) / np.float32(64))
    ang = (np.arange(S, dtype=np.float32)[:, None] * inv[None]).reshape(TT, P, 64).transpose(1, 0, 2)
    put("cos", np.concatenate([np.cos(ang.astype(np.float64))] * 2, axis=1))
    put("sin", np.concatenate([np.sin(ang.astype(np.float64))] * 2, axis=1))
    t = np.arange(S)
    band = np.zeros((P, 4, 3, P))
    for g, win in enumerate(POOL_WINDOWS):
        m = ((t[None] <= t[:, None]) & (t[None] > t[:, None] - win)) / np.minimum(t + 1.0, win)[:, None] - np.eye(S)
        mt = m.T
        band[:, g, 0], band[:, g, 1], band[:, g, 2] = mt[:P, :P], mt[:P, P:], mt[P:, P:]
    put("band", band)
    dec = np.zeros((P, 2, NH, P))
    for h in range(NH):
        lg = np.log1p(-np.exp2(-5.0 - h))
        dist = t[:, None] - t[None]
        w = np.where(t[:, None] // 64 == t[None] // 64, np.exp(np.abs(dist) * lg),
                     np.where(t[:, None] // 64 > t[None] // 64, np.exp(np.maximum(dist, 0) * lg), 0.0))
        w = w.T * P ** -0.5
        dec[:, 0, h], dec[:, 1, h] = w[:P, :P], w[:P, P:]
    put("ret_decay", dec)
    lev = np.zeros((P, len(LEVELS), P))
    for n, m in enumerate(LEVELS):
        lev[:, n] = (i[:, None] // (2 * m) == i[None] // (2 * m)) & (i[:, None] % (2 * m) < m) & (i[None] % (2 * m) >= m)
    put("level", lev)
    return c


COL_A = {"norm_g": (0, KD), "mem_norm_g": (16, KD), "mix_pre": (32, KD), "ffn_pre": (48, KD),
         "lb": (64, NH), "pool_scale": (72, NH)}
COL_A_ROWS = 80
COL_B_ROWS = DEPTH * 4 * 12

ORDER_1 = [f"xT{i}" for i in range(4)] + ["kmT0", "kmT1", "qhT0", "qhT1", "fhT0", "fhT1"] \
    + [f"hg{n}_{t}" for n in range(5) for t in range(2)] + ["qaT0", "qaT1", "kaT0", "kaT1"] \
    + ["hg5_0", "hg5_1"] + [f"sc{h}" for h in range(4)] + ["hg6_0", "hg6_1"] + [f"sc{h}" for h in range(4, 8)] \
    + ["hg7_0", "hg7_1", "hg8_1"] + [f"pt{h}" for h in range(8)] + ["oa0", "oa1", "qmT0", "qmT1"] \
    + [f"ms{h}" for h in range(4)] + ["hgo0", "hgo1"] + [f"mpt{h}" for h in range(4)] + ["om0", "om1"] \
    + [f"yT{i}" for i in range(6)]
ORDER_2 = [f"xT{i}" for i in range(4)] + [f"dT{j}{t}" for j in range(3) for t in range(2)] + ["ba", "cg", "gb0", "gb1"] \
    + [f"bT{j}{t}" for j in range(3) for t in range(2)] \
    + ["kT0", "kT1", "qT0", "qT1", "kbT0", "kbT1", "mm0", "mm1", "at0", "at1"] \
    + [f"{s}{n}_{t}" for n in range(len(LEVELS)) for s in ("Y", "Z", "W") for t in range(2)
       if not (s == "Z" and n == len(LEVELS) - 1)] \
    + ["u0", "wT", "st", "vn1", "do0", "do1"] \
    + ["rqT0", "rqT1", "rkT0", "rkT1", "rs0", "rs1", "rs2", "ro0", "ro1", "pm0", "pm1", "py0", "py1",
       "oT_r0", "oT_r1", "oT_d0", "oT_d1"] \
    + [f"yT{i}" for i in range(4)] + [f"fT{i}" for i in range(4)] + [f"HT{j}" for j in range(FF_G)]
PRE = ["colA", "colB", "memT0", "memT1", "memT2", "memT3"]
STEPS = PRE + [f"A{l}.{s}" for l in range(DEPTH) for s in ORDER_1] + [f"B{l}.{s}" for l in range(DEPTH) for s in ORDER_2]
STEP_NO = {s: n for n, s in enumerate(STEPS)}

GROUPS_1 = [("KM", KD), ("VM", KD), ("QH", KD), ("FH", KD), ("IH", KD), ("QA", KD), ("KA", KD), ("VA", KD),
            ("QM", KD), ("Z0", KD), ("Z1", KD), ("Z2", KD), ("O0", 12), ("O1", 12)]
GROUPS_2 = [("Q", KD), ("K", KD), ("V", KD), ("RQ", KD), ("RK", KD), ("RV", KD), ("PU", KD), ("RG", KD), ("DZ", KD)] \
    + [(f"G{j}", KD) for j in (2, 3, 4, 5, 0, 1)] \
    + [(f"BP{j}", NH) for j in range(2)] + [(f"BR{j}", NH) for j in range(2)] + [(f"BD{j}", NH) for j in range(2)] \
    + [("M0", KD), ("M1", KD)] + [(f"F{j}", KD) for j in range(FF_G)] + [("E0", KF), ("E1", KF)]
GROUPS = [(f"A{l}.{g}", k) for l in range(DEPTH) for g, k in GROUPS_1] + [(f"B{l}.{g}", k) for l in range(DEPTH) for g, k in GROUPS_2]
GROUP_NO = {g: n for n, (g, _) in enumerate(GROUPS)}
COL_1 = {g: 512 * n for n, g in enumerate(["QA", "KA", "VA", "QH", "FH", "IH", "QM", "Z0", "Z1", "Z2"])}
COL_2 = {"Q": 0, "K": 512, "V": 1024, "DZ": 1536, "RQ": 2056, "RK": 2568, "RV": 3080, "RG": 3592, "PU": 4104}
COL_2.update({f"G{j}": 4616 + 512 * j for j in range(6)})
BA_COL = 2048


def weight_units():
    out = []
    for g, (_, k) in enumerate(GROUPS):
        for k0 in range(0, k, UNIT_K):
            out.append((g, k0, min(UNIT_K, k - k0)))
    return out


UNITS = weight_units()
POWS_PRE, POWS_1, POWS_2 = 1, 5, 7


def mixer_program(nc, w, out):
    F = mybir.dt.float32
    ALU = mybir.AluOpType
    ACT = mybir.ActivationFunctionType
    X = mybir.AxisListType.X
    ctx = ExitStack()
    with ctx:
        def sb(name, shape, dt=F):
            return ctx.enter_context(nc.sbuf_tensor(name, shape, dt))

        def sem(name):
            return ctx.enter_context(nc.semaphore(name))

        wt = sb("wt", [P, SLOTS, UNIT_K, F32_COLS])
        const = sb("const", [P, CONST_COLS])
        x = sb("x", [P, TT, D])
        hT = sb("hT", [P, TT, KD, P])
        cols = sb("cols", [P, COL_A_ROWS + COL_B_ROWS])
        rot = sb("rot", [P, 2, 4, ROT])
        pos = sb("pos", [P, TT], mybir.dt.int32)
        small = sb("small", [P, 512])
        rs_in = sb("rs_in", [P, 32])
        rs_out = sb("rs_out", [P, 32])
        minus_half = sb("minus_half", [P, 32])
        g_qk = sb("g_qk", [P, DEPTH, 2, DH_A])
        g_mq = sb("g_mq", [P, DEPTH, P])
        g_mk = sb("g_mk", [P, DEPTH, P])
        g_ho = sb("g_ho", [P, DEPTH, P])
        a_log = sb("a_log", [P, DEPTH, NH])
        dt_bias = sb("dt_bias", [P, DEPTH, NH])
        w_ba = sb("w_ba", [P, DEPTH, KD, 8])
        ARENA = 36992
        arena = sb("arena", [P, ARENA])

        def C(name):
            at, width = CONST_AT[name]
            return const[:, at:at + width]

        ident, upper, ones = C("ident"), C("upper"), C("ones")
        level = C("level").rearrange("p (n i) -> p n i", n=len(LEVELS))
        band = C("band").rearrange("p (g b t) -> p g b t", g=4, b=3)
        decay_c = C("ret_decay").rearrange("p (b h t) -> p b h t", b=2, h=NH)

        def region(at, *shape):
            n = int(np.prod(shape))
            assert at + n <= ARENA
            v = arena[:, at:at + n]
            if len(shape) == 1:
                return v
            names = "abcd"[:len(shape)]
            return v.rearrange(f"p ({' '.join(names)}) -> p {' '.join(names)}",
                               **{c: s for c, s in zip(names[:-1], shape[:-1])})

        R1 = {g: 1024 * n for n, g in enumerate(["QH", "FH", "IH", "QA", "KA", "VA", "QM", "Z0", "Z1", "Z2", "KM", "VM"])}
        at = 12 * 1024

        def take(n):
            nonlocal at
            at += n
            return at - n
        a_memh, a_memT = take(2048), take(2048)
        a_qs, a_ks, a_B, a_qm, a_km, a_st, a_sto, a_rm = (take(1024), take(1024), take(1024), take(2048), take(2048),
                                                          take(1024), take(512), take(1024))
        a_QT, a_KT, a_S, a_PT, a_o = take(2048), take(1024), take(3072), take(3072), take(1024)
        assert at <= ARENA, at
        mem_hat = region(a_memh, TT, KD, P)
        mem_s = region(a_memT, TT, KD, P)
        dtmp, etmp = region(a_memT, NH, S), region(a_memT + 1024, NH, S)
        qs, ks, cum = region(a_qs, NH, S), region(a_ks, NH, S), region(a_B, NH, S)
        qmul = [region(a_qm + 1024 * i, NH, S) for i in range(2)]
        kmul = [region(a_km + 1024 * i, NH, S) for i in range(2)]
        hst, hst_off = region(a_st, TT, NH, P), region(a_sto, NH, P)
        restart = region(a_rm, 1024)
        QT, KT = region(a_QT, NH_A, S), region(a_KT, 4, S)
        sco, prT = region(a_S, NH_A, 384), region(a_PT, NH_A, 384)
        msc, mprT = region(a_S, NH, TT, MEM), region(a_PT, NH, 4, P)
        xs = region(a_S, TT, D)
        sq = region(a_PT, 2048)
        o_tmp = region(a_o, TT, G)

        names_2 = ["Q", "K", "V", "DZ", "RQ", "RK", "RV", "RG", "PU", "G0", "G1", "G2", "G3", "G4", "G5"]
        R2 = {g: 1024 * n for n, g in enumerate(names_2)}
        at = 15 * 1024
        b_x, b_c, b_e = take(3072), take(3072), take(3072)
        b_ml, b_kb, b_kt, b_wt, b_ss, b_vn, b_qd, b_eg = (take(1024), take(1024), take(512), take(512), take(512),
                                                          take(1024), take(512), take(512))
        b_rst, b_tmp, b_mx = take(1536), take(1024), take(1024)
        b_gd, b_gr, b_gm, b_gf, b_pw = take(128), take(512), take(1024), take(1024), take(512)
        assert at <= ARENA, at
        xT3, cT3, e3 = region(b_x, 12, S), region(b_c, 12, S), region(b_e, 12, S)
        kT, qT, kbT = (region(b_x + 1024 * i, TT, NH, P) for i in range(3))
        decT, mT, atT = (region(b_c + 1024 * i, TT, NH, P) for i in range(3))
        inv, invT, yl = (region(b_e + 1024 * i, TT, NH, P) for i in range(3))
        gbc = region(b_ml, 8, P)
        ml, kb = region(b_ml, TT, NH, P), region(b_kb, TT, NH, P)
        ktl, wT_, ss_ = region(b_kt, NH, P), region(b_wt, NH, P), region(b_ss, NH, P)
        vn, qd, eg = region(b_vn, TT, NH, P), region(b_qd, NH, P), region(b_eg, NH, P)
        rst, tmp, mx = region(b_rst, 3, NH, P), region(b_tmp, 1024), region(b_mx, 4, S)
        g_do, g_ro, g_mp, g_fp = region(b_gd, P), region(b_gr, G), region(b_gm, D), region(b_gf, D)
        pw = region(b_pw, 4, P)
        xs2 = region(b_e, TT, D)
        sq2 = region(b_e, 2048)
        hid = region(R2["RV"], FF_G, TT, 256)
        sg = region(b_tmp, TT, 2, 256)
        mres = region(R2["Q"], 2, TT, G)

        def reg(blk, g):
            return region((R1 if blk == "A" else R2)[g], TT, F32_COLS)

        def heads(v, n=NH):
            return v.rearrange("p t (h d) -> p (t h) d", h=n)

        gp = ctx.enter_context(nc.psum_tensor("gp", [P, 4, F32_COLS], F))
        mp = ctx.enter_context(nc.psum_tensor("mp", [P, 4, F32_COLS], F))

        loaded = {n: sem("loaded_" + n) for n in ("const", "rows", "x", "mem", "gain1", "gain2", "post", "ba")}
        w_loaded = [sem(f"w_loaded{i}") for i in range(SLOTS)]
        w_used = sem("w_used")
        group_read = [sem(f"group_read{i}") for i in range(2)]
        step_done = sem("step_done")
        step_read = [sem(f"step_read{i}") for i in range(4)]
        pow_asked, pow_given = sem("pow_asked"), sem("pow_given")
        v_chain, a_chain = sem("v_chain"), sem("a_chain")
        out_done = sem("out_done")
        named = {}

        def sig(name):
            if name not in named:
                named[name] = sem(name)
            return named[name]

        def computed(step):
            return step_done, STEP_NO[step] + 1

        def read_out(step):
            return step_read[STEP_NO[step] % 4], STEP_NO[step] // 4 + 1

        def bank(step, *dims):
            v = mp[:, STEP_NO[step] % 4]
            if len(dims) == 2:
                n = dims[0] * dims[1]
                return v[:, 0:n].rearrange("p (a b) -> p a b", a=dims[0])
            return v[:, 0:dims[0]] if dims else v

        def group_bank(group, t):
            return gp[:, 2 * (GROUP_NO[group] % 2) + t]

        def summed(group):
            return w_used, 1 + max(u for u, (g, _, _) in enumerate(UNITS) if g == GROUP_NO[group])

        def taken(group):
            return group_read[GROUP_NO[group] % 2], GROUP_NO[group] // 2 + 1

        def group_banks(group):
            b = 2 * (GROUP_NO[group] % 2)
            return gp[:, b:b + 2, :]

        lbs = small[:, 460:472]

        def cT3s(j):
            return cT3[:, 4 * j:4 * j + 4, :]

        block = ctx.enter_context(nc.Block())

        def unit_loads(u):
            g, k0, nk = UNITS[u]
            name = GROUPS[g][0]
            l, n = int(name[1]), name[3:]

            def piece(src, c0, width=F32_COLS, to=0):
                return (wt[:, u % SLOTS, 0:nk, to:to + width],
                        src[l, k0 * P:(k0 + nk) * P, c0:c0 + width].rearrange("(k p) n -> p k n", p=P))
            if name[0] == "A":
                if n in ("KM", "VM"):
                    return [piece(w["w_mem_kv"], 0 if n == "KM" else G)]
                if n[0] == "O":
                    return [piece(w["w_out"], G * int(n[1]))]
                return [piece(w["w_in"], COL_1[n])]
            if n in COL_2:
                return [piece(w["w_in_2"], COL_2[n])]
            j = int(n[-1]) if n[0] != "F" else int(n[1:])
            if n[0] == "B":
                return [piece(w[{"P": "w_branch_pool_2", "R": "w_branch_ret_2", "D": "w_branch_dn_2"}[n[1]]], G * j)]
            if n[0] == "M":
                return [piece(w["w_out_2"], G * j)]
            if n[0] == "F":
                return [piece(w["ffn_gate_2"], 256 * j, 256), piece(w["ffn_up_2"], 256 * j, 256, 256)]
            return [piece(w["ffn_down_2"], G * j)]

        slot_total = [0] * SLOTS
        unit_value = []
        for u in range(len(UNITS)):
            slot_total[u % SLOTS] += 16 * len(unit_loads(u))
            unit_value.append(slot_total[u % SLOTS])

        @block.sync
        def _(sp):
            sp.dma_start(const[:, :], w["shape_constants"]).then_inc(loaded["const"], 16)
            sp.dma_start(region(a_S, TT, D), w["mem"][0].rearrange("(t p) d -> p t d", p=P)).then_inc(loaded["mem"], 16)
            sp.dma_start(x[:, :, :], w["x"][0].rearrange("(t p) d -> p t d", p=P)).then_inc(loaded["x"], 16)
            for u in range(len(UNITS)):
                if u >= SLOTS:
                    sp.wait_ge(w_used, u - SLOTS + 1)
                for dst, src in unit_loads(u):
                    sp.dma_start(dst, src).then_inc(w_loaded[u % SLOTS], 16)
            sp.wait_ge(sig("x_summed"), 2 * DEPTH)
            sp.dma_start(out[0].rearrange("(t p) d -> p t d", p=P), x[:, :, :]).then_inc(out_done, 16)
            sp.wait_ge(out_done, 16)

        @block.gpsimd
        def _(pool):
            for n in range(POWS_PRE + DEPTH * (POWS_1 + POWS_2)):
                pool.wait_ge(pow_asked, n + 1)
                nc.gpsimd.tensor_tensor(rs_out[:, :], rs_in[:, :], minus_half[:, :], ALU.pow).then_inc(pow_given, 1)

        @block.tensor
        def _(pe):
            state = {"unit": 0, "step": 0}

            def begin(step, *waits):
                n = STEP_NO[step]
                assert n == state["step"], (step, STEPS[state["step"]])
                state["step"] += 1
                if n >= 4:
                    pe.wait_ge(step_read[n % 4], n // 4)
                for wait in waits:
                    pe.wait_ge(*wait)

            def end(ins):
                ins.then_inc(step_done, 1)

            def transposes(step, tiles, *waits):
                begin(step, *waits)
                for j, tile in enumerate(tiles):
                    last = nc.tensor.transpose(bank(step)[:, P * j:P * j + P], tile, ident)
                end(last)

            def units(group, stationary, count, *waits):
                for _ in range(count):
                    u = state["unit"]
                    g, k0, nk = UNITS[u]
                    assert GROUPS[g][0] == group, (group, GROUPS[g][0])
                    state["unit"] += 1
                    if k0 == 0:
                        if g >= 2:
                            pe.wait_ge(group_read[g % 2], g // 2)
                        for wait in waits:
                            pe.wait_ge(*wait)
                    pe.wait_ge(w_loaded[u % SLOTS], unit_value[u])
                    for t in range(TT):
                        for k in range(nk):
                            last = nc.tensor.matmul(group_bank(group, t), stationary(k0 + k, t), wt[:, u % SLOTS, k, :],
                                                    start=(k0 + k == 0), stop=(k0 + k == GROUPS[g][1] - 1))
                    last.then_inc(w_used, 1)

            def from_hT(k, t):
                return hT[:, t, k, :]

            pe.wait_ge(loaded["const"], 16)
            pe.wait_ge(loaded["rows"], 16 * 7)
            pe.wait_ge(sig("v_start"), 1)
            begin("colA")
            end(nc.tensor.transpose(bank("colA")[:, 0:COL_A_ROWS], small[0:COL_A_ROWS, 0:P], ident[0:COL_A_ROWS, 0:COL_A_ROWS]))
            begin("colB")
            end(nc.tensor.transpose(bank("colB")[:, 0:COL_B_ROWS], small[0:COL_B_ROWS, P:2 * P], ident[0:COL_B_ROWS, 0:COL_B_ROWS]))
            for i in range(4):
                t, q = divmod(i, 2)
                transposes(f"memT{i}", [region(a_S, TT, D)[:, t, (4 * q + j) * P:(4 * q + j + 1) * P] for j in range(4)],
                           (sig("mem_normed"), 1))

            for l in range(DEPTH):
                s = lambda n: f"A{l}.{n}"
                pe.wait_ge(sig("mem_scaled"), l + 1)
                for g in ("KM", "VM"):
                    units(s(g), lambda k, t: mem_s[:, t, k, :], 2)
                for i in range(4):
                    t, q = divmod(i, 2)
                    transposes(s(f"xT{i}"), [xs[:, t, (4 * q + j) * P:(4 * q + j + 1) * P] for j in range(4)],
                               (sig("x_normed"), l + 1))
                for i in range(4):
                    pe.wait_ge(*read_out(s(f"xT{i}")))
                units(s("QH"), from_hT, 2)
                for t in range(TT):
                    transposes(s(f"kmT{t}"), [reg("A", "KM")[:, t, P * j:P * j + P] for j in range(4)], (sig("km_normed"), l + 1))
                units(s("FH"), from_hT, 2)
                for t in range(TT):
                    transposes(s(f"qhT{t}"), [reg("A", "QH")[:, t, P * j:P * j + P] for j in range(4)],
                               (group_read[GROUP_NO[s("QH")] % 2], GROUP_NO[s("QH")] // 2 + 1))
                units(s("IH"), from_hT, 1)
                for t in range(TT):
                    transposes(s(f"fhT{t}"), [reg("A", "FH")[:, t, P * j:P * j + P] for j in range(4)],
                               (group_read[GROUP_NO[s("FH")] % 2], GROUP_NO[s("FH")] // 2 + 1))
                units(s("IH"), from_hT, 1)
                units(s("QA"), from_hT, 2)

                def hg_level(n):
                    src_q, src_k = (qs, ks) if n == 0 else (qmul[n % 2], kmul[n % 2])
                    for t in (range(TT) if n < 8 else (1,)):
                        begin(s(f"hg{n}_{t}"), (sig("hg_factors"), 9 * l + n + 1))
                        kt = t if n < 8 else 0
                        for h in range(NH):
                            last = nc.tensor.matmul(bank(s(f"hg{n}_{t}"))[:, P * h:P * h + P], src_k[:, h, kt * P:kt * P + P],
                                                    src_q[:, h, t * P:t * P + P], start=True, stop=True)
                        end(last)
                hg_level(0)
                units(s("KA"), from_hT, 1)
                hg_level(1)
                units(s("KA"), from_hT, 1)
                hg_level(2)
                units(s("VA"), from_hT, 1)
                hg_level(3)
                units(s("VA"), from_hT, 1)
                hg_level(4)
                for src, n in (("QA", "qaT"), ("KA", "kaT")):
                    for t in range(TT):
                        transposes(s(f"{n}{t}"), [reg("A", src)[:, t, P * j:P * j + P] for j in range(4)], (sig("qk_rotated"), l + 1))
                units(s("QM"), from_hT, 1)
                hg_level(5)

                def scores(h):
                    begin(s(f"sc{h}"), read_out(s("kaT0")), read_out(s("kaT1")), read_out(s("qaT0")), read_out(s("qaT1")))
                    b = bank(s(f"sc{h}"))
                    nc.tensor.matmul(b[:, 0:P], QT[:, h, 0:P], KT[:, h // 2, 0:P], start=True, stop=True)
                    end(nc.tensor.matmul(b[:, P:3 * P], QT[:, h, P:S], KT[:, h // 2, :], start=True, stop=True))
                for h in range(4):
                    scores(h)
                units(s("QM"), from_hT, 1)
                hg_level(6)
                for h in range(4, 8):
                    scores(h)
                units(s("Z0"), from_hT, 1)
                hg_level(7)
                hg_level(8)
                for h in range(8):
                    if h == 4:
                        units(s("Z0"), from_hT, 1)
                    transposes(s(f"pt{h}"), [sco[:, h, P * j:P * j + P] for j in range(3)],
                               (sig("attn_probs"), 2 * NH_A * l + 2 * h + 2))
                for t in range(TT):
                    begin(s(f"oa{t}"), *[read_out(s(f"pt{h}")) for h in range(4, 8)])
                    pe.wait_ge(group_read[GROUP_NO[s("VA")] % 2], GROUP_NO[s("VA")] // 2 + 1)
                    for h in range(8):
                        for st in range(t + 1):
                            last = nc.tensor.matmul(bank(s(f"oa{t}"))[:, DH_A * h:DH_A * (h + 1)],
                                                    prT[:, h, (t + st) * P:(t + st + 1) * P],
                                                    reg("A", "VA")[:, st, DH_A * h:DH_A * (h + 1)], start=(st == 0), stop=(st == t))
                    end(last)
                units(s("Z1"), from_hT, 1)
                for t in range(TT):
                    transposes(s(f"qmT{t}"), [reg("A", "QM")[:, t, P * j:P * j + P] for j in range(4)], (sig("qm_normed"), l + 1))
                km3 = reg("A", "KM").rearrange("p t (h m) -> p t h m", h=NH)
                for h in range(NH):
                    begin(s(f"ms{h}"), read_out(s("kmT0")), read_out(s("kmT1")), read_out(s("qmT0")), read_out(s("qmT1")))
                    for t in range(TT):
                        last = nc.tensor.matmul(bank(s(f"ms{h}"), TT, MEM)[:, t, :].rearrange("p (a b) -> p a b", a=TT),
                                                reg("A", "QM")[:, t, P * h:P * h + P], km3[:, :, h, :], start=True, stop=True)
                    end(last)
                units(s("Z1"), from_hT, 1)
                for t in range(TT):
                    begin(s(f"hgo{t}"), read_out(s("hg7_0")), read_out(s("hg7_1")), read_out(s("hg8_1")))
                    pe.wait_ge(group_read[GROUP_NO[s("IH")] % 2], GROUP_NO[s("IH")] // 2 + 1)
                    for h in range(NH):
                        o = bank(s(f"hgo{t}"))[:, P * h:P * h + P]
                        if t == 1:
                            nc.tensor.matmul(o, hst_off[:, h, :], reg("A", "IH")[:, 0, P * h:P * h + P], start=True, stop=False)
                        last = nc.tensor.matmul(o, hst[:, t, h, :], reg("A", "IH")[:, t, P * h:P * h + P], start=(t == 0), stop=True)
                    end(last)
                units(s("Z2"), from_hT, 1)
                for h in range(NH):
                    transposes(s(f"mpt{h}"), [msc[:, h, t, P * j:P * j + P] for t in range(TT) for j in range(2)], read_out(s(f"ms{h}")))
                units(s("Z2"), from_hT, 1)
                for t in range(TT):
                    begin(s(f"om{t}"), *[read_out(s(f"mpt{h}")) for h in range(4)])
                    pe.wait_ge(group_read[GROUP_NO[s("VM")] % 2], GROUP_NO[s("VM")] // 2 + 1)
                    for h in range(NH):
                        for st in range(TT):
                            last = nc.tensor.matmul(bank(s(f"om{t}"))[:, P * h:P * h + P], mprT[:, h, 2 * t + st, :],
                                                    reg("A", "VM")[:, st, P * h:P * h + P], start=(st == 0), stop=(st == 1))
                    end(last)
                for i in range(6):
                    j, t = divmod(i, 2)
                    transposes(s(f"yT{i}"), [reg("A", f"Z{j}")[:, t, P * q:P * q + P] for q in range(4)], (sig("y_ready"), 3 * l + j + 1))
                for i in range(2, 6):
                    pe.wait_ge(*read_out(s(f"yT{i}")))
                for g in ("O0", "O1"):
                    units(s(g), lambda k, t: reg("A", f"Z{k // 4}")[:, t, P * (k % 4):P * (k % 4) + P], 3)

            for l in range(DEPTH):
                s = lambda n: f"B{l}.{n}"

                def group_in(g):
                    n = GROUP_NO[s(g)]
                    return group_read[n % 2], n // 2 + 1
                for i in range(4):
                    t, q = divmod(i, 2)
                    transposes(s(f"xT{i}"), [xs2[:, t, (4 * q + j) * P:(4 * q + j + 1) * P] for j in range(4)],
                               (sig("x_normed_b"), 2 * l + 1))
                for i in range(4):
                    pe.wait_ge(*read_out(s(f"xT{i}")))
                for j, g in enumerate("QKV"):
                    units(s(g), from_hT, 2)
                units(s("RQ"), from_hT, 1)
                for j, g in enumerate("QKV"):
                    for t in range(TT):
                        transposes(s(f"dT{j}{t}"), [reg("B", g)[:, t, P * q:P * q + P] for q in range(4)], group_in(g))
                begin(s("ba"), (loaded["ba"], 16 * DEPTH))
                for t in range(TT):
                    for k in range(KD):
                        last = nc.tensor.matmul(bank(s("ba"))[:, 8 * t:8 * t + 8], hT[:, t, k, :], w_ba[:, l, k, :],
                                                start=(k == 0), stop=(k == KD - 1))
                end(last)
                units(s("RQ"), from_hT, 1)
                begin(s("cg"), (sig("gates_ready"), l + 1))
                gcol = small[:, 0:8]
                nc.tensor.matmul(bank(s("cg"))[:, 0:8], upper, gcol, start=True, stop=True)
                end(nc.tensor.matmul(bank(s("cg"))[:, 8:16], ones, gcol, start=True, stop=True))
                for t in range(TT):
                    begin(s(f"gb{t}"), (sig("gates_ready"), l + 1))
                    for h in range(NH):
                        last = nc.tensor.matmul(bank(s(f"gb{t}"))[:, P * h:P * h + P], gbc[:, NH * t + h, :], upper, start=True, stop=True)
                    end(last)
                units(s("RK"), from_hT, 2)
                for j in range(3):
                    for t in range(TT):
                        transposes(s(f"bT{j}{t}"), [cT3[:, 4 * j + q, t * P:t * P + P] for q in range(4)], (sig("conv_done"), l + 1))
                units(s("RV"), from_hT, 2)
                for n, v in (("kT", reg("B", "K")), ("qT", reg("B", "Q")), ("kbT", kb.rearrange("p t h d -> p t (h d)"))):
                    for t in range(TT):
                        transposes(s(f"{n}{t}"), [v[:, t, P * q:P * q + P] for q in range(4)], (sig("dn_normed"), l + 1))
                for n, v in (("mm", kbT), ("at", qT)):
                    for t in range(TT):
                        begin(s(f"{n}{t}"), *[read_out(s(f"{m}{t}")) for m in ("kT", "qT", "kbT")])
                        for h in range(NH):
                            last = nc.tensor.matmul(bank(s(f"{n}{t}"))[:, P * h:P * h + P], kT[:, t, h, :], v[:, t, h, :], start=True, stop=True)
                        end(last)

                def quad(step, lhs, rhs, *waits):
                    begin(step, *waits)
                    for h in range(NH):
                        last = nc.tensor.matmul(bank(step)[:, P * h:P * h + P], lhs(h), rhs(h), start=True, stop=True)
                    end(last)
                fill = [(g, 1) for g in ("PU", "PU", "RG", "RG", "DZ", "DZ", "G2", "G2", "G3", "G3", "G4", "G4", "G5", "G5", "G0", "G0", "G1", "G1")]

                def filler():
                    if fill:
                        g, c = fill.pop(0)
                        units(s(g), from_hT, c)
                for n in range(len(LEVELS)):
                    for t in range(TT):
                        quad(s(f"Y{n}_{t}"), lambda h: ml[:, t, h, :], lambda h: inv[:, t, h, :], (sig("inv_ready"), len(LEVELS) * l + n + 1))
                    filler()
                    if n < len(LEVELS) - 1:
                        for t in range(TT):
                            quad(s(f"Z{n}_{t}"), lambda h: invT[:, t, h, :], lambda h: yl[:, t, h, :], read_out(s(f"Y{n}_{t}")))
                    for t in range(TT):
                        quad(s(f"W{n}_{t}"), lambda h: yl[:, t, h, :], lambda h: invT[:, t, h, :], read_out(s(f"Y{n}_{t}")))
                    filler()
                last = len(LEVELS) - 1
                inv_done = [read_out(s(f"W{last}_{t}")) for t in range(TT)]
                vb = reg("B", "V").rearrange("p t (h d) -> p t h d", h=NH)
                quad(s("u0"), lambda h: invT[:, 0, h, :], lambda h: vb[:, 0, h, :], *inv_done)
                quad(s("wT"), lambda h: kb[:, 1, h, :], lambda h: invT[:, 1, h, :], *inv_done)
                filler()
                quad(s("st"), lambda h: ktl[:, h, :], lambda h: vn[:, 0, h, :], read_out(s("u0")))
                begin(s("vn1"), read_out(s("wT")), read_out(s("st")))
                for h in range(NH):
                    nc.tensor.matmul(bank(s("vn1"))[:, P * h:P * h + P], invT[:, 1, h, :], vb[:, 1, h, :], start=True, stop=False)
                    last = nc.tensor.matmul(bank(s("vn1"))[:, P * h:P * h + P], wT_[:, h, :], ss_[:, h, :], start=False, stop=True)
                end(last)
                filler()
                quad(s("do0"), lambda h: atT[:, 0, h, :], lambda h: vn[:, 0, h, :])
                begin(s("do1"), read_out(s("vn1")))
                for h in range(NH):
                    nc.tensor.matmul(bank(s("do1"))[:, P * h:P * h + P], qd[:, h, :], ss_[:, h, :], start=True, stop=False)
                    last = nc.tensor.matmul(bank(s("do1"))[:, P * h:P * h + P], atT[:, 1, h, :], vn[:, 1, h, :], start=False, stop=True)
                end(last)
                filler()
                for n, g in (("rqT", "RQ"), ("rkT", "RK")):
                    for t in range(TT):
                        transposes(s(f"{n}{t}"), [reg("B", g)[:, t, P * q:P * q + P] for q in range(4)], (sig("ret_rotated"), l + 1))
                for i, (jt, it) in enumerate(((0, 0), (0, 1), (1, 1))):
                    quad(s(f"rs{i}"), lambda h: reg("B", "RK")[:, jt, P * h:P * h + P], lambda h: reg("B", "RQ")[:, it, P * h:P * h + P],
                         *[read_out(s(f"{n}{t}")) for n in ("rqT", "rkT") for t in range(TT)])
                filler()
                for t in range(TT):
                    begin(s(f"ro{t}"), *[read_out(s(f"rs{i}")) for i in range(3)])
                    for h in range(NH):
                        o = bank(s(f"ro{t}"))[:, P * h:P * h + P]
                        if t == 1:
                            nc.tensor.matmul(o, rst[:, 1, h, :], reg("B", "RV")[:, 0, P * h:P * h + P], start=True, stop=False)
                        last = nc.tensor.matmul(o, rst[:, 2 * t, h, :], reg("B", "RV")[:, t, P * h:P * h + P], start=(t == 0), stop=True)
                    end(last)
                pu = reg("B", "PU")
                for i in range(2):
                    begin(s(f"pm{i}"))
                    for q in range(2):
                        g = 2 * i + q
                        o = bank(s(f"pm{i}"), 2, S)[:, q, :]
                        nc.tensor.matmul(o[:, 0:P], pu[:, 0, P * g:P * g + P], band[:, g, 0, :], start=True, stop=True)
                        nc.tensor.matmul(o[:, P:S], pu[:, 0, P * g:P * g + P], band[:, g, 1, :], start=True, stop=False)
                        last = nc.tensor.matmul(o[:, P:S], pu[:, 1, P * g:P * g + P], band[:, g, 2, :], start=False, stop=True)
                    end(last)
                while len(fill) > 0:
                    filler()
                for i in range(2):
                    begin(s(f"py{i}"), read_out(s(f"pm{i}")), (loaded["post"], 16 * 5 * (l + 1)))
                    for q in range(2):
                        last = nc.tensor.matmul(bank(s(f"py{i}"), 2, S)[:, q, :], pw[:, 2 * i + q, :], mx[:, 2 * i + q, :], start=True, stop=True)
                    end(last)
                for i in range(2):
                    pe.wait_ge(*read_out(s(f"py{i}")))
                po = reg("B", "PU").rearrange("p t (c i) -> p (t c i)", c=4).rearrange("p (k s) -> p k s", k=4)
                for j in range(2):
                    units(s(f"BP{j}"), lambda k, t: po[:, k, t * P:t * P + P], 1)
                for t in range(TT):
                    transposes(s(f"oT_r{t}"), [reg("B", "RQ")[:, t, P * q:P * q + P] for q in range(4)], (sig("ret_out"), l + 1))
                for t in range(TT):
                    pe.wait_ge(*read_out(s(f"oT_r{t}")))
                for j in range(2):
                    units(s(f"BR{j}"), lambda k, t: reg("B", "RQ")[:, t, P * k:P * k + P], 1)
                for t in range(TT):
                    transposes(s(f"oT_d{t}"), [reg("B", "Q")[:, t, P * q:P * q + P] for q in range(4)], (sig("dn_out"), l + 1))
                for t in range(TT):
                    pe.wait_ge(*read_out(s(f"oT_d{t}")))
                for j in range(2):
                    units(s(f"BD{j}"), lambda k, t: reg("B", "Q")[:, t, P * k:P * k + P], 1)
                for i in range(4):
                    j, t = divmod(i, 2)
                    transposes(s(f"yT{i}"), [reg("B", f"G{2 + j}")[:, t, P * q:P * q + P] for q in range(4)], (sig("mix_sum"), 2 * l + j + 1))
                for i in range(4):
                    pe.wait_ge(*read_out(s(f"yT{i}")))
                for j in range(2):
                    units(s(f"M{j}"), lambda k, t: reg("B", f"G{2 + k // 4}")[:, t, P * (k % 4):P * (k % 4) + P], 2)
                for i in range(4):
                    t, q = divmod(i, 2)
                    transposes(s(f"fT{i}"), [xs2[:, t, (4 * q + j) * P:(4 * q + j + 1) * P] for j in range(4)],
                               (sig("x_normed_b"), 2 * l + 2))
                for i in range(4):
                    pe.wait_ge(*read_out(s(f"fT{i}")))

                def hidden_T(j):
                    transposes(s(f"HT{j}"), [hid[:, j, t, P * q:P * q + P] for t in range(TT) for q in range(2)],
                               (group_read[GROUP_NO[s(f"F{j}")] % 2], GROUP_NO[s(f"F{j}")] // 2 + 1))
                for j in range(FF_G):
                    units(s(f"F{j}"), from_hT, 2)
                    if j >= 1:
                        hidden_T(j - 1)
                hidden_T(FF_G - 1)
                for j in range(FF_G - 4, FF_G):
                    pe.wait_ge(*read_out(s(f"HT{j}")))
                for j in range(2):
                    units(s(f"E{j}"), lambda k, t: hid[:, k // 2, t, P * (k % 2):P * (k % 2) + P], -(-KF // UNIT_K))
            assert state["unit"] == len(UNITS) and state["step"] == len(STEPS)

        @block.scalar
        def _(act):
            chain = [0]

            def a(ins):
                chain[0] += 1
                ins.then_inc(a_chain, 1)
                act.wait_ge(a_chain, chain[0])

            def move(name, func=ACT.Copy):
                act.wait_ge(*summed(name))
                nc.scalar.activation(reg(name[0], name[3:]), group_banks(name), func).then_inc(group_read[GROUP_NO[name] % 2], 1)

            for name, src in (("norm_g", "norm_g"), ("mem_norm_g", "mem_norm_g"), ("mix_pre", "mix_pre_norm_2"),
                              ("ffn_pre", "ffn_pre_norm_2"), ("lb", "hgrn_lb_logits"), ("pool_scale", "pool_scale_2")):
                r0, k = COL_A[name]
                act.dma_start(small[r0:r0 + DEPTH * k, 0:P], w[src].rearrange("l (k p) -> (l k) p", p=P)).then_inc(loaded["rows"], 16)
            act.dma_start(small[0:COL_B_ROWS, P:2 * P], w["dn_conv_2"].rearrange("l w (k p) -> (l w k) p", p=P)).then_inc(loaded["rows"], 16)
            act.dma_start(pos[:, :], w["positions"][0].rearrange("(t p) -> p t", p=P), allow_slow_non_contiguous=True).then_inc(loaded["gain1"], 16)
            for l in range(DEPTH):
                for dst, src in ((g_qk[:, l, 0], "moba_q_norm"), (g_qk[:, l, 1], "moba_k_norm"), (g_mq[:, l], "mem_q_norm"),
                                 (g_mk[:, l], "mem_k_norm"), (g_ho[:, l], "hgrn_o_norm"), (a_log[:, l], "dn_A_log_2"),
                                 (dt_bias[:, l], "dn_dt_bias_2")):
                    act.dma_start(dst, w[src][l:l + 1].to_broadcast([P, dst.shape[1]])).then_inc(loaded["gain1"], 16)
                act.dma_start(w_ba[:, l], w["w_in_2"][l, :, BA_COL:BA_COL + 8].rearrange("(k p) n -> p k n", p=P)).then_inc(loaded["ba"], 16)
            act.wait_ge(sig("angles"), 1)
            a(nc.scalar.activation(rot[:, 1, 0:2, :], small[:, 320:336].rearrange("p (t j) -> p t j", t=2), ACT.Sin))
            nc.scalar.activation(rot[:, 0, 0:2, :], small[:, 336:352].rearrange("p (t j) -> p t j", t=2), ACT.Sin).then_inc(sig("rot_ready"), 1)
            act.wait_ge(loaded["mem"], 16)
            for t in range(TT):
                ins = nc.scalar.activation(region(a_PT, TT, D)[:, t], region(a_S, TT, D)[:, t], ACT.Square, accum_out=small[:, 360 + t:361 + t])
            ins.then_inc(sig("mem_squared"), 1)

            for l in range(DEPTH):
                s = lambda n: f"A{l}.{n}"
                if l == 0:
                    act.wait_ge(loaded["x"], 16)
                    act.wait_ge(sig("mem_scaled"), 1)
                else:
                    act.wait_ge(*taken(f"A{l - 1}.O1"))
                for t in range(TT):
                    ins = nc.scalar.activation(sq[:, t * D:(t + 1) * D], x[:, t, :], ACT.Square, accum_out=small[:, 360 + t:361 + t])
                ins.then_inc(sig("x_squared"), 1)
                for g in ("KM", "VM", "QH", "FH"):
                    move(s(g))
                act.wait_ge(sig("hg_q_in"), l + 1)
                nc.scalar.activation(etmp, qs, ACT.Sigmoid).then_inc(sig("hg_q_sig"), 1)
                act.wait_ge(sig("hg_f_in"), l + 1)
                a(nc.scalar.activation(ks, cum, ACT.Sigmoid, scale=-1.0))
                a(nc.scalar.activation(dtmp, dtmp, ACT.Exp, scale=-1.0))
                nc.scalar.activation(dtmp, dtmp, ACT.Ln, bias=1.0).then_inc(sig("hg_ln"), 1)
                move(s("IH"))
                if l > 0:
                    act.wait_ge(sig("hg_lb_in"), l)
                    a(nc.scalar.activation(dtmp, dtmp, ACT.Exp, scale=-1.0))
                    nc.scalar.activation(dtmp, dtmp, ACT.Ln, bias=1.0).then_inc(sig("hg_lb_ln"), 1)
                after_level = {1: ["QA"], 2: ["KA"], 4: ["VA"], 6: ["QM"]}
                for n in range(1, 9):
                    act.wait_ge(sig("hg_diff"), 8 * l + n)
                    m = 2 ** (n - 1)
                    if n < 8:
                        dv = dtmp.rearrange("p h (b m) -> p (h b) m", m=2 * m)
                        ev = etmp.rearrange("p h (b m) -> p (h b) m", m=2 * m)
                        left, right = (dv[:, :, 0:m], ev[:, :, 0:m]), (dv[:, :, m:], ev[:, :, m:])
                    else:
                        left, right = (dtmp[:, :, 0:P], etmp[:, :, 0:P]), (dtmp[:, :, P:S], etmp[:, :, P:S])
                    nc.scalar.activation(left[1], left[0], ACT.Exp, scale=-1.0)
                    nc.scalar.activation(right[1], right[0], ACT.Exp).then_inc(sig("hg_exp"), 1)
                    for g in after_level.get(n, []):
                        move(s(g))
                    if n in (6, 8):
                        for h in range(4 * (n // 8), 4 * (n // 8) + 4):
                            act.wait_ge(sig("attn_max"), 2 * l + n // 8 + 1)
                            for t in range(TT):
                                sc = sco[:, h, 0:P] if t == 0 else sco[:, h, P:3 * P]
                                nc.scalar.activation(sc, sc, ACT.Exp, bias=small[:, 368 + 8 * t + h:369 + 8 * t + h],
                                                     accum_out=small[:, 384 + 8 * t + h:385 + 8 * t + h]).then_inc(sig("attn_probs"), 1)
                for j in range(3):
                    move(s(f"Z{j}"))
                    act.wait_ge(*taken(s(f"Z{j}")))
                    act.wait_ge(*((sig("hg_factors"), 9 * (l + 1)) if j == 0 else (sig("y_ready"), 3 * l + j)))
                    nc.scalar.activation(region(a_memT, TT, G), reg("A", f"Z{j}"), ACT.Sigmoid).then_inc(sig("z_sig"), 1)
                    if j == 0:
                        for h in range(NH):
                            act.wait_ge(sig("mem_max"), NH * l + h + 1)
                            for t in range(TT):
                                ins = nc.scalar.activation(msc[:, h, t, :], bank(s(f"ms{h}"), TT, MEM)[:, t, :], ACT.Exp, scale=P ** -0.5,
                                                           bias=small[:, 400 + 4 * t + h:401 + 4 * t + h],
                                                           accum_out=small[:, 408 + 4 * t + h:409 + 4 * t + h])
                            ins.then_inc(step_read[STEP_NO[s(f"ms{h}")] % 4], 1)
                if l == 0:
                    act.wait_ge(sig("lb_in"), 1)
                    a(nc.scalar.activation(small[:, 496:504], small[:, 488:496], ACT.Exp, scale=-1.0))
                    nc.scalar.activation(small[:, 496:504], small[:, 496:504], ACT.Ln, bias=1.0).then_inc(sig("lb_ln"), 1)
                    nc.scalar.activation(lbs[:, 8:12], small[:, 484:488], ACT.Sigmoid).then_inc(sig("lb_sig"), 1)

            for l in range(DEPTH):
                s = lambda n: f"B{l}.{n}"

                def squares(src, asked, done):
                    act.wait_ge(*asked)
                    for t in range(TT):
                        ins = nc.scalar.activation(xs2[:, t, :], src[:, t, :], ACT.Square, accum_out=small[:, 360 + t:361 + t])
                    ins.then_inc(done, 1)

                def result(name):
                    act.wait_ge(*summed(name))
                    j = int(name[-1])
                    for t in range(TT):
                        a(nc.scalar.activation(mres[:, j, t, :], group_bank(name, t), ACT.Copy))
                        ins = nc.scalar.activation(xs2[:, j, t * G:(t + 1) * G], group_bank(name, t), ACT.Square,
                                                   accum_out=small[:, 364 + 2 * j + t:365 + 2 * j + t])
                    ins.then_inc(group_read[GROUP_NO[name] % 2], 1)
                squares(x, (sig("x_summed"), 2 * l) if l else taken(f"A{DEPTH - 1}.O1"), sig("x_squared_b"))
                for dst, src in ((g_do, w["dn_out_norm_2"][l:l + 1]), (g_ro, w["ret_out_norm_2"][l:l + 1]),
                                 (g_mp, w["mix_post_norm_2"][l:l + 1]), (g_fp, w["ffn_post_norm_2"][l:l + 1])):
                    act.dma_start(dst, src.to_broadcast([P, dst.shape[1]])).then_inc(loaded["post"], 16)
                act.dma_start(pw, w["pool_w_2"][l].rearrange("g c d -> c g d")).then_inc(loaded["post"], 16)
                for g in ("Q", "K", "V"):
                    move(s(g))
                act.wait_ge(sig("ba_in"), l + 1)
                nc.scalar.activation(small[:, 16:24], small[:, 24:32], ACT.Sigmoid).then_inc(sig("beta_ready"), 1)
                a(nc.scalar.activation(small[:, 40:48], small[:, 32:40], ACT.Exp, scale=-1.0))
                a(nc.scalar.activation(small[:, 48:52], a_log[:, l], ACT.Exp))
                nc.scalar.activation(small[:, 40:48], small[:, 40:48], ACT.Ln, bias=1.0).then_inc(sig("gate_parts"), 1)
                move(s("RQ"))
                for j in range(3):
                    act.wait_ge(sig("conv_in"), 3 * l + j + 1)
                    nc.scalar.activation(e3[:, 4 * j:4 * j + 4, :], cT3s(j), ACT.Sigmoid).then_inc(sig("conv_sig"), 1)
                move(s("RK"))
                act.wait_ge(sig("decay_in"), l + 1)
                nc.scalar.activation(yl, yl, ACT.Exp).then_inc(sig("decay_exp"), 1)
                nc.scalar.activation(small[:, 80:96], small[:, 56:72], ACT.Exp)
                nc.scalar.activation(eg, bank(s("gb1"), NH, P), ACT.Exp).then_inc(step_read[STEP_NO[s("gb1")] % 4], 1)
                move(s("RV"))
                order = ["PU", "RG", "DZ", "G2", "G3", "G4", "G5", "G0", "G1"]
                filled, moved = 0, 0
                for n in range(len(LEVELS)):
                    for t in range(TT):
                        act.wait_ge(*computed(s(f"Y{n}_{t}")))
                        nc.scalar.activation(yl[:, t], bank(s(f"Y{n}_{t}"), NH, P), ACT.Copy).then_inc(step_read[STEP_NO[s(f"Y{n}_{t}")] % 4], 1)
                    filled += 2
                    while moved < filled // 2:
                        g = order[moved]
                        move(s(g), ACT.Sigmoid if g[0] == "G" else ACT.Copy)
                        moved += 1
                act.wait_ge(*computed(s("u0")))
                nc.scalar.activation(vn[:, 0], bank(s("u0"), NH, P), ACT.Copy).then_inc(step_read[STEP_NO[s("u0")] % 4], 1)
                act.wait_ge(*computed(s("wT")))
                nc.scalar.activation(wT_, bank(s("wT"), NH, P), ACT.Copy, scale=-1.0).then_inc(step_read[STEP_NO[s("wT")] % 4], 1)
                act.wait_ge(*computed(s("st")))
                nc.scalar.activation(ss_, bank(s("st"), NH, P), ACT.Copy).then_inc(step_read[STEP_NO[s("st")] % 4], 1)
                act.wait_ge(*computed(s("vn1")))
                nc.scalar.activation(vn[:, 1], bank(s("vn1"), NH, P), ACT.Copy).then_inc(step_read[STEP_NO[s("vn1")] % 4], 1)
                act.wait_ge(*read_out(s(f"W{len(LEVELS) - 1}_1")))
                nc.scalar.activation(region(b_x, TT, G), reg("B", "RG"), ACT.Sigmoid)
                nc.scalar.activation(region(b_x + 1024, TT, G), reg("B", "DZ"), ACT.Sigmoid).then_inc(sig("out_sig"), 1)
                for g in order[moved:]:
                    move(s(g), ACT.Sigmoid)
                act.wait_ge(sig("mix_sum"), 2 * l + 2)
                for j in range(2):
                    result(s(f"M{j}"))
                squares(x, (sig("x_summed"), 2 * l + 1), sig("x_squared_b"))
                for j in range(FF_G):
                    act.wait_ge(*summed(s(f"F{j}")))
                    nc.scalar.activation(sg[:, j % 2], group_banks(s(f"F{j}"))[:, :, 0:256], ACT.Sigmoid).then_inc(sig("ff_sig"), 1)
                for j in range(2):
                    result(s(f"E{j}"))

        @block.vector
        def _(dve):
            chain = [0]
            pows = [0]

            def v(ins):
                chain[0] += 1
                ins.then_inc(v_chain, 1)
                dve.wait_ge(v_chain, chain[0])

            def evac(ins, step):
                ins.then_inc(step_read[STEP_NO[step] % 4], 1)
                dve.wait_ge(*read_out(step))

            def mul(o, i0, i1):
                return nc.vector.tensor_tensor(o, i0, i1, ALU.mult)

            def add(o, i0, i1):
                return nc.vector.tensor_tensor(o, i0, i1, ALU.add)

            def sub(o, i0, i1):
                return nc.vector.tensor_tensor(o, i0, i1, ALU.subtract)

            def rstd(src, n, scale, eps):
                pows[0] += 1
                nc.vector.tensor_scalar(rs_in[:, 0:n], src, scale, eps, ALU.mult, ALU.add).then_inc(pow_asked, 1)
                dve.wait_ge(pow_given, pows[0])
                return rs_out[:, 0:n]

            def over(v2, n, d):
                return v2[:, :, None].to_broadcast([P, n, d])

            def head_norm(vw, n, d, gain, scale, eps, tmp2):
                v(mul(tmp2, vw, vw))
                v(nc.vector.tensor_reduce(small[:, 420:420 + n], tmp2, X, ALU.add))
                r = rstd(small[:, 420:420 + n], n, scale, eps)
                v(mul(vw, vw, over(r, n, d)))
                if gain is not None:
                    v(mul(vw, vw, gain))

            def absolute(o, i):
                return nc.vector.scalar_tensor_tensor(o, i, -1.0, i, ALU.mult, ALU.max)

            def copy(o, i):
                return nc.vector.tensor_copy(o, i)

            v(nc.vector.memset(minus_half[:, :], -0.5))
            v(nc.vector.memset(rs_in[:, :], 1.0))
            v(nc.vector.memset(QT, 0.0))
            v(nc.vector.memset(region(a_qm, 4096), 0.0))
            v(nc.vector.memset(restart, 1.0))
            v(nc.vector.memset(restart.rearrange("p (c i) -> p c i", i=64)[:, :, 0:1], 0.0))
            dve.wait_ge(loaded["rows"], 16 * 7)
            nc.vector.memset(region(a_st, 1024), 0.0).then_inc(sig("v_start"), 1)
            dve.wait_ge(loaded["const"], 16)
            dve.wait_ge(loaded["gain1"], 16 * (1 + 7 * DEPTH))
            dve.wait_ge(*computed("colA"))
            evac(copy(cols[:, 0:COL_A_ROWS], bank("colA", COL_A_ROWS)), "colA")
            dve.wait_ge(*computed("colB"))
            evac(copy(cols[:, COL_A_ROWS:], bank("colB", COL_B_ROWS)), "colB")

            def col(name, l):
                r0, k = COL_A[name]
                return cols[:, r0 + l * k:r0 + (l + 1) * k]
            pf, ang, turns = small[:, 288:290], small[:, 304:320].rearrange("p (t j) -> p t j", t=2), small[:, 352:360]
            an = small[:, 304:320]
            red, co, tr = small[:, 320:336], small[:, 336:352], small[:, 440:456]
            v(nc.vector.tensor_scalar(pf, pos[:, :], 1.0, None, ALU.mult))
            v(mul(ang, pf[:, :, None].to_broadcast([P, 2, ROT]), C("inv_freq")[:, None, :].to_broadcast([P, 2, ROT])))
            v(nc.vector.tensor_scalar(tr, an, float(1 / (2 * np.pi)), ROUND_MAGIC, ALU.mult, ALU.add))
            v(nc.vector.tensor_scalar(tr, tr, ROUND_MAGIC, None, ALU.subtract))
            v(nc.vector.scalar_tensor_tensor(red, tr, -TWO_PI_PARTS[0], an, ALU.mult, ALU.add))
            v(nc.vector.scalar_tensor_tensor(red, tr, -TWO_PI_PARTS[1], red, ALU.mult, ALU.add))
            v(nc.vector.scalar_tensor_tensor(red, tr, -TWO_PI_PARTS[2], red, ALU.mult, ALU.add))
            v(nc.vector.tensor_scalar(red, red, 3.1415925, -3.1415925, ALU.min, ALU.max))
            v(nc.vector.scalar_tensor_tensor(co, red, -1.0, red, ALU.mult, ALU.min))
            nc.vector.tensor_scalar(co, co, float(np.pi / 2), None, ALU.add).then_inc(sig("angles"), 1)
            dve.wait_ge(sig("rot_ready"), 1)
            v(copy(rot[:, :, 2:4, :], rot[:, :, 0:2, :]))
            dve.wait_ge(sig("mem_squared"), 1)
            r = rstd(small[:, 360:362], 2, 1.0 / D, 1e-6)
            mem_in = region(a_S, TT, D)
            v(nc.vector.tensor_scalar(mem_in[:, 0], mem_in[:, 0], r[:, 0:1], None, ALU.mult))
            nc.vector.tensor_scalar(mem_in[:, 1], mem_in[:, 1], r[:, 1:2], None, ALU.mult).then_inc(sig("mem_normed"), 1)
            for i in range(4):
                t, q = divmod(i, 2)
                dve.wait_ge(*computed(f"memT{i}"))
                evac(copy(mem_hat[:, t, 4 * q:4 * q + 4, :], bank(f"memT{i}", 4, P)), f"memT{i}")
            def normed_T(step, src_gain, dst):
                dve.wait_ge(*computed(step))
                evac(mul(dst, bank(step, 4, P), src_gain[:, :, None].to_broadcast([P, 4, P])), step)

            for l in range(DEPTH):
                s = lambda n: f"A{l}.{n}"
                for t in range(TT):
                    ins = mul(mem_s[:, t], mem_hat[:, t], col("mem_norm_g", l)[:, :, None].to_broadcast([P, KD, P]))
                ins.then_inc(sig("mem_scaled"), 1)
                dve.wait_ge(sig("x_squared"), l + 1)
                r = rstd(small[:, 360:362], 2, 1.0 / D, 1e-6)
                v(nc.vector.tensor_scalar(xs[:, 0], x[:, 0], r[:, 0:1], None, ALU.mult))
                nc.vector.tensor_scalar(xs[:, 1], x[:, 1], r[:, 1:2], None, ALU.mult).then_inc(sig("x_normed"), 1)
                for i in range(4):
                    t, q = divmod(i, 2)
                    normed_T(s(f"xT{i}"), col("norm_g", l)[:, 4 * q:4 * q + 4], hT[:, t, 4 * q:4 * q + 4, :])

                def group_in(g):
                    n = GROUP_NO[s(g)]
                    return group_read[n % 2], n // 2 + 1
                dve.wait_ge(*group_in("KM"))
                km = heads(reg("A", "KM"))
                v(mul(sq[:, 0:1024].rearrange("p (n d) -> p n d", n=8), km, km))
                v(nc.vector.tensor_reduce(small[:, 420:428], sq[:, 0:1024].rearrange("p (n d) -> p n d", n=8), X, ALU.add))
                r = rstd(small[:, 420:428], 8, 1.0 / P, 1e-6)
                v(mul(km, km, over(r, 8, P)))
                mul(km, km, g_mk[:, l][:, None, :].to_broadcast([P, 8, P])).then_inc(sig("km_normed"), 1)
                for t in range(TT):
                    dve.wait_ge(*computed(s(f"kmT{t}")))
                    evac(copy(reg("A", "KM")[:, t, :], bank(s(f"kmT{t}"))), s(f"kmT{t}"))
                for t in range(TT):
                    dve.wait_ge(*computed(s(f"qhT{t}")))
                    evac(copy(qs[:, :, t * P:t * P + P], bank(s(f"qhT{t}"), NH, P)), s(f"qhT{t}"))
                nc.vector.memset(hst, 0.0).then_inc(sig("hg_q_in"), 1)
                for t in range(TT):
                    dve.wait_ge(*computed(s(f"fhT{t}")))
                    evac(copy(cum[:, :, t * P:t * P + P], bank(s(f"fhT{t}"), NH, P)), s(f"fhT{t}"))
                dve.wait_ge(sig("hg_q_sig"), l + 1)
                v(mul(qs, qs, etmp))
                absolute(dtmp, cum).then_inc(sig("hg_f_in"), 1)
                dve.wait_ge(sig("hg_ln"), l + 1)
                v(nc.vector.scalar_tensor_tensor(etmp, cum, 0.0, dtmp, ALU.min, ALU.subtract))
                if l > 0:
                    v(add(etmp, etmp, lbs[:, 4:8][:, :, None].to_broadcast([P, NH, S])))
                    v(sub(dtmp, etmp, lbs[:, 0:4][:, :, None].to_broadcast([P, NH, S])))
                    absolute(dtmp, dtmp).then_inc(sig("hg_lb_in"), 1)
                    v(nc.vector.tensor_tensor(etmp, etmp, lbs[:, 0:4][:, :, None].to_broadcast([P, NH, S]), ALU.max))
                    v(mul(ks, ks, lbs[:, 8:12][:, :, None].to_broadcast([P, NH, S])))
                    dve.wait_ge(sig("hg_lb_ln"), l)
                    v(add(etmp, etmp, dtmp))
                nc.vector.tensor_tensor_scan(cum.rearrange("p h s -> p (h s)"), restart, etmp.rearrange("p h s -> p (h s)"),
                                             0.0, ALU.mult, ALU.add).then_inc(sig("hg_factors"), 1)
                dve.wait_ge(sig("hg_factors"), 9 * l + 1)

                def factors(n):
                    m = 2 ** (n - 1)
                    q2, k2 = qmul[n % 2], kmul[n % 2]
                    ends = cum.rearrange("p h (c i) -> p h c i", i=64)[:, :, :, 63:64].rearrange("p h c o -> p h (c o)")
                    if n <= 6:
                        b = cum.rearrange("p h (b m) -> p (h b) m", m=2 * m)
                        dv = dtmp.rearrange("p h (b m) -> p (h b) m", m=2 * m)
                        sub(dv, b, b[:, :, m - 1:m].to_broadcast([P, 1024 // (2 * m), 2 * m])).then_inc(sig("hg_diff"), 1)
                    else:
                        c4 = cum.rearrange("p h (c i) -> p (h c) i", i=64)
                        d4 = dtmp.rearrange("p h (c i) -> p (h c) i", i=64)
                        if n == 7:
                            v(copy(d4[:, 1::2, :], c4[:, 1::2, :]))
                            sub(d4[:, 0::2, :], c4[:, 0::2, :], c4[:, 0::2, 63:64].to_broadcast([P, 8, 64])).then_inc(sig("hg_diff"), 1)
                        else:
                            c5 = cum.rearrange("p h (c i) -> p h c i", i=64)
                            d5 = dtmp.rearrange("p h (c i) -> p h c i", i=64)
                            two = small[:, 472:476][:, :, None]
                            v(add(two, c5[:, :, 0, 63:64], c5[:, :, 1, 63:64]))
                            v(copy(d5[:, :, 2, :], c5[:, :, 2, :]))
                            v(add(d5[:, :, 3, :], c5[:, :, 3, :], c5[:, :, 2, 63:64].to_broadcast([P, NH, 64])))
                            v(sub(d5[:, :, 1, :], c5[:, :, 1, :], c5[:, :, 1, 63:64].to_broadcast([P, NH, 64])))
                            sub(d5[:, :, 0, :], c5[:, :, 0, :], two.to_broadcast([P, NH, 64])).then_inc(sig("hg_diff"), 1)
                    dve.wait_ge(sig("hg_exp"), 8 * l + n)
                    mm = min(m, P)

                    def half(z, right):
                        z2 = z.rearrange("p h (b m) -> p (h b) m", m=2 * mm)
                        return z2[:, :, mm:] if right else z2[:, :, 0:mm]
                    v(mul(half(k2, False), half(ks, False), half(etmp, False)))
                    mul(half(q2, True), half(qs, True), half(etmp, True)).then_inc(sig("hg_factors"), 1)
                    dve.wait_ge(sig("hg_factors"), 9 * l + n + 1)

                def collect(n):
                    for t in (range(TT) if n < 8 else (1,)):
                        st = s(f"hg{n}_{t}")
                        dve.wait_ge(*computed(st))
                        if n == 8:
                            evac(copy(hst_off, bank(st, NH, P)), st)
                            continue
                        mask = (ident if n == 0 else level[:, n - 1, :]).bitcast(mybir.dt.uint32)
                        evac(nc.vector.copy_predicated(hst[:, t], mask[:, None, :].to_broadcast([P, NH, P]), bank(st, NH, P)), st)
                factors(1)
                collect(0)
                factors(2)
                collect(1)
                dve.wait_ge(*group_in("QA"))
                dve.wait_ge(*group_in("KA"))
                qk = region(R1["QA"], 32, DH_A)
                head_norm(qk, 32, DH_A, None, 1.0 / DH_A, 1e-6, sq.rearrange("p (n d) -> p n d", n=32))
                qk2 = region(R1["QA"], 2, 16, DH_A)
                v(mul(qk2, qk2, g_qk[:, l][:, :, None, :].to_broadcast([P, 2, 16, DH_A])))
                factors(3)
                collect(2)
                qkr = region(R1["QA"], 4, NH_A, DH_A)
                x1, x2 = qkr[:, :, :, 0:ROT], qkr[:, :, :, ROT:2 * ROT]
                cosv, sinv = (rot[:, i][:, :, None, :].to_broadcast([P, 4, NH_A, ROT]) for i in range(2))
                ta, tb = (sq[:, 256 * i:256 * i + 256].rearrange("p (a h j) -> p a h j", a=4, h=NH_A) for i in range(2))
                v(mul(ta, x1, sinv))
                v(mul(tb, x2, sinv))
                v(mul(x1, x1, cosv))
                v(sub(x1, x1, tb))
                v(mul(x2, x2, cosv))
                add(x2, x2, ta).then_inc(sig("qk_rotated"), 1)
                factors(4)
                collect(3)
                factors(5)
                collect(4)
                for t in range(TT):
                    st = s(f"qaT{t}")
                    dve.wait_ge(*computed(st))
                    v(copy(QT[0:64, 0:8:2, t * P:t * P + P], bank(st, 4, P)[0:64]))
                    evac(copy(QT[64:128, 1:8:2, t * P:t * P + P], bank(st, 4, P)[64:128]), st)
                for t in range(TT):
                    dve.wait_ge(*computed(s(f"kaT{t}")))
                    evac(copy(KT[:, :, t * P:t * P + P], bank(s(f"kaT{t}"), 4, P)), s(f"kaT{t}"))

                def attn_scores(h0):
                    for h in range(h0, h0 + 4):
                        dve.wait_ge(*computed(s(f"sc{h}")))
                        evac(nc.vector.scalar_tensor_tensor(sco[:, h, :], bank(s(f"sc{h}"), 384), DH_A ** -0.5, C("causal"),
                                                            ALU.mult, ALU.add), s(f"sc{h}"))
                    v(nc.vector.tensor_reduce(small[:, 368 + h0:372 + h0], sco[:, h0:h0 + 4, 0:P], X, ALU.max, negate=True))
                    nc.vector.tensor_reduce(small[:, 376 + h0:380 + h0], sco[:, h0:h0 + 4, P:3 * P], X, ALU.max, negate=True)\
                        .then_inc(sig("attn_max"), 1)
                factors(6)
                collect(5)
                attn_scores(0)
                factors(7)
                collect(6)
                attn_scores(4)
                factors(8)
                collect(7)
                collect(8)
                for h in range(8):
                    dve.wait_ge(*computed(s(f"pt{h}")))
                    evac(copy(prT[:, h, :], bank(s(f"pt{h}"), 384)), s(f"pt{h}"))
                v(nc.vector.reciprocal(small[:, 384:400], small[:, 384:400]))

                def gate(j, o):
                    dve.wait_ge(sig("z_sig"), 3 * l + j + 1)
                    z = reg("A", f"Z{j}")
                    v(mul(z, z, region(a_memT, TT, G)))
                    mul(z, z, o).then_inc(sig("y_ready"), 1)
                    dve.wait_ge(sig("y_ready"), 3 * l + j + 1)
                for t in range(TT):
                    st = s(f"oa{t}")
                    dve.wait_ge(*computed(st))
                    evac(mul(o_tmp[:, t].rearrange("p (h d) -> p h d", h=NH_A), bank(st, NH_A, DH_A),
                             over(small[:, 384 + 8 * t:392 + 8 * t], NH_A, DH_A)), st)
                dve.wait_ge(*group_in("QM"))
                qm = heads(reg("A", "QM"))
                sq8 = region(a_B, 8, P)
                v(mul(sq8, qm, qm))
                v(nc.vector.tensor_reduce(small[:, 420:428], sq8, X, ALU.add))
                r = rstd(small[:, 420:428], 8, 1.0 / P, 1e-6)
                v(mul(qm, qm, over(r, 8, P)))
                mul(qm, qm, g_mq[:, l][:, None, :].to_broadcast([P, 8, P])).then_inc(sig("qm_normed"), 1)
                gate(0, o_tmp)
                for t in range(TT):
                    dve.wait_ge(*computed(s(f"qmT{t}")))
                    evac(copy(reg("A", "QM")[:, t, :], bank(s(f"qmT{t}"))), s(f"qmT{t}"))
                for h in range(NH):
                    dve.wait_ge(*computed(s(f"ms{h}")))
                    mxv = small[:, 400:408].rearrange("p (t h) -> p t h", t=2)[:, :, h:h + 1]
                    v(nc.vector.tensor_reduce(mxv, bank(s(f"ms{h}"), TT, MEM), X, ALU.max, negate=True))
                    nc.vector.tensor_scalar(mxv, mxv, P ** -0.5, None, ALU.mult).then_inc(sig("mem_max"), 1)
                for t in range(TT):
                    dve.wait_ge(*computed(s(f"hgo{t}")))
                    evac(copy(o_tmp[:, t, :], bank(s(f"hgo{t}"))), s(f"hgo{t}"))
                ov = heads(o_tmp)
                head_norm(ov, 8, P, g_ho[:, l][:, None, :].to_broadcast([P, 8, P]), 1.0 / P, 1e-6, sq8)
                gate(1, o_tmp)
                for h in range(NH):
                    dve.wait_ge(*computed(s(f"mpt{h}")))
                    evac(copy(mprT[:, h], bank(s(f"mpt{h}"), 4, P)), s(f"mpt{h}"))
                v(nc.vector.reciprocal(small[:, 408:416], small[:, 408:416]))
                for t in range(TT):
                    st = s(f"om{t}")
                    dve.wait_ge(*computed(st))
                    evac(mul(o_tmp[:, t].rearrange("p (h d) -> p h d", h=NH), bank(st, NH, P),
                             over(small[:, 408 + 4 * t:412 + 4 * t], NH, P)), st)
                gate(2, o_tmp)
                for i in range(6):
                    j, t = divmod(i, 2)
                    dve.wait_ge(*computed(s(f"yT{i}")))
                    evac(copy(reg("A", f"Z{j}")[:, t, :], bank(s(f"yT{i}"))), s(f"yT{i}"))
                if l == 0:
                    dd, e = small[:, 480:488], small[:, 488:496]
                    v(sub(dd[:, 0:4], col("lb", 1), col("lb", 0)))
                    v(sub(dd[:, 4:8], col("lb", 0), col("lb", 1)))
                    absolute(e, dd).then_inc(sig("lb_in"), 1)
                for j in range(2):
                    dve.wait_ge(*summed(s(f"O{j}")))
                    for t in range(TT):
                        xv = x[:, t, G * j:G * j + G]
                        ins = add(xv, xv, group_bank(s(f"O{j}"), t))
                    ins.then_inc(group_read[GROUP_NO[s(f"O{j}")] % 2], 1)
                dve.wait_ge(*group_in("O1"))
                if l == 0:
                    dve.wait_ge(sig("lb_ln"), 1)
                    v(nc.vector.scalar_tensor_tensor(lbs[:, 0:8], dd, 0.0, small[:, 496:504], ALU.min, ALU.subtract))
                    dve.wait_ge(sig("lb_sig"), 1)

            for l in range(DEPTH):
                s = lambda n: f"B{l}.{n}"

                def group_in(g):
                    n = GROUP_NO[s(g)]
                    return group_read[n % 2], n // 2 + 1

                def norm_x(count, gain, prefix):
                    dve.wait_ge(sig("x_squared_b"), count)
                    r = rstd(small[:, 360:362], 2, 1.0 / D, 1e-6)
                    v(nc.vector.tensor_scalar(xs2[:, 0], x[:, 0], r[:, 0:1], None, ALU.mult))
                    nc.vector.tensor_scalar(xs2[:, 1], x[:, 1], r[:, 1:2], None, ALU.mult).then_inc(sig("x_normed_b"), 1)
                    for i in range(4):
                        t, q = divmod(i, 2)
                        normed_T(s(f"{prefix}{i}"), col(gain, l)[:, 4 * q:4 * q + 4], hT[:, t, 4 * q:4 * q + 4, :])

                def add_result(last, gain):
                    for j in range(2):
                        dve.wait_ge(*group_in(f"{last}{j}"))
                    v(add(small[:, 420:422], small[:, 364:366], small[:, 366:368]))
                    r = rstd(small[:, 420:422], 2, 1.0 / D, 1e-6)
                    for t in range(TT):
                        for j in range(2):
                            v(nc.vector.scalar_tensor_tensor(mres[:, j, t, :], mres[:, j, t, :], r[:, t:t + 1], gain[:, G * j:G * j + G],
                                                             ALU.mult, ALU.mult))
                            ins = add(x[:, t, G * j:G * j + G], x[:, t, G * j:G * j + G], mres[:, j, t, :])
                    ins.then_inc(sig("x_summed"), 1)
                norm_x(2 * l + 1, "mix_pre", "xT")
                for j in range(3):
                    for t in range(TT):
                        st = s(f"dT{j}{t}")
                        dve.wait_ge(*computed(st))
                        evac(copy(xT3[:, 4 * j:4 * j + 4, t * P:t * P + P], bank(st, 4, P)), st)
                dve.wait_ge(*computed(s("ba")))
                ba = bank(s("ba"), 2, 8)
                v(copy(small[:, 24:32].rearrange("p (t h) -> p t h", t=2), ba[:, :, 0:4]))
                evac(add(small[:, 104:112].rearrange("p (t h) -> p t h", t=2), ba[:, :, 4:8],
                         dt_bias[:, l][:, None, :].to_broadcast([P, 2, 4])), s("ba"))
                absolute(small[:, 32:40], small[:, 104:112]).then_inc(sig("ba_in"), 1)
                dve.wait_ge(sig("gate_parts"), l + 1)
                gates = small[:, 0:8]
                gates2 = gates.rearrange("p (t h) -> p t h", t=2)
                v(nc.vector.scalar_tensor_tensor(gates, small[:, 104:112], 0.0, small[:, 40:48], ALU.max, ALU.add))
                v(nc.vector.scalar_tensor_tensor(gates2, gates2, -1.0, small[:, 48:52][:, None, :].to_broadcast([P, 2, 4]), ALU.mult, ALU.mult))
                copy(gbc, gates[:, :, None].to_broadcast([P, 8, P])).then_inc(sig("gates_ready"), 1)
                taps = cols[:, COL_A_ROWS + 48 * l:COL_A_ROWS + 48 * (l + 1)].rearrange("p (w k) -> p w k", w=4)
                for j in range(3):
                    for k in range(4 * j, 4 * j + 4):
                        ins = nc.vector.tensor_scalar(cT3[:, k, :], xT3[:, k, :], taps[:, 3, k:k + 1], None, ALU.mult)
                    for d in (1, 2, 3):
                        v(ins)
                        for k in range(4 * j, 4 * j + 4):
                            ins = nc.vector.scalar_tensor_tensor(cT3[:, k, d:], xT3[:, k, 0:S - d], taps[:, 3 - d, k:k + 1], cT3[:, k, d:],
                                                                 ALU.mult, ALU.add)
                    ins.then_inc(sig("conv_in"), 1)
                for j in range(3):
                    dve.wait_ge(sig("conv_sig"), 3 * l + j + 1)
                    ins = mul(cT3s(j), cT3s(j), e3[:, 4 * j:4 * j + 4, :])
                ins.then_inc(sig("conv_done"), 1)
                dve.wait_ge(sig("conv_done"), l + 1)
                dve.wait_ge(*computed(s("cg")))
                v(copy(small[:, 56:64], bank(s("cg"))[:, 0:8]))
                evac(sub(small[:, 64:72], bank(s("cg"))[:, 8:16], small[:, 56:64]), s("cg"))
                dve.wait_ge(*computed(s("gb0")))
                evac(sub(yl[:, 0], bank(s("gb0"), NH, P), over(small[:, 56:60], NH, P)), s("gb0"))
                dve.wait_ge(*computed(s("gb1")))
                v(sub(yl[:, 1], bank(s("gb1"), NH, P), over(small[:, 60:64], NH, P)))
                nc.vector.tensor_scalar(yl, yl, 0.0, None, ALU.min).then_inc(sig("decay_in"), 1)
                for j, g in enumerate("QKV"):
                    for t in range(TT):
                        dve.wait_ge(*computed(s(f"bT{j}{t}")))
                        evac(copy(reg("B", g)[:, t, :], bank(s(f"bT{j}{t}"))), s(f"bT{j}{t}"))
                qk = region(R2["Q"], 16, P)
                qv, kv, vv = (heads(reg("B", g)) for g in "QKV")
                sq16 = sq2.rearrange("p (n d) -> p n d", n=16)
                v(mul(sq16, qk, qk))
                v(nc.vector.tensor_reduce(small[:, 420:436], sq16, X, ALU.add))
                r = rstd(small[:, 420:436], 16, 1.0, 1e-6)
                v(nc.vector.tensor_scalar(small[:, 420:428], r[:, 0:8], P ** -0.5, None, ALU.mult))
                v(mul(qv, qv, over(small[:, 420:428], 8, P)))
                v(mul(kv, kv, over(r[:, 8:16], 8, P)))
                dve.wait_ge(sig("beta_ready"), l + 1)
                kb8 = kb.rearrange("p t h d -> p (t h) d")
                v(mul(vv, vv, over(small[:, 16:24], 8, P)))
                mul(kb8, kv, over(small[:, 16:24], 8, P)).then_inc(sig("dn_normed"), 1)
                dve.wait_ge(sig("decay_exp"), l + 1)
                v(mul(decT.rearrange("p t h i -> p (t h) i"), yl.rearrange("p t h i -> p (t h) i"), upper[:, None, :].to_broadcast([P, 8, P])))
                dve.wait_ge(*read_out(s("gb1")))
                v(mul(ktl, kv[:, 0:4, :], over(small[:, 88:92], NH, P)))
                for n, dst in (("kT", kT), ("qT", qT), ("kbT", kbT)):
                    for t in range(TT):
                        dve.wait_ge(*computed(s(f"{n}{t}")))
                        evac(copy(dst[:, t], bank(s(f"{n}{t}"), NH, P)), s(f"{n}{t}"))
                v(mul(kb[:, 1], kb[:, 1], over(small[:, 84:88], NH, P)))
                v(mul(qd, qT[:, 1], eg))
                for n, dst in (("mm", mT), ("at", atT)):
                    for t in range(TT):
                        dve.wait_ge(*computed(s(f"{n}{t}")))
                        evac(mul(dst[:, t], bank(s(f"{n}{t}"), NH, P), decT[:, t]), s(f"{n}{t}"))
                iv, ivT = (z.rearrange("p t h i -> p (t h) i") for z in (inv, invT))
                v(copy(iv, ident[:, None, :].to_broadcast([P, 8, P])))
                v(copy(ivT, ident[:, None, :].to_broadcast([P, 8, P])))

                def level_mask(n):
                    mul(ml.rearrange("p t h i -> p (t h) i"), mT.rearrange("p t h i -> p (t h) i"),
                        level[:, n, :][:, None, :].to_broadcast([P, 8, P])).then_inc(sig("inv_ready"), 1)
                    dve.wait_ge(sig("inv_ready"), len(LEVELS) * l + n + 1)
                level_mask(0)
                for n in range(len(LEVELS)):
                    if n < len(LEVELS) - 1:
                        for t in range(TT):
                            st = s(f"Z{n}_{t}")
                            dve.wait_ge(*computed(st))
                            evac(sub(inv[:, t], inv[:, t], bank(st, NH, P)), st)
                    for t in range(TT):
                        st = s(f"W{n}_{t}")
                        dve.wait_ge(*computed(st))
                        evac(sub(invT[:, t], invT[:, t], bank(st, NH, P)), st)
                    if n < len(LEVELS) - 1:
                        level_mask(n + 1)
                    if n == 0:
                        dve.wait_ge(*group_in("RQ"))
                        dve.wait_ge(*group_in("RK"))
                        rr = region(R2["RQ"], 4, NH, P)
                        x1, x2 = rr[:, :, :, 0:64], rr[:, :, :, 64:P]
                        cosv, sinv = (C(n_).rearrange("p (a j) -> p a j", a=4)[:, :, None, :].to_broadcast([P, 4, NH, 64]) for n_ in ("cos", "sin"))
                        ta = region(b_tmp, 4, NH, 64)
                        tb = region(b_rst, 4, NH, 64)
                        v(mul(ta, x1, sinv))
                        v(mul(tb, x2, sinv))
                        v(mul(x1, x1, cosv))
                        v(sub(x1, x1, tb))
                        v(mul(x2, x2, cosv))
                        add(x2, x2, ta).then_inc(sig("ret_rotated"), 1)
                for t in range(TT):
                    dve.wait_ge(*computed(s(f"do{t}")))
                    evac(copy(reg("B", "Q")[:, t, :], bank(s(f"do{t}"))), s(f"do{t}"))
                for g, n in (("RQ", "rqT"), ("RK", "rkT")):
                    for t in range(TT):
                        dve.wait_ge(*computed(s(f"{n}{t}")))
                        evac(copy(reg("B", g)[:, t, :], bank(s(f"{n}{t}"))), s(f"{n}{t}"))
                for i in range(3):
                    dve.wait_ge(*computed(s(f"rs{i}")))
                    evac(mul(rst[:, i], bank(s(f"rs{i}"), NH, P), decay_c[:, i % 2]), s(f"rs{i}"))
                for t in range(TT):
                    dve.wait_ge(*computed(s(f"ro{t}")))
                    evac(copy(reg("B", "RQ")[:, t, :], bank(s(f"ro{t}"))), s(f"ro{t}"))
                for i in range(2):
                    dve.wait_ge(*computed(s(f"pm{i}")))
                    evac(copy(mx[:, 2 * i:2 * i + 2, :], bank(s(f"pm{i}"), 2, S)), s(f"pm{i}"))
                po = region(R2["PU"], 4, S)
                for i in range(2):
                    dve.wait_ge(*computed(s(f"py{i}")))
                    evac(mul(po[:, 2 * i:2 * i + 2, :], bank(s(f"py{i}"), 2, S),
                             col("pool_scale", l)[:, 2 * i:2 * i + 2][:, :, None].to_broadcast([P, 2, S])), s(f"py{i}"))
                dve.wait_ge(loaded["post"], 16 * 5 * (l + 1))
                ro = heads(reg("B", "RQ"))
                t8 = tmp.rearrange("p (n d) -> p n d", n=8)
                v(nc.vector.tensor_reduce(small[:, 420:428], ro, X, ALU.add))
                v(nc.vector.tensor_scalar(small[:, 420:428], small[:, 420:428], 1.0 / P, None, ALU.mult))
                v(sub(ro, ro, over(small[:, 420:428], 8, P)))
                v(mul(t8, ro, ro))
                v(nc.vector.tensor_reduce(small[:, 420:428], t8, X, ALU.add))
                r = rstd(small[:, 420:428], 8, 1.0 / P, 1e-5)
                v(mul(ro, ro, over(r, 8, P)))
                v(mul(reg("B", "RQ"), reg("B", "RQ"), g_ro[:, None, :].to_broadcast([P, TT, G])))
                dve.wait_ge(sig("out_sig"), l + 1)
                v(mul(reg("B", "RG"), reg("B", "RG"), region(b_x, TT, G)))
                mul(reg("B", "RQ"), reg("B", "RQ"), reg("B", "RG")).then_inc(sig("ret_out"), 1)
                for j in range(2):
                    n = s(f"BP{j}")
                    dve.wait_ge(*summed(n))
                    dve.wait_ge(*group_in(f"G{2 + j}"))
                    gt = reg("B", f"G{2 + j}")
                    mul(gt, gt, group_banks(n)).then_inc(group_read[GROUP_NO[n] % 2], 1)
                for t in range(TT):
                    dve.wait_ge(*computed(s(f"oT_r{t}")))
                    evac(copy(reg("B", "RQ")[:, t, :], bank(s(f"oT_r{t}"))), s(f"oT_r{t}"))
                od = heads(reg("B", "Q"))
                head_norm(od, 8, P, g_do[:, None, :].to_broadcast([P, 8, P]), 1.0 / P, 1e-6, sq2[:, 0:1024].rearrange("p (n d) -> p n d", n=8))
                v(mul(reg("B", "DZ"), reg("B", "DZ"), region(b_x + 1024, TT, G)))
                mul(reg("B", "Q"), reg("B", "Q"), reg("B", "DZ")).then_inc(sig("dn_out"), 1)

                def add_branch(b, g0, done):
                    for j in range(2):
                        n = s(f"{b}{j}")
                        dve.wait_ge(*summed(n))
                        gt = reg("B", f"G{g0 + j}")
                        mul(gt, gt, group_banks(n)).then_inc(group_read[GROUP_NO[n] % 2], 1)
                        dve.wait_ge(*taken(n))
                        acc = reg("B", f"G{2 + j}")
                        ins = add(acc, acc, gt)
                        if done:
                            ins.then_inc(sig("mix_sum"), 1)
                        else:
                            v(ins)
                add_branch("BR", 4, False)
                for t in range(TT):
                    dve.wait_ge(*computed(s(f"oT_d{t}")))
                    evac(copy(reg("B", "Q")[:, t, :], bank(s(f"oT_d{t}"))), s(f"oT_d{t}"))
                add_branch("BD", 0, True)
                for i in range(4):
                    j, t = divmod(i, 2)
                    dve.wait_ge(*computed(s(f"yT{i}")))
                    evac(copy(reg("B", f"G{2 + j}")[:, t, :], bank(s(f"yT{i}"))), s(f"yT{i}"))
                add_result("M", g_mp)
                norm_x(2 * l + 2, "ffn_pre", "fT")

                def hidden_out(j):
                    dve.wait_ge(*computed(s(f"HT{j}")))
                    evac(copy(hid[:, j].rearrange("p t c -> p (t c)"), bank(s(f"HT{j}"))), s(f"HT{j}"))
                for j in range(FF_G):
                    n = s(f"F{j}")
                    dve.wait_ge(sig("ff_sig"), FF_G * l + j + 1)
                    v(mul(sg[:, j % 2], sg[:, j % 2], group_banks(n)[:, :, 0:256]))
                    mul(hid[:, j], sg[:, j % 2], group_banks(n)[:, :, 256:512]).then_inc(group_read[GROUP_NO[n] % 2], 1)
                    if j >= 1:
                        hidden_out(j - 1)
                hidden_out(FF_G - 1)
                add_result("E", g_fp)


INS = ["x", "mem", "positions", "norm_g", "w_in", "w_out", "moba_q_norm", "moba_k_norm", "hgrn_lb_logits",
       "hgrn_o_norm", "mem_norm_g", "w_mem_kv", "mem_q_norm", "mem_k_norm", "mix_pre_norm_2", "mix_post_norm_2",
       "w_in_2", "dn_conv_2", "dn_A_log_2", "dn_dt_bias_2", "dn_out_norm_2", "ret_out_norm_2", "pool_w_2",
       "pool_scale_2", "w_branch_dn_2", "w_branch_ret_2", "w_branch_pool_2", "w_out_2", "ffn_pre_norm_2",
       "ffn_post_norm_2", "ffn_gate_2", "ffn_up_2", "ffn_down_2"]


def kernel(**inputs):
    import concourse.bacc as bacc
    from concourse.bass_utils import run_bass_kernel_spmd as run

    nc = bacc.Bacc("TRN2", target_bir_lowering=False, num_devices=1, dynamic_dma_scratch_size=1024)
    arrays = {n: np.ascontiguousarray(inputs[n]) for n in INS}
    arrays["shape_constants"] = shape_constants()
    w = {n: nc.dram_tensor("in_" + n, a.shape, mybir.dt.from_np(a.dtype), kind="ExternalInput").ap() for n, a in arrays.items()}
    out = nc.dram_tensor("out", (1, S, D), mybir.dt.float32, kind="ExternalOutput").ap()
    mixer_program(nc, w, out)
    return run(nc, [{"in_" + n: a for n, a in arrays.items()}], core_ids=[0]).results[0]["out"]
```

```python
import numpy as np
import concourse.bass as bass
from concourse import mybir
from contextlib import ExitStack

P = 128
S = 256
TT = S // P
D = 1024
KD = D // P
DEPTH = 2
G = D // 2
MEM = 256
F32_COLS = 512
NH_A, DH_A = 8, 64
NH = 4
ROT = 8
D_FF = 2816
FF_G = D_FF // 256
KF = D_FF // P
UNIT_K = 4
SLOTS = 4
POOL_WINDOWS = (2, 4, 8, 16)
LEVELS = (1, 2, 4, 8, 16, 32, 64)
NEG = -1.0e30
TWO_PI_PARTS = (6.28125, 0.0019350051879882812, 3.0199157663446385e-07)
ROUND_MAGIC = 12582912.0

CONST_WIDTHS = [("ident", P), ("inv_freq", ROT), ("upper", P), ("ones", P), ("causal", 3 * P),
                ("cos", 4 * 64), ("sin", 4 * 64), ("band", 4 * 3 * P), ("ret_decay", 2 * NH * P),
                ("level", len(LEVELS) * P)]
CONST_AT = {}
_at = 0
for _n, _w in CONST_WIDTHS:
    CONST_AT[_n] = (_at, _w)
    _at += _w
CONST_COLS = _at


def shape_constants():
    c = np.zeros((P, CONST_COLS), np.float32)

    def put(name, a):
        at, w = CONST_AT[name]
        c[:, at:at + w] = np.asarray(a, np.float64).reshape(P, w).astype(np.float32)

    i = np.arange(P)
    upper = (i[:, None] <= i[None, :])
    put("ident", np.eye(P))
    put("upper", upper)
    put("ones", np.ones((P, P)))
    late = np.where(upper.T, 0.0, NEG)
    put("causal", np.concatenate([late, np.zeros((P, P)), late], axis=1))
    inv = np.float32(500000.0) ** (-np.arange(ROT, dtype=np.float32) / np.float32(ROT))
    put("inv_freq", np.broadcast_to(inv, (P, ROT)))
    inv = np.float32(10000.0) ** (-np.arange(64, dtype=np.float32) / np.float32(64))
    ang = (np.arange(S, dtype=np.float32)[:, None] * inv[None]).reshape(TT, P, 64).transpose(1, 0, 2)
    put("cos", np.concatenate([np.cos(ang.astype(np.float64))] * 2, axis=1))
    put("sin", np.concatenate([np.sin(ang.astype(np.float64))] * 2, axis=1))
    t = np.arange(S)
    band = np.zeros((P, 4, 3, P))
    for g, win in enumerate(POOL_WINDOWS):
        m = ((t[None] <= t[:, None]) & (t[None] > t[:, None] - win)) / np.minimum(t + 1.0, win)[:, None] - np.eye(S)
        mt = m.T
        band[:, g, 0], band[:, g, 1], band[:, g, 2] = mt[:P, :P], mt[:P, P:], mt[P:, P:]
    put("band", band)
    dec = np.zeros((P, 2, NH, P))
    for h in range(NH):
        lg = np.log1p(-np.exp2(-5.0 - h))
        dist = t[:, None] - t[None]
        w = np.where(t[:, None] // 64 == t[None] // 64, np.exp(np.abs(dist) * lg),
                     np.where(t[:, None] // 64 > t[None] // 64, np.exp(np.maximum(dist, 0) * lg), 0.0))
        w = w.T * P ** -0.5
        dec[:, 0, h], dec[:, 1, h] = w[:P, :P], w[:P, P:]
    put("ret_decay", dec)
    lev = np.zeros((P, len(LEVELS), P))
    for n, m in enumerate(LEVELS):
        lev[:, n] = (i[:, None] // (2 * m) == i[None] // (2 * m)) & (i[:, None] % (2 * m) < m) & (i[None] % (2 * m) >= m)
    put("level", lev)
    return c


COL_A = {"norm_g": (0, KD), "mem_norm_g": (16, KD), "mix_pre": (32, KD), "ffn_pre": (48, KD),
         "lb": (64, NH), "pool_scale": (72, NH)}
COL_A_ROWS = 80
COL_B_ROWS = DEPTH * 4 * 12

ORDER_1 = [f"xT{i}" for i in range(4)] + ["kmT0", "kmT1"] \
    + [f"hg{n}_{t}" for n in range(5) for t in range(2)] + ["qaT0", "qaT1", "kaT0", "kaT1"] \
    + ["hg5_0", "hg5_1"] + [f"sc{h}" for h in range(4)] + ["hg6_0", "hg6_1"] + [f"sc{h}" for h in range(4, 8)] \
    + ["hg7_0", "hg7_1", "hg8_1"] + [f"pt{h}" for h in range(8)] + ["oa0", "oa1", "qmT0", "qmT1"] \
    + [f"ms{h}" for h in range(4)] + ["hgo0", "hgo1"] + [f"mpt{h}" for h in range(4)] + ["om0", "om1"] \
    + [f"yT{i}" for i in range(6)]
ORDER_2 = [f"xT{i}" for i in range(4)] + ["ba", "cg", "gb0", "gb1"] \
    + [f"bT{j}{t}" for j in range(3) for t in range(2)] \
    + ["kT0", "kT1", "qT0", "qT1", "kbT0", "kbT1", "mm0", "mm1", "at0", "at1"] \
    + [f"{s}{n}_{t}" for n in range(len(LEVELS)) for s in ("Y", "Z", "W") for t in range(2)
       if not (s == "Z" and n == len(LEVELS) - 1)] \
    + ["u0", "wT", "st", "vn1", "do0", "do1"] \
    + ["rqT0", "rqT1", "rkT0", "rkT1", "rs0", "rs1", "rs2", "ro0", "ro1", "pm0", "pm1", "py0", "py1",
       "oT_r0", "oT_r1", "oT_d0", "oT_d1"] \
    + [f"yT{i}" for i in range(4)] + [f"fT{i}" for i in range(4)]
PRE = ["memT0", "memT1", "memT2", "memT3", "colA", "colB"]
STEPS = PRE + [f"A{l}.{s}" for l in range(DEPTH) for s in ORDER_1] + [f"B{l}.{s}" for l in range(DEPTH) for s in ORDER_2]
STEP_NO = {s: n for n, s in enumerate(STEPS)}

GROUPS_1 = [("KM", KD), ("VM", KD), ("QH", KD), ("FH", KD), ("IH", KD), ("QA", KD), ("KA", KD), ("VA", KD),
            ("QM", KD), ("Z0", KD), ("Z1", KD), ("Z2", KD), ("O0", 12), ("O1", 12)]
GROUPS_2 = [("Q", KD), ("K", KD), ("V", KD), ("RQ", KD), ("RK", KD), ("RV", KD), ("PU", KD), ("RG", KD), ("DZ", KD)] \
    + [(f"G{j}", KD) for j in (2, 3, 4, 5, 0, 1)] \
    + [(f"BP{j}", NH) for j in range(2)] + [(f"BR{j}", NH) for j in range(2)] + [(f"BD{j}", NH) for j in range(2)] \
    + [("M0", KD), ("M1", KD)] + [(f"F{j}", KD) for j in range(FF_G)] + [("E0", KF), ("E1", KF)]
GROUPS = [(f"A{l}.{g}", k) for l in range(DEPTH) for g, k in GROUPS_1] + [(f"B{l}.{g}", k) for l in range(DEPTH) for g, k in GROUPS_2]
GROUP_NO = {g: n for n, (g, _) in enumerate(GROUPS)}
BY_COLUMN = {f"A{l}.{g}" for l in range(DEPTH) for g in ("QH", "FH")} \
    | {f"B{l}.{g}" for l in range(DEPTH) for g in ["Q", "K", "V"] + [f"F{j}" for j in range(FF_G)]}
COL_1 = {g: 512 * n for n, g in enumerate(["QA", "KA", "VA", "QH", "FH", "IH", "QM", "Z0", "Z1", "Z2"])}
COL_2 = {"Q": 0, "K": 512, "V": 1024, "DZ": 1536, "RQ": 2056, "RK": 2568, "RV": 3080, "RG": 3592, "PU": 4104}
COL_2.update({f"G{j}": 4616 + 512 * j for j in range(6)})
BA_COL = 2048


def weight_units():
    out = []
    for g, (_, k) in enumerate(GROUPS):
        for k0 in range(0, k, UNIT_K):
            out.append((g, k0, min(UNIT_K, k - k0)))
    return out


UNITS = weight_units()
SPLIT_MIX = {f"B{l}.{g}" for l in range(DEPTH) for g in COL_2}
SPLIT = SPLIT_MIX | {f"B{l}.{g}" for l in range(DEPTH) for g in [f"F{j}" for j in range(FF_G)] + ["E0", "E1"]}
MIX_HI = 2
AHEAD = 2
PART_K = 2
PARTS = [(u, k, min(PART_K, nk - k)) for u, (g, _, nk) in enumerate(UNITS) if GROUPS[g][0] in SPLIT for k in range(0, nk, PART_K)]


def parts_until(u):
    return sum(1 for v, _, _ in PARTS if v <= u)


def last_unit(group):
    return max(u for u, (g, _, _) in enumerate(UNITS) if g == GROUP_NO[group])


def first_unit(group):
    return min(u for u, (g, _, _) in enumerate(UNITS) if g == GROUP_NO[group])




def mixer_program(nc, w, out):
    F = mybir.dt.float32
    FR = mybir.dt.float32r
    ALU = mybir.AluOpType
    ACT = mybir.ActivationFunctionType
    X = mybir.AxisListType.X
    ctx = ExitStack()
    with ctx:
        def sb(name, shape, dt=F):
            return ctx.enter_context(nc.sbuf_tensor(name, shape, dt))

        def sem(name):
            return ctx.enter_context(nc.semaphore(name))

        wt = sb("wt", [P, SLOTS, UNIT_K, F32_COLS])
        wt_byte = nc.sbuf_base - 4 * SLOTS * UNIT_K * F32_COLS
        ARENA = 36992
        arena = sb("arena", [P, ARENA])
        arena_byte = nc.sbuf_base - 4 * ARENA
        const = sb("const", [P, CONST_COLS])
        x = sb("x", [P, TT, D])
        hT = sb("hT", [P, TT, KD, P])
        hT_byte = nc.sbuf_base - 4 * TT * KD * P
        cols = sb("cols", [P, COL_A_ROWS + COL_B_ROWS])
        rot = sb("rot", [P, 2, 4, ROT])
        pos = sb("pos", [P, TT], mybir.dt.int32)
        small = sb("small", [P, 512])
        rs_in = sb("rs_in", [P, 32])
        rs_out = sb("rs_out", [P, 32])
        minus_half = sb("minus_half", [P, 32])
        g_qk = sb("g_qk", [P, DEPTH, 2, DH_A])
        g_mq = sb("g_mq", [P, DEPTH, P])
        g_mk = sb("g_mk", [P, DEPTH, P])
        g_ho = sb("g_ho", [P, DEPTH, P])
        a_log = sb("a_log", [P, DEPTH, NH])
        dt_bias = sb("dt_bias", [P, DEPTH, NH])
        w_ba = sb("w_ba", [P, DEPTH, KD, 8])

        def C(name):
            at, width = CONST_AT[name]
            return const[:, at:at + width]

        ident, upper, ones = C("ident"), C("upper"), C("ones")
        level = C("level").rearrange("p (n i) -> p n i", n=len(LEVELS))
        band = C("band").rearrange("p (g b t) -> p g b t", g=4, b=3)
        decay_c = C("ret_decay").rearrange("p (b h t) -> p b h t", b=2, h=NH)

        def region(at, *shape):
            n = int(np.prod(shape))
            assert at + n <= ARENA
            v = arena[:, at:at + n]
            if len(shape) == 1:
                return v
            names = "abcd"[:len(shape)]
            return v.rearrange(f"p ({' '.join(names)}) -> p {' '.join(names)}",
                               **{c: s for c, s in zip(names[:-1], shape[:-1])})

        R1 = {g: 1024 * n for n, g in enumerate(["QH", "FH", "IH", "QA", "KA", "VA", "QM", "Z0", "Z1", "Z2", "KM", "VM"])}
        at = 12 * 1024

        def take(n):
            nonlocal at
            at += n
            return at - n
        a_memh, a_memT = take(2048), take(2048)
        a_qs, a_ks, a_B, a_qm, a_km, a_st, a_sto, a_rm = (take(1024), take(1024), take(1024), take(2048), take(2048),
                                                          take(1024), take(512), take(1024))
        a_QT, a_KT, a_S, a_PT, a_o = take(2048), take(1024), take(3072), take(3072), take(1024)
        assert at <= ARENA, at
        mem_hat = region(a_memh, TT, KD, P)
        mem_s = region(a_memT, TT, KD, P)
        dtmp, etmp = region(a_memT, NH, S), region(a_memT + 1024, NH, S)
        qs, ks, cum = region(a_qs, NH, S), region(a_ks, NH, S), region(a_B, NH, S)
        qmul = [region(a_qm + 1024 * i, NH, S) for i in range(2)]
        kmul = [region(a_km + 1024 * i, NH, S) for i in range(2)]
        hst, hst_off = region(a_st, TT, NH, P), region(a_sto, NH, P)
        restart = region(a_rm, 1024)
        QT, KT = region(a_QT, NH_A, S), region(a_KT, 4, S)
        sco, prT = region(a_S, NH_A, 384), region(a_PT, NH_A, 384)
        msc, mprT = region(a_S, NH, TT, MEM), region(a_PT, NH, 4, P)
        xs = region(a_S, TT, D)
        sq = region(a_PT, 2048)
        o_tmp = region(a_o, TT, G)

        names_2 = ["Q", "K", "V", "DZ", "RQ", "RK", "RV", "RG", "PU", "G0", "G1", "G2", "G3", "G4", "G5"]
        R2 = {g: 1024 * n for n, g in enumerate(names_2)}
        at = 15 * 1024
        b_x, b_c, b_e = take(3072), take(3072), take(3072)
        b_ml, b_kb, b_kt, b_wt, b_ss, b_vn, b_qd, b_eg = (take(1024), take(1024), take(512), take(512), take(512),
                                                          take(1024), take(512), take(512))
        b_rst, b_gr, b_gm, b_gf = take(1536), take(512), take(1024), take(1024)
        b_tmp, b_mx, b_gd, b_pw = take(1024), take(1024), take(128), take(512)
        assert at <= ARENA, at
        xT3, cT3, e3 = region(b_x, 12, S), region(b_c, 12, S), region(b_e, 12, S)
        kT, qT, kbT = (region(b_x + 1024 * i, TT, NH, P) for i in range(3))
        decT, mT, atT = (region(b_c + 1024 * i, TT, NH, P) for i in range(3))
        inv, invT, yl = (region(b_e + 1024 * i, TT, NH, P) for i in range(3))
        gbc = region(b_ml, 8, P)
        ml, kb = region(b_ml, TT, NH, P), region(b_kb, TT, NH, P)
        ktl, wT_, ss_ = region(b_kt, NH, P), region(b_wt, NH, P), region(b_ss, NH, P)
        vn, qd, eg = region(b_vn, TT, NH, P), region(b_qd, NH, P), region(b_eg, NH, P)
        rst, tmp, mx = region(b_rst, 3, NH, P), region(b_tmp, 1024), region(b_mx, 4, S)
        g_do, g_ro, g_mp, g_fp = region(b_gd, P), region(b_gr, G), region(b_gm, D), region(b_gf, D)
        pw = region(b_pw, 4, P)
        xs2 = region(b_e, TT, D)
        sq2 = region(b_e, 2048)
        sg = region(b_tmp, 2, 2, S)
        def part(name, at, *shape):
            assert at + int(np.prod(shape)) <= ARENA
            return nc.alloc_sbuf_tensor_at(name, [P, *shape], FR, offset=arena_byte + 4 * at)

        wt_rest = nc.alloc_sbuf_tensor_at("wt_rest", [P, SLOTS, UNIT_K, F32_COLS], FR, offset=wt_byte)
        wt_hi = [part(f"wt_hi{i}", [b_x + 2048, b_c + 1024, b_ml, b_kt][i], UNIT_K, F32_COLS) for i in range(SLOTS)]
        mix_hi = [part(f"mix_hi{i}", [b_rst, b_gm][i], UNIT_K, F32_COLS) for i in range(MIX_HI)]
        mix_hT_hi = part("mix_hT_hi", b_tmp, TT, KD, P)
        mix_hT_rest = nc.alloc_sbuf_tensor_at("mix_hT_rest", [P, TT, KD, P], FR, offset=hT_byte)
        hT_hi, hT_rest = part("hT_hi", R2["V"], TT, KD, P), part("hT_rest", R2["RQ"], TT, KD, P)
        hid_hi, hid_rest = part("hid_hi", R2["RV"], FF_G, 2, S), part("hid_rest", R2["RV"] + FF_G * 2 * S, FF_G, 2, S)
        assert R2["RV"] + 2 * FF_G * 2 * S <= b_x + 2048 and b_kt + 2048 <= b_qd
        mres = region(R2["Q"], TT, D)

        def reg(blk, g):
            return region((R1 if blk == "A" else R2)[g], TT, F32_COLS)

        def heads(v, n=NH):
            return v.rearrange("p t (h d) -> p (t h) d", h=n)

        gp = ctx.enter_context(nc.psum_tensor("gp", [P, 4, F32_COLS], F))
        mp = ctx.enter_context(nc.psum_tensor("mp", [P, 4, F32_COLS], F))

        loaded = {n: sem("loaded_" + n) for n in ("ident", "const", "rows", "x", "mem", "gain1", "early", "late", "ba")}
        w_loaded = [sem(f"w_loaded{i}") for i in range(SLOTS)]
        w_used = sem("w_used")
        group_read = [sem(f"group_read{i}") for i in range(2)]
        step_done = sem("step_done")
        step_read = [sem(f"step_read{i}") for i in range(4)]
        pow_asked, pow_given = sem("pow_asked"), sem("pow_given")
        v_chain, a_chain = sem("v_chain"), sem("a_chain")
        out_done = sem("out_done")
        w_rounded, w_split = sem("w_rounded"), sem("w_split")
        named = {}
        pow_widths = []

        def sig(name):
            if name not in named:
                named[name] = sem(name)
            return named[name]

        def computed(step):
            return step_done, STEP_NO[step] + 1

        def read_out(step):
            return step_read[STEP_NO[step] % 4], STEP_NO[step] // 4 + 1

        def bank(step, *dims):
            v = mp[:, STEP_NO[step] % 4]
            if len(dims) == 2:
                n = dims[0] * dims[1]
                return v[:, 0:n].rearrange("p (a b) -> p a b", a=dims[0])
            return v[:, 0:dims[0]] if dims else v

        def group_bank(group, t):
            return gp[:, 2 * (GROUP_NO[group] % 2) + t]

        def summed(group):
            return w_used, 1 + last_unit(group)

        def taken(group):
            return group_read[GROUP_NO[group] % 2], GROUP_NO[group] // 2 + 1

        def mixer_index(u):
            name = GROUPS[UNITS[u][0]][0]
            return u - first_unit(name[:3] + "Q") if name in SPLIT_MIX else None

        def rounded_part(u):
            i = mixer_index(u)
            return wt_hi[u % SLOTS] if i is None else mix_hi[i % MIX_HI]

        def group_banks(group):
            b = 2 * (GROUP_NO[group] % 2)
            return gp[:, b:b + 2, :]

        lbs = small[:, 460:472]

        def cT3s(j):
            return cT3[:, 4 * j:4 * j + 4, :]

        block = ctx.enter_context(nc.Block())

        def unit_loads(u):
            g, k0, nk = UNITS[u]
            name = GROUPS[g][0]
            l, n = int(name[1]), name[3:]

            def piece(src, c0, width=F32_COLS, to=0):
                return (wt[:, u % SLOTS, 0:nk, to:to + width],
                        src[l, k0 * P:(k0 + nk) * P, c0:c0 + width].rearrange("(k p) n -> p k n", p=P))
            if name[0] == "A":
                if n in ("KM", "VM"):
                    return [piece(w["w_mem_kv"], 0 if n == "KM" else G)]
                if n[0] == "O":
                    return [piece(w["w_out"], G * int(n[1]))]
                return [piece(w["w_in"], COL_1[n])]
            if n in COL_2:
                return [piece(w["w_in_2"], COL_2[n])]
            j = int(n[-1]) if n[0] != "F" else int(n[1:])
            if n[0] == "B":
                return [piece(w[{"P": "w_branch_pool_2", "R": "w_branch_ret_2", "D": "w_branch_dn_2"}[n[1]]], G * j)]
            if n[0] == "M":
                return [piece(w["w_out_2"], G * j)]
            if n[0] == "F":
                return [piece(w["ffn_gate_2"], 256 * j, 256), piece(w["ffn_up_2"], 256 * j, 256, 256)]
            return [piece(w["ffn_down_2"], G * j)]

        slot_total = [0] * SLOTS
        unit_value = []
        for u in range(len(UNITS)):
            slot_total[u % SLOTS] += 16 * len(unit_loads(u))
            unit_value.append(slot_total[u % SLOTS])

        @block.sync
        def _(sp):
            sp.dma_start(const[:, 0:P + ROT], w["shape_constants"][:, 0:P + ROT]).then_inc(loaded["ident"], 16)
            sp.dma_start(region(a_S, TT, D), w["mem"][0].rearrange("(t p) d -> p t d", p=P)).then_inc(loaded["mem"], 16)
            sp.wait_ge(loaded["rows"], 16 * 7)
            sp.dma_start(x[:, :, :], w["x"][0].rearrange("(t p) d -> p t d", p=P)).then_inc(loaded["x"], 16)
            for u in range(len(UNITS)):
                if u == SLOTS:
                    sp.dma_start(const[:, P + ROT:], w["shape_constants"][:, P + ROT:]).then_inc(loaded["const"], 16)
                if u >= SLOTS:
                    sp.wait_ge(w_used, u - SLOTS + 1)
                for dst, src in unit_loads(u):
                    sp.dma_start(dst, src).then_inc(w_loaded[u % SLOTS], 16)
            sp.wait_ge(sig("x_tile"), 2 * (3 * DEPTH))
            sp.dma_start(out[0].rearrange("(t p) d -> p t d", p=P), x[:, :, :]).then_inc(out_done, 16)
            sp.wait_ge(out_done, 16)

        @block.tensor
        def _(pe):
            state = {"unit": 0, "step": 0}

            def begin(step, *waits):
                n = STEP_NO[step]
                assert n == state["step"], (step, STEPS[state["step"]])
                state["step"] += 1
                if n >= 4:
                    pe.wait_ge(step_read[n % 4], n // 4)
                for wait in waits:
                    pe.wait_ge(*wait)

            def end(ins):
                ins.then_inc(step_done, 1)

            def transposes(step, tiles, *waits):
                begin(step, *waits)
                for j, tile in enumerate(tiles):
                    last = nc.tensor.transpose(bank(step)[:, P * j:P * j + P], tile, ident)
                end(last)

            def units(group, stationary, count, *waits):
                for _ in range(count):
                    u = state["unit"]
                    g, k0, nk = UNITS[u]
                    assert GROUPS[g][0] == group, (group, GROUPS[g][0])
                    state["unit"] += 1
                    if k0 == 0:
                        if g >= 2:
                            pe.wait_ge(group_read[g % 2], g // 2)
                        for wait in waits:
                            pe.wait_ge(*wait)
                    pe.wait_ge(w_loaded[u % SLOTS], unit_value[u])
                    if group in BY_COLUMN:
                        for k in range(nk):
                            for c in range(4):
                                last = nc.tensor.matmul(group_bank(group, c // 2)[:, S * (c % 2):S * (c % 2) + S],
                                                        wt[:, u % SLOTS, k, P * c:P * c + P], hT[:, :, k0 + k, :],
                                                        start=(k0 + k == 0 and c % 2 == 0), stop=(k0 + k == KD - 1),
                                                        skip_group_check=True)
                    else:
                        for t in range(TT):
                            for k in range(nk):
                                last = nc.tensor.matmul(group_bank(group, t), stationary(k0 + k, t), wt[:, u % SLOTS, k, :],
                                                        start=(k0 + k == 0), stop=(k0 + k == GROUPS[g][1] - 1))
                    last.then_inc(w_used, 1)

            def split_part(n, t_range, rows=None):
                u, k1, nk = PARTS[n]
                g, k0, _ = UNITS[u]
                group = GROUPS[g][0]
                hi, rest = rounded_part(u), wt_rest[:, u % SLOTS]
                h_hi, h_rest = (hT_hi, hT_rest) if mixer_index(u) is None else (mix_hT_hi, mix_hT_rest)
                pe.wait_ge(w_split, n + 1)
                if group in BY_COLUMN:
                    for k in range(k1, k1 + nk):
                        for c in range(4):
                            o = group_bank(group, c // 2)[:, S * (c % 2):S * (c % 2) + S]
                            for i, (a, b) in enumerate(((hi, h_hi), (hi, h_rest), (rest, h_hi))):
                                last = nc.tensor.matmul(o, a[:, k, P * c:P * c + P], b[:, :, k0 + k, :],
                                                        start=(k0 + k == 0 and c % 2 == 0 and i == 0),
                                                        stop=(k0 + k == KD - 1 and i == 2), skip_group_check=True)
                else:
                    for t in t_range:
                        for k in range(k1, k1 + nk):
                            kk = k0 + k
                            if mixer_index(u) is None:
                                s_hi, s_rest = (z[:, kk // 2, kk % 2, P * t:P * t + P] for z in (hid_hi, hid_rest))
                            else:
                                s_hi, s_rest = h_hi[:, t, kk, :], h_rest[:, t, kk, :]
                            for i, (a, b) in enumerate(((s_hi, hi), (s_hi, rest), (s_rest, hi))):
                                last = nc.tensor.matmul(group_bank(group, t), a, b[:, k, :],
                                                        start=(kk == 0 and i == 0), stop=(kk == GROUPS[g][1] - 1 and i == 2))
                return last

            def split_units(group, count):
                for _ in range(count):
                    u = state["unit"]
                    g, k0, _ = UNITS[u]
                    assert GROUPS[g][0] == group
                    state["unit"] += 1
                    if k0 == 0:
                        pe.wait_ge(group_read[g % 2], g // 2)
                    for n in range(parts_until(u - 1), parts_until(u)):
                        last = split_part(n, range(TT))
                    last.then_inc(w_used, 1)

            def split_tail(count):
                first = state["unit"]
                state["unit"] += count
                for t in range(TT):
                    for u in range(first, first + count):
                        for n in range(parts_until(u - 1), parts_until(u)):
                            last = split_part(n, (t,))
                        if t == TT - 1:
                            last.then_inc(w_used, 1)
                    if t == 0:
                        last.then_inc(sig("first_tile"), 1)

            def tail(count, stationary):
                first = state["unit"]
                state["unit"] += count
                for t in range(TT):
                    for u in range(first, first + count):
                        g, k0, nk = UNITS[u]
                        if t == 0:
                            if k0 == 0 and g >= 2:
                                pe.wait_ge(group_read[g % 2], g // 2)
                            pe.wait_ge(w_loaded[u % SLOTS], unit_value[u])
                        for k in range(nk):
                            last = nc.tensor.matmul(group_bank(GROUPS[g][0], t), stationary(k0 + k, t), wt[:, u % SLOTS, k, :],
                                                    start=(k0 + k == 0), stop=(k0 + k == GROUPS[g][1] - 1))
                        if t == TT - 1:
                            last.then_inc(w_used, 1)
                    if t == 0:
                        last.then_inc(sig("first_tile"), 1)

            def x_transposes(names, src, n):
                for i in range(4):
                    t, q = divmod(i, 2)
                    transposes(names(i), [src[:, t, (4 * q + j) * P:(4 * q + j + 1) * P] for j in range(4)],
                               (sig("x_normed"), 2 * n + t + 1))
                for i in range(4):
                    pe.wait_ge(*read_out(names(i)))

            def from_hT(k, t):
                return hT[:, t, k, :]

            pe.wait_ge(loaded["ident"], 16)
            for i in range(4):
                t, q = divmod(i, 2)
                transposes(f"memT{i}", [region(a_S, TT, D)[:, t, (4 * q + j) * P:(4 * q + j + 1) * P] for j in range(4)],
                           (sig("mem_normed"), 1))
            pe.wait_ge(loaded["rows"], 16 * 7)
            begin("colA")
            end(nc.tensor.transpose(bank("colA")[:, 0:COL_A_ROWS], small[0:COL_A_ROWS, 0:P], ident[0:COL_A_ROWS, 0:COL_A_ROWS]))
            begin("colB")
            end(nc.tensor.transpose(bank("colB")[:, 0:COL_B_ROWS], small[0:COL_B_ROWS, P:2 * P], ident[0:COL_B_ROWS, 0:COL_B_ROWS]))

            for l in range(DEPTH):
                s = lambda n: f"A{l}.{n}"
                pe.wait_ge(sig("mem_scaled"), l + 1)
                for g in ("KM", "VM"):
                    units(s(g), lambda k, t: mem_s[:, t, k, :], 2)
                x_transposes(lambda i: s(f"xT{i}"), xs, l)
                units(s("QH"), None, 2)
                for t in range(TT):
                    transposes(s(f"kmT{t}"), [reg("A", "KM")[:, t, P * j:P * j + P] for j in range(4)], (sig("km_normed"), l + 1))
                units(s("FH"), None, 2)
                units(s("IH"), from_hT, 2)
                units(s("QA"), from_hT, 2)

                def hg_level(n):
                    src_q, src_k = (qs, ks) if n == 0 else (qmul[n % 2], kmul[n % 2])
                    for t in (range(TT) if n < 8 else (1,)):
                        begin(s(f"hg{n}_{t}"), (sig("hg_factors"), 9 * l + n + 1))
                        kt = t if n < 8 else 0
                        for h in range(NH):
                            last = nc.tensor.matmul(bank(s(f"hg{n}_{t}"))[:, P * h:P * h + P], src_k[:, h, kt * P:kt * P + P],
                                                    src_q[:, h, t * P:t * P + P], start=True, stop=True)
                        end(last)
                hg_level(0)
                units(s("KA"), from_hT, 1)
                hg_level(1)
                units(s("KA"), from_hT, 1)
                hg_level(2)
                units(s("VA"), from_hT, 1)
                hg_level(3)
                units(s("VA"), from_hT, 1)
                units(s("QM"), from_hT, 1)
                hg_level(4)
                units(s("QM"), from_hT, 1)
                for src, n in (("QA", "qaT"), ("KA", "kaT")):
                    for t in range(TT):
                        transposes(s(f"{n}{t}"), [reg("A", src)[:, t, P * j:P * j + P] for j in range(4)], (sig("qk_rotated"), l + 1))
                hg_level(5)

                def scores(h):
                    begin(s(f"sc{h}"), read_out(s("kaT0")), read_out(s("kaT1")), read_out(s("qaT0")), read_out(s("qaT1")))
                    b = bank(s(f"sc{h}"))
                    nc.tensor.matmul(b[:, 0:P], QT[:, h, 0:P], KT[:, h // 2, 0:P], start=True, stop=True)
                    end(nc.tensor.matmul(b[:, P:3 * P], QT[:, h, P:S], KT[:, h // 2, :], start=True, stop=True))
                for h in range(4):
                    scores(h)
                units(s("Z0"), from_hT, 1)
                hg_level(6)
                for h in range(4, 8):
                    scores(h)
                units(s("Z0"), from_hT, 1)
                hg_level(7)
                hg_level(8)
                for h in range(8):
                    transposes(s(f"pt{h}"), [sco[:, h, P * j:P * j + P] for j in range(3)],
                               (sig("attn_probs"), 2 * NH_A * l + 2 * h + 2))
                for t in range(TT):
                    begin(s(f"oa{t}"), *[read_out(s(f"pt{h}")) for h in range(4, 8)])
                    pe.wait_ge(group_read[GROUP_NO[s("VA")] % 2], GROUP_NO[s("VA")] // 2 + 1)
                    for h in range(8):
                        for st in range(t + 1):
                            last = nc.tensor.matmul(bank(s(f"oa{t}"))[:, DH_A * h:DH_A * (h + 1)],
                                                    prT[:, h, (t + st) * P:(t + st + 1) * P],
                                                    reg("A", "VA")[:, st, DH_A * h:DH_A * (h + 1)], start=(st == 0), stop=(st == t))
                    end(last)
                units(s("Z1"), from_hT, 1)
                for t in range(TT):
                    transposes(s(f"qmT{t}"), [reg("A", "QM")[:, t, P * j:P * j + P] for j in range(4)], (sig("qm_normed"), l + 1))
                km3 = reg("A", "KM").rearrange("p t (h m) -> p t h m", h=NH)
                for h in range(NH):
                    begin(s(f"ms{h}"), read_out(s("kmT0")), read_out(s("kmT1")), read_out(s("qmT0")), read_out(s("qmT1")))
                    for t in range(TT):
                        last = nc.tensor.matmul(bank(s(f"ms{h}"), TT, MEM)[:, t, :].rearrange("p (a b) -> p a b", a=TT),
                                                reg("A", "QM")[:, t, P * h:P * h + P], km3[:, :, h, :], start=True, stop=True)
                    end(last)
                units(s("Z1"), from_hT, 1)
                for t in range(TT):
                    begin(s(f"hgo{t}"), read_out(s("hg7_0")), read_out(s("hg7_1")), read_out(s("hg8_1")))
                    pe.wait_ge(group_read[GROUP_NO[s("IH")] % 2], GROUP_NO[s("IH")] // 2 + 1)
                    for h in range(NH):
                        o = bank(s(f"hgo{t}"))[:, P * h:P * h + P]
                        if t == 1:
                            nc.tensor.matmul(o, hst_off[:, h, :], reg("A", "IH")[:, 0, P * h:P * h + P], start=True, stop=False)
                        last = nc.tensor.matmul(o, hst[:, t, h, :], reg("A", "IH")[:, t, P * h:P * h + P], start=(t == 0), stop=True)
                    end(last)
                units(s("Z2"), from_hT, 1)
                for h in range(NH):
                    transposes(s(f"mpt{h}"), [msc[:, h, t, P * j:P * j + P] for t in range(TT) for j in range(2)], read_out(s(f"ms{h}")))
                units(s("Z2"), from_hT, 1)
                for t in range(TT):
                    begin(s(f"om{t}"), *[read_out(s(f"mpt{h}")) for h in range(4)])
                    pe.wait_ge(group_read[GROUP_NO[s("VM")] % 2], GROUP_NO[s("VM")] // 2 + 1)
                    for h in range(NH):
                        for st in range(TT):
                            last = nc.tensor.matmul(bank(s(f"om{t}"))[:, P * h:P * h + P], mprT[:, h, 2 * t + st, :],
                                                    reg("A", "VM")[:, st, P * h:P * h + P], start=(st == 0), stop=(st == 1))
                    end(last)
                for i in range(6):
                    j, t = divmod(i, 2)
                    transposes(s(f"yT{i}"), [reg("A", f"Z{j}")[:, t, P * q:P * q + P] for q in range(4)], (sig("y_ready"), 3 * l + j + 1))
                for i in range(2, 6):
                    pe.wait_ge(*read_out(s(f"yT{i}")))
                from_y = lambda k, t: reg("A", f"Z{k // 4}")[:, t, P * (k % 4):P * (k % 4) + P]
                units(s("O0"), from_y, 3)
                tail(3, from_y)

            for l in range(DEPTH):
                s = lambda n: f"B{l}.{n}"

                def group_in(g):
                    n = GROUP_NO[s(g)]
                    return group_read[n % 2], n // 2 + 1
                x_transposes(lambda i: s(f"xT{i}"), xs2, DEPTH + 2 * l)
                pe.wait_ge(sig("h_split"), 2 * TT * l + TT)
                for g in "QKV":
                    split_units(s(g), 2)
                split_units(s("RQ"), 1)
                begin(s("ba"), (loaded["ba"], 16 * DEPTH))
                for t in range(TT):
                    for k in range(KD):
                        for i, h_part in enumerate((mix_hT_hi, mix_hT_rest)):
                            last = nc.tensor.matmul(bank(s("ba"))[:, 8 * t:8 * t + 8], h_part[:, t, k, :].bitcast(F), w_ba[:, l, k, :],
                                                    start=(k == 0 and i == 0), stop=(k == KD - 1 and i == 1))
                end(last)
                split_units(s("RQ"), 1)
                begin(s("cg"), (sig("gates_ready"), l + 1))
                gcol = small[:, 0:8]
                nc.tensor.matmul(bank(s("cg"))[:, 0:8], upper, gcol, start=True, stop=True)
                end(nc.tensor.matmul(bank(s("cg"))[:, 8:16], ones, gcol, start=True, stop=True))
                for t in range(TT):
                    begin(s(f"gb{t}"), (sig("gates_ready"), l + 1))
                    for h in range(NH):
                        last = nc.tensor.matmul(bank(s(f"gb{t}"))[:, P * h:P * h + P], gbc[:, NH * t + h, :], upper, start=True, stop=True)
                    end(last)
                split_units(s("RK"), 2)
                split_units(s("RV"), 2)
                for j in range(3):
                    for t in range(TT):
                        transposes(s(f"bT{j}{t}"), [cT3[:, 4 * j + q, t * P:t * P + P] for q in range(4)], (sig("conv_done"), l + 1))
                split_units(s("PU"), 2)
                for n, v in (("kT", reg("B", "K")), ("qT", reg("B", "Q")), ("kbT", kb.rearrange("p t h d -> p t (h d)"))):
                    for t in range(TT):
                        transposes(s(f"{n}{t}"), [v[:, t, P * q:P * q + P] for q in range(4)], (sig("dn_normed"), l + 1))
                for n, v in (("mm", kbT), ("at", qT)):
                    for t in range(TT):
                        begin(s(f"{n}{t}"), *[read_out(s(f"{m}{t}")) for m in ("kT", "qT", "kbT")])
                        for h in range(NH):
                            last = nc.tensor.matmul(bank(s(f"{n}{t}"))[:, P * h:P * h + P], kT[:, t, h, :], v[:, t, h, :], start=True, stop=True)
                        end(last)

                def quad(step, lhs, rhs, *waits):
                    begin(step, *waits)
                    for h in range(NH):
                        last = nc.tensor.matmul(bank(step)[:, P * h:P * h + P], lhs(h), rhs(h), start=True, stop=True)
                    end(last)
                fill = [(g, 1) for g in ("RG", "RG", "DZ", "DZ", "G2", "G2", "G3", "G3", "G4", "G4", "G5", "G5", "G0", "G0", "G1", "G1")]

                def filler():
                    if fill:
                        g, c = fill.pop(0)
                        split_units(s(g), c)
                for n in range(len(LEVELS)):
                    for t in range(TT):
                        quad(s(f"Y{n}_{t}"), lambda h: ml[:, t, h, :], lambda h: inv[:, t, h, :], (sig("inv_ready"), len(LEVELS) * l + n + 1))
                    filler()
                    if n < len(LEVELS) - 1:
                        for t in range(TT):
                            quad(s(f"Z{n}_{t}"), lambda h: invT[:, t, h, :], lambda h: yl[:, t, h, :], read_out(s(f"Y{n}_{t}")))
                    for t in range(TT):
                        quad(s(f"W{n}_{t}"), lambda h: yl[:, t, h, :], lambda h: invT[:, t, h, :], read_out(s(f"Y{n}_{t}")))
                    filler()
                last = len(LEVELS) - 1
                inv_done = [read_out(s(f"W{last}_{t}")) for t in range(TT)]
                vb = reg("B", "V").rearrange("p t (h d) -> p t h d", h=NH)
                quad(s("u0"), lambda h: invT[:, 0, h, :], lambda h: vb[:, 0, h, :], *inv_done)
                quad(s("wT"), lambda h: kb[:, 1, h, :], lambda h: invT[:, 1, h, :], *inv_done)
                filler()
                quad(s("st"), lambda h: ktl[:, h, :], lambda h: vn[:, 0, h, :], read_out(s("u0")))
                begin(s("vn1"), read_out(s("wT")), read_out(s("st")))
                for h in range(NH):
                    nc.tensor.matmul(bank(s("vn1"))[:, P * h:P * h + P], invT[:, 1, h, :], vb[:, 1, h, :], start=True, stop=False)
                    last = nc.tensor.matmul(bank(s("vn1"))[:, P * h:P * h + P], wT_[:, h, :], ss_[:, h, :], start=False, stop=True)
                end(last)
                filler()
                quad(s("do0"), lambda h: atT[:, 0, h, :], lambda h: vn[:, 0, h, :])
                begin(s("do1"), read_out(s("vn1")))
                for h in range(NH):
                    nc.tensor.matmul(bank(s("do1"))[:, P * h:P * h + P], qd[:, h, :], ss_[:, h, :], start=True, stop=False)
                    last = nc.tensor.matmul(bank(s("do1"))[:, P * h:P * h + P], atT[:, 1, h, :], vn[:, 1, h, :], start=False, stop=True)
                end(last)
                for n, g in (("rqT", "RQ"), ("rkT", "RK")):
                    for t in range(TT):
                        transposes(s(f"{n}{t}"), [reg("B", g)[:, t, P * q:P * q + P] for q in range(4)], (sig("ret_rotated"), l + 1))
                assert not fill
                for i, (jt, it) in enumerate(((0, 0), (0, 1), (1, 1))):
                    quad(s(f"rs{i}"), lambda h: reg("B", "RK")[:, jt, P * h:P * h + P], lambda h: reg("B", "RQ")[:, it, P * h:P * h + P],
                         *[read_out(s(f"{n}{t}")) for n in ("rqT", "rkT") for t in range(TT)])
                for t in range(TT):
                    begin(s(f"ro{t}"), *[read_out(s(f"rs{i}")) for i in range(3)])
                    for h in range(NH):
                        o = bank(s(f"ro{t}"))[:, P * h:P * h + P]
                        if t == 1:
                            nc.tensor.matmul(o, rst[:, 1, h, :], reg("B", "RV")[:, 0, P * h:P * h + P], start=True, stop=False)
                        last = nc.tensor.matmul(o, rst[:, 2 * t, h, :], reg("B", "RV")[:, t, P * h:P * h + P], start=(t == 0), stop=True)
                    end(last)
                pu = reg("B", "PU")
                for i in range(2):
                    begin(s(f"pm{i}"))
                    for q in range(2):
                        g = 2 * i + q
                        o = bank(s(f"pm{i}"), 2, S)[:, q, :]
                        nc.tensor.matmul(o[:, 0:P], pu[:, 0, P * g:P * g + P], band[:, g, 0, :], start=True, stop=True)
                        nc.tensor.matmul(o[:, P:S], pu[:, 0, P * g:P * g + P], band[:, g, 1, :], start=True, stop=False)
                        last = nc.tensor.matmul(o[:, P:S], pu[:, 1, P * g:P * g + P], band[:, g, 2, :], start=False, stop=True)
                    end(last)
                for i in range(2):
                    begin(s(f"py{i}"), read_out(s(f"pm{i}")), (loaded["early"], 16 * 2 * (l + 1)))
                    for q in range(2):
                        last = nc.tensor.matmul(bank(s(f"py{i}"), 2, S)[:, q, :], pw[:, 2 * i + q, :], mx[:, 2 * i + q, :], start=True, stop=True)
                    end(last)
                for i in range(2):
                    pe.wait_ge(*read_out(s(f"py{i}")))
                po = reg("B", "PU").rearrange("p t (c i) -> p (t c i)", c=4).rearrange("p (k s) -> p k s", k=4)
                for j in range(2):
                    units(s(f"BP{j}"), lambda k, t: po[:, k, t * P:t * P + P], 1)
                for t in range(TT):
                    transposes(s(f"oT_r{t}"), [reg("B", "RQ")[:, t, P * q:P * q + P] for q in range(4)], (sig("ret_out"), l + 1))
                for t in range(TT):
                    pe.wait_ge(*read_out(s(f"oT_r{t}")))
                for j in range(2):
                    units(s(f"BR{j}"), lambda k, t: reg("B", "RQ")[:, t, P * k:P * k + P], 1)
                for t in range(TT):
                    transposes(s(f"oT_d{t}"), [reg("B", "Q")[:, t, P * q:P * q + P] for q in range(4)], (sig("dn_out"), l + 1))
                for t in range(TT):
                    pe.wait_ge(*read_out(s(f"oT_d{t}")))
                for j in range(2):
                    units(s(f"BD{j}"), lambda k, t: reg("B", "Q")[:, t, P * k:P * k + P], 1)
                for i in range(4):
                    j, t = divmod(i, 2)
                    transposes(s(f"yT{i}"), [reg("B", f"G{2 + j}")[:, t, P * q:P * q + P] for q in range(4)], (sig("mix_sum"), 2 * l + j + 1))
                for i in range(4):
                    pe.wait_ge(*read_out(s(f"yT{i}")))
                tail(4, lambda k, t: reg("B", f"G{2 + k // 4}")[:, t, P * (k % 4):P * (k % 4) + P])
                x_transposes(lambda i: s(f"fT{i}"), xs2, DEPTH + 2 * l + 1)
                pe.wait_ge(sig("h_split"), 2 * TT * (l + 1))
                for j in range(FF_G):
                    split_units(s(f"F{j}"), 2)
                for c in range(-(-KF // UNIT_K)):
                    pe.wait_ge(sig("hid_split"), FF_G * l + min(2 * (c + 1), FF_G))
                    split_units(s("E0"), 1)
                split_units(s("E1"), -(-KF // UNIT_K) - SLOTS)
                split_tail(SLOTS)
            assert state["unit"] == len(UNITS) and state["step"] == len(STEPS)

        @block.scalar
        def _(act):
            chain = [0]

            def a(ins):
                chain[0] += 1
                ins.then_inc(a_chain, 1)
                act.wait_ge(a_chain, chain[0])

            def move(name, func=ACT.Copy, dst=None):
                act.wait_ge(*summed(name))
                dst = reg(name[0], name[3:]) if dst is None else dst
                nc.scalar.activation(dst, group_banks(name), func).then_inc(group_read[GROUP_NO[name] % 2], 1)

            rounded = [0]

            def round_weights(count):
                while rounded[0] < count:
                    u, k, nk = PARTS[rounded[0]]
                    act.wait_ge(w_loaded[u % SLOTS], unit_value[u])
                    if (mixer_index(u) or 0) >= MIX_HI and k == 0:
                        act.wait_ge(w_used, u - MIX_HI + 1)
                    nc.scalar.activation(rounded_part(u)[:, k:k + nk, :], wt[:, u % SLOTS, k:k + nk, :], ACT.Copy)\
                        .then_inc(w_rounded, 1)
                    rounded[0] += 1

            def x_square(n, t, junk):
                if n > 0:
                    act.wait_ge(sig("x_tile"), 2 * (n - 1) + t + 1)
                nc.scalar.activation(junk, x[:, t, :], ACT.Square, accum_out=small[:, 360 + t:361 + t]).then_inc(sig("x_sq"), 1)

            for name, src in (("norm_g", "norm_g"), ("mem_norm_g", "mem_norm_g"), ("mix_pre", "mix_pre_norm_2"),
                              ("ffn_pre", "ffn_pre_norm_2"), ("lb", "hgrn_lb_logits"), ("pool_scale", "pool_scale_2")):
                r0, k = COL_A[name]
                act.dma_start(small[r0:r0 + DEPTH * k, 0:P], w[src].rearrange("l (k p) -> (l k) p", p=P)).then_inc(loaded["rows"], 16)
            act.dma_start(small[0:COL_B_ROWS, P:2 * P], w["dn_conv_2"].rearrange("l w (k p) -> (l w k) p", p=P)).then_inc(loaded["rows"], 16)
            act.wait_ge(loaded["mem"], 16)
            for t in range(TT):
                ins = nc.scalar.activation(region(a_PT, TT, D)[:, t], region(a_S, TT, D)[:, t], ACT.Square, accum_out=small[:, 360 + t:361 + t])
            ins.then_inc(sig("mem_squared"), 1)
            act.dma_start(pos[:, :], w["positions"][0].rearrange("(t p) -> p t", p=P), allow_slow_non_contiguous=True).then_inc(loaded["gain1"], 16)
            for l in range(DEPTH):
                for dst, src in ((g_qk[:, l, 0], "moba_q_norm"), (g_qk[:, l, 1], "moba_k_norm"), (g_mq[:, l], "mem_q_norm"),
                                 (g_mk[:, l], "mem_k_norm"), (g_ho[:, l], "hgrn_o_norm"), (a_log[:, l], "dn_A_log_2"),
                                 (dt_bias[:, l], "dn_dt_bias_2")):
                    act.dma_start(dst, w[src][l:l + 1].to_broadcast([P, dst.shape[1]])).then_inc(loaded["gain1"], 16)
                act.dma_start(w_ba[:, l], w["w_in_2"][l, :, BA_COL:BA_COL + 8].rearrange("(k p) n -> p k n", p=P)).then_inc(loaded["ba"], 16)

            for l in range(DEPTH):
                s = lambda n: f"A{l}.{n}"
                if l == 0:
                    act.wait_ge(loaded["x"], 16)
                    act.wait_ge(sig("mem_normed"), 1)
                for t in range(TT):
                    x_square(l, t, sq[:, t * D:(t + 1) * D])
                for g in ("KM", "VM"):
                    move(s(g))
                if l == 0:
                    act.wait_ge(sig("angles"), 1)
                    a(nc.scalar.activation(rot[:, 1, 0:2, :], small[:, 320:336].rearrange("p (t j) -> p t j", t=2), ACT.Sin))
                    nc.scalar.activation(rot[:, 0, 0:2, :], small[:, 336:352].rearrange("p (t j) -> p t j", t=2), ACT.Sin).then_inc(sig("rot_ready"), 1)
                act.wait_ge(*summed(s("QH")))
                nc.scalar.activation(etmp.rearrange("p (b c) s -> p b (c s)", b=2), group_banks(s("QH")), ACT.Sigmoid).then_inc(sig("hg_q_sig"), 1)
                act.wait_ge(*summed(s("FH")))
                nc.scalar.activation(ks.rearrange("p (b c) s -> p b (c s)", b=2), group_banks(s("FH")), ACT.Sigmoid, scale=-1.0)
                move(s("FH"), dst=cum.rearrange("p (b c) s -> p b (c s)", b=2))
                act.wait_ge(sig("hg_f_in"), l + 1)
                a(nc.scalar.activation(dtmp, dtmp, ACT.Exp, scale=-1.0))
                nc.scalar.activation(dtmp, dtmp, ACT.Ln, bias=1.0).then_inc(sig("hg_ln"), 1)
                move(s("IH"))
                if l > 0:
                    act.wait_ge(sig("hg_lb_in"), l)
                    a(nc.scalar.activation(dtmp, dtmp, ACT.Exp, scale=-1.0))
                    nc.scalar.activation(dtmp, dtmp, ACT.Ln, bias=1.0).then_inc(sig("hg_lb_ln"), 1)
                after_level = {1: ["QA"], 2: ["KA"], 4: ["VA"], 6: ["QM"]}
                for n in range(1, 9):
                    act.wait_ge(sig("hg_diff"), 8 * l + n)
                    m = 2 ** (n - 1)
                    if n < 8:
                        dv = dtmp.rearrange("p h (b m) -> p (h b) m", m=2 * m)
                        ev = etmp.rearrange("p h (b m) -> p (h b) m", m=2 * m)
                        left, right = (dv[:, :, 0:m], ev[:, :, 0:m]), (dv[:, :, m:], ev[:, :, m:])
                    else:
                        left, right = (dtmp[:, :, 0:P], etmp[:, :, 0:P]), (dtmp[:, :, P:S], etmp[:, :, P:S])
                    nc.scalar.activation(left[1], left[0], ACT.Exp, scale=-1.0)
                    nc.scalar.activation(right[1], right[0], ACT.Exp).then_inc(sig("hg_exp"), 1)
                    for g in after_level.get(n, []):
                        move(s(g))
                    if n in (6, 8):
                        for h in range(4 * (n // 8), 4 * (n // 8) + 4):
                            act.wait_ge(sig("attn_max"), 2 * l + n // 8 + 1)
                            for t in range(TT):
                                sc = sco[:, h, 0:P] if t == 0 else sco[:, h, P:3 * P]
                                nc.scalar.activation(sc, sc, ACT.Exp, bias=small[:, 368 + 8 * t + h:369 + 8 * t + h],
                                                     accum_out=small[:, 384 + 8 * t + h:385 + 8 * t + h]).then_inc(sig("attn_probs"), 1)
                for j in range(3):
                    move(s(f"Z{j}"))
                    act.wait_ge(*taken(s(f"Z{j}")))
                    act.wait_ge(*((sig("hg_factors"), 9 * (l + 1)) if j == 0 else (sig("y_ready"), 3 * l + j)))
                    nc.scalar.activation(region(a_memT, TT, G), reg("A", f"Z{j}"), ACT.Sigmoid).then_inc(sig("z_sig"), 1)
                    if j == 0:
                        for h in range(NH):
                            act.wait_ge(sig("mem_max"), NH * l + h + 1)
                            for t in range(TT):
                                ins = nc.scalar.activation(msc[:, h, t, :], bank(s(f"ms{h}"), TT, MEM)[:, t, :], ACT.Exp, scale=P ** -0.5,
                                                           bias=small[:, 400 + 4 * t + h:401 + 4 * t + h],
                                                           accum_out=small[:, 408 + 4 * t + h:409 + 4 * t + h])
                            ins.then_inc(step_read[STEP_NO[s(f"ms{h}")] % 4], 1)
                if l == 0:
                    act.wait_ge(sig("lb_in"), 1)
                    a(nc.scalar.activation(small[:, 496:504], small[:, 488:496], ACT.Exp, scale=-1.0))
                    nc.scalar.activation(small[:, 496:504], small[:, 496:504], ACT.Ln, bias=1.0).then_inc(sig("lb_ln"), 1)
                    nc.scalar.activation(lbs[:, 8:12], small[:, 484:488], ACT.Sigmoid).then_inc(sig("lb_sig"), 1)

            for l in range(DEPTH):
                s = lambda n: f"B{l}.{n}"

                def result(names, n, parts=0):
                    for t in range(TT):
                        act.wait_ge(*((sig("first_tile"), DEPTH + 2 * l + (n - DEPTH) % 2 + 1) if t == 0 else summed(names[1])))
                        for j in range(2):
                            ins = nc.scalar.activation(xs2[:, t, G * j:G * j + G], group_bank(names[j], t), ACT.Square,
                                                       accum_out=small[:, 364 + 2 * j + t:365 + 2 * j + t])
                        ins.then_inc(sig("res_sq"), 1)
                        if n + 1 < 3 * DEPTH:
                            x_square(n + 1, t, xs2[:, t, :])
                        if t == 0:
                            round_weights(parts)
                if l == 0:
                    for t in range(TT):
                        x_square(DEPTH, t, xs2[:, t, :])

                def round_until(i):
                    round_weights(parts_until(first_unit(s("Q")) + i))
                round_until(1)
                act.dma_start(g_do, w["dn_out_norm_2"][l:l + 1].to_broadcast([P, P])).then_inc(loaded["early"], 16)
                act.dma_start(pw, w["pool_w_2"][l].rearrange("g c d -> c g d")).then_inc(loaded["early"], 16)
                for j, g in enumerate("QKV"):
                    round_until(2 * j + 2)
                    move(s(g), dst=xT3[:, 4 * j:4 * j + 4, :].rearrange("p (b c) s -> p b (c s)", b=2))
                round_until(7)
                act.wait_ge(sig("ba_in"), l + 1)
                nc.scalar.activation(small[:, 16:24], small[:, 24:32], ACT.Sigmoid).then_inc(sig("beta_ready"), 1)
                a(nc.scalar.activation(small[:, 40:48], small[:, 32:40], ACT.Exp, scale=-1.0))
                a(nc.scalar.activation(small[:, 48:52], a_log[:, l], ACT.Exp))
                nc.scalar.activation(small[:, 40:48], small[:, 40:48], ACT.Ln, bias=1.0).then_inc(sig("gate_parts"), 1)
                round_until(8)
                move(s("RQ"))
                round_until(9)
                for j in range(3):
                    act.wait_ge(sig("conv_in"), 3 * l + j + 1)
                    nc.scalar.activation(e3[:, 4 * j:4 * j + 4, :], cT3s(j), ACT.Sigmoid).then_inc(sig("conv_sig"), 1)
                    if j < 2:
                        round_until(10 + j)
                move(s("RK"))
                round_until(12)
                act.wait_ge(sig("decay_in"), l + 1)
                nc.scalar.activation(yl, yl, ACT.Exp).then_inc(sig("decay_exp"), 1)
                nc.scalar.activation(small[:, 80:96], small[:, 56:72], ACT.Exp)
                nc.scalar.activation(eg, bank(s("gb1"), NH, P), ACT.Exp).then_inc(step_read[STEP_NO[s("gb1")] % 4], 1)
                round_until(13)
                move(s("RV"))
                round_until(14)
                move(s("PU"))
                order = ["PU", "RG", "DZ", "G2", "G3", "G4", "G5", "G0", "G1"]
                filled, moved = 2, 1
                for n in range(len(LEVELS)):
                    round_until(15 + 2 * n)
                    for t in range(TT):
                        act.wait_ge(*computed(s(f"Y{n}_{t}")))
                        nc.scalar.activation(yl[:, t], bank(s(f"Y{n}_{t}"), NH, P), ACT.Copy).then_inc(step_read[STEP_NO[s(f"Y{n}_{t}")] % 4], 1)
                    filled += 2
                    round_until(16 + 2 * n)
                    while moved < filled // 2:
                        g = order[moved]
                        move(s(g), ACT.Sigmoid if g[0] == "G" else ACT.Copy)
                        moved += 1
                round_until(29)
                act.wait_ge(*computed(s("u0")))
                nc.scalar.activation(vn[:, 0], bank(s("u0"), NH, P), ACT.Copy).then_inc(step_read[STEP_NO[s("u0")] % 4], 1)
                act.wait_ge(*computed(s("wT")))
                nc.scalar.activation(wT_, bank(s("wT"), NH, P), ACT.Copy, scale=-1.0).then_inc(step_read[STEP_NO[s("wT")] % 4], 1)
                act.wait_ge(*computed(s("st")))
                nc.scalar.activation(ss_, bank(s("st"), NH, P), ACT.Copy).then_inc(step_read[STEP_NO[s("st")] % 4], 1)
                act.wait_ge(*computed(s("vn1")))
                nc.scalar.activation(vn[:, 1], bank(s("vn1"), NH, P), ACT.Copy).then_inc(step_read[STEP_NO[s("vn1")] % 4], 1)
                act.wait_ge(*read_out(s(f"W{len(LEVELS) - 1}_1")))
                nc.scalar.activation(region(b_x, TT, G), reg("B", "RG"), ACT.Sigmoid)
                nc.scalar.activation(region(b_x + 1024, TT, G), reg("B", "DZ"), ACT.Sigmoid).then_inc(sig("out_sig"), 1)
                for g in order[moved:]:
                    move(s(g), ACT.Sigmoid)
                for dst, src in ((g_ro, w["ret_out_norm_2"][l:l + 1]), (g_mp, w["mix_post_norm_2"][l:l + 1]),
                                 (g_fp, w["ffn_post_norm_2"][l:l + 1])):
                    act.dma_start(dst, src.to_broadcast([P, dst.shape[1]])).then_inc(loaded["late"], 16)
                act.wait_ge(sig("mix_sum"), 2 * l + 2)
                result((s("M0"), s("M1")), DEPTH + 2 * l, parts_until(last_unit(s("M1"))) + 2)
                for j in range(FF_G):
                    round_weights(parts_until(last_unit(s(f"F{j}")) + AHEAD))
                    if j >= 2:
                        act.wait_ge(sig("hid_split"), FF_G * l + j - 1)
                    act.wait_ge(*summed(s(f"F{j}")))
                    nc.scalar.activation(sg[:, j % 2].rearrange("p c s -> p (c s)"), group_bank(s(f"F{j}"), 0), ACT.Sigmoid)\
                        .then_inc(sig("ff_sig"), 1)
                round_weights(parts_until(last_unit(s("E1"))))
                result((s("E0"), s("E1")), DEPTH + 2 * l + 1, parts_until(last_unit(s("E1")) + 1))

        @block.vector
        def _(dve):
            chain = [0]

            def v(ins):
                chain[0] += 1
                ins.then_inc(v_chain, 1)
                dve.wait_ge(v_chain, chain[0])

            def evac(ins, step):
                ins.then_inc(step_read[STEP_NO[step] % 4], 1)
                dve.wait_ge(*read_out(step))

            def mul(o, i0, i1):
                return nc.vector.tensor_tensor(o, i0, i1, ALU.mult)

            def add(o, i0, i1):
                return nc.vector.tensor_tensor(o, i0, i1, ALU.add)

            def sub(o, i0, i1):
                return nc.vector.tensor_tensor(o, i0, i1, ALU.subtract)

            def rstd(src, n, scale, eps):
                pow_widths.append(n)
                nc.vector.tensor_scalar(rs_in[:, 0:n], src, scale, eps, ALU.mult, ALU.add).then_inc(pow_asked, 1)
                dve.wait_ge(pow_given, len(pow_widths))
                return rs_out[:, 0:n]

            halved = [0]

            def weight_rests(count):
                while halved[0] < count:
                    u, k, nk = PARTS[halved[0]]
                    dve.wait_ge(w_rounded, halved[0] + 1)
                    sub(wt_rest[:, u % SLOTS, k:k + nk, :], wt[:, u % SLOTS, k:k + nk, :], rounded_part(u)[:, k:k + nk, :].bitcast(F))\
                        .then_inc(w_split, 1)
                    halved[0] += 1

            def over(v2, n, d):
                return v2[:, :, None].to_broadcast([P, n, d])

            def head_norm(vw, n, d, gain, scale, eps, tmp2):
                v(mul(tmp2, vw, vw))
                v(nc.vector.tensor_reduce(small[:, 420:420 + n], tmp2, X, ALU.add))
                r = rstd(small[:, 420:420 + n], n, scale, eps)
                v(mul(vw, vw, over(r, n, d)))
                if gain is not None:
                    v(mul(vw, vw, gain))

            def absolute(o, i):
                return nc.vector.scalar_tensor_tensor(o, i, -1.0, i, ALU.mult, ALU.max)

            def copy(o, i):
                return nc.vector.tensor_copy(o, i)

            v(nc.vector.memset(minus_half[:, :], -0.5))

            def col(name, l):
                r0, k = COL_A[name]
                return cols[:, r0 + l * k:r0 + (l + 1) * k]
            dve.wait_ge(sig("mem_squared"), 1)
            r = rstd(small[:, 360:362], 2, 1.0 / D, 1e-6)
            mem_in = region(a_S, TT, D)
            v(nc.vector.tensor_scalar(mem_in[:, 0], mem_in[:, 0], r[:, 0:1], None, ALU.mult))
            nc.vector.tensor_scalar(mem_in[:, 1], mem_in[:, 1], r[:, 1:2], None, ALU.mult).then_inc(sig("mem_normed"), 1)
            for i in range(4):
                t, q = divmod(i, 2)
                dve.wait_ge(*computed(f"memT{i}"))
                evac(copy(mem_hat[:, t, 4 * q:4 * q + 4, :], bank(f"memT{i}", 4, P)), f"memT{i}")
            dve.wait_ge(*computed("colA"))
            evac(copy(cols[:, 0:COL_A_ROWS], bank("colA", COL_A_ROWS)), "colA")
            dve.wait_ge(*computed("colB"))
            evac(copy(cols[:, COL_A_ROWS:], bank("colB", COL_B_ROWS)), "colB")

            def rotation_and_zeros():
                dve.wait_ge(loaded["ident"], 16)
                dve.wait_ge(loaded["gain1"], 16 * (1 + 7 * DEPTH))
                pf, ang, turns = small[:, 288:290], small[:, 304:320].rearrange("p (t j) -> p t j", t=2), small[:, 352:360]
                an = small[:, 304:320]
                red, co, tr = small[:, 320:336], small[:, 336:352], small[:, 440:456]
                v(nc.vector.tensor_scalar(pf, pos[:, :], 1.0, None, ALU.mult))
                v(mul(ang, pf[:, :, None].to_broadcast([P, 2, ROT]), C("inv_freq")[:, None, :].to_broadcast([P, 2, ROT])))
                v(nc.vector.tensor_scalar(tr, an, float(1 / (2 * np.pi)), ROUND_MAGIC, ALU.mult, ALU.add))
                v(nc.vector.tensor_scalar(tr, tr, ROUND_MAGIC, None, ALU.subtract))
                v(nc.vector.scalar_tensor_tensor(red, tr, -TWO_PI_PARTS[0], an, ALU.mult, ALU.add))
                v(nc.vector.scalar_tensor_tensor(red, tr, -TWO_PI_PARTS[1], red, ALU.mult, ALU.add))
                v(nc.vector.scalar_tensor_tensor(red, tr, -TWO_PI_PARTS[2], red, ALU.mult, ALU.add))
                v(nc.vector.tensor_scalar(red, red, 3.1415925, -3.1415925, ALU.min, ALU.max))
                v(nc.vector.scalar_tensor_tensor(co, red, -1.0, red, ALU.mult, ALU.min))
                nc.vector.tensor_scalar(co, co, float(np.pi / 2), None, ALU.add).then_inc(sig("angles"), 1)
                dve.wait_ge(sig("rot_ready"), 1)
                v(copy(rot[:, :, 2:4, :], rot[:, :, 0:2, :]))
                v(nc.vector.memset(QT, 0.0))
                v(nc.vector.memset(region(a_qm, 4096), 0.0))
                v(nc.vector.memset(restart, 1.0))
                v(nc.vector.memset(restart.rearrange("p (c i) -> p c i", i=64)[:, :, 0:1], 0.0))
                dve.wait_ge(loaded["const"], 16)

            def normed_T(step, src_gain, dst):
                dve.wait_ge(*computed(step))
                evac(mul(dst, bank(step, 4, P), src_gain[:, :, None].to_broadcast([P, 4, P])), step)

            def norm_tile(n, t, dst):
                dve.wait_ge(sig("x_sq"), 2 * n + t + 1)
                r = rstd(small[:, 360 + t:361 + t], 1, 1.0 / D, 1e-6)
                nc.vector.tensor_scalar(dst[:, t], x[:, t], r[:, 0:1], None, ALU.mult).then_inc(sig("x_normed"), 1)

            def scale_memory(l):
                for t in range(TT):
                    ins = mul(mem_s[:, t], mem_hat[:, t], col("mem_norm_g", l)[:, :, None].to_broadcast([P, KD, P]))
                ins.then_inc(sig("mem_scaled"), 1)

            for l in range(DEPTH):
                s = lambda n: f"A{l}.{n}"
                if l == 0:
                    scale_memory(0)
                    for t in range(TT):
                        norm_tile(0, t, xs)
                for i in range(4):
                    t, q = divmod(i, 2)
                    normed_T(s(f"xT{i}"), col("norm_g", l)[:, 4 * q:4 * q + 4], hT[:, t, 4 * q:4 * q + 4, :])

                def group_in(g):
                    n = GROUP_NO[s(g)]
                    return group_read[n % 2], n // 2 + 1
                if l == 0:
                    rotation_and_zeros()
                dve.wait_ge(*group_in("KM"))
                km = heads(reg("A", "KM"))
                v(mul(sq[:, 0:1024].rearrange("p (n d) -> p n d", n=8), km, km))
                v(nc.vector.tensor_reduce(small[:, 420:428], sq[:, 0:1024].rearrange("p (n d) -> p n d", n=8), X, ALU.add))
                r = rstd(small[:, 420:428], 8, 1.0 / P, 1e-6)
                v(mul(km, km, over(r, 8, P)))
                mul(km, km, g_mk[:, l][:, None, :].to_broadcast([P, 8, P])).then_inc(sig("km_normed"), 1)
                for t in range(TT):
                    dve.wait_ge(*computed(s(f"kmT{t}")))
                    evac(copy(reg("A", "KM")[:, t, :], bank(s(f"kmT{t}"))), s(f"kmT{t}"))
                v(nc.vector.memset(hst, 0.0))
                dve.wait_ge(sig("hg_q_sig"), l + 1)
                mul(qs.rearrange("p (b c) s -> p b (c s)", b=2), group_banks(s("QH")), etmp.rearrange("p (b c) s -> p b (c s)", b=2))\
                    .then_inc(group_read[GROUP_NO[s("QH")] % 2], 1)
                dve.wait_ge(*taken(s("QH")))
                dve.wait_ge(*taken(s("FH")))
                absolute(dtmp, cum).then_inc(sig("hg_f_in"), 1)
                dve.wait_ge(sig("hg_ln"), l + 1)
                v(nc.vector.scalar_tensor_tensor(etmp, cum, 0.0, dtmp, ALU.min, ALU.subtract))
                if l > 0:
                    v(add(etmp, etmp, lbs[:, 4:8][:, :, None].to_broadcast([P, NH, S])))
                    v(sub(dtmp, etmp, lbs[:, 0:4][:, :, None].to_broadcast([P, NH, S])))
                    absolute(dtmp, dtmp).then_inc(sig("hg_lb_in"), 1)
                    v(nc.vector.tensor_tensor(etmp, etmp, lbs[:, 0:4][:, :, None].to_broadcast([P, NH, S]), ALU.max))
                    v(mul(ks, ks, lbs[:, 8:12][:, :, None].to_broadcast([P, NH, S])))
                    dve.wait_ge(sig("hg_lb_ln"), l)
                    v(add(etmp, etmp, dtmp))
                nc.vector.tensor_tensor_scan(cum.rearrange("p h s -> p (h s)"), restart, etmp.rearrange("p h s -> p (h s)"),
                                             0.0, ALU.mult, ALU.add).then_inc(sig("hg_factors"), 1)
                dve.wait_ge(sig("hg_factors"), 9 * l + 1)

                def factors(n):
                    m = 2 ** (n - 1)
                    q2, k2 = qmul[n % 2], kmul[n % 2]
                    ends = cum.rearrange("p h (c i) -> p h c i", i=64)[:, :, :, 63:64].rearrange("p h c o -> p h (c o)")
                    if n <= 6:
                        b = cum.rearrange("p h (b m) -> p (h b) m", m=2 * m)
                        dv = dtmp.rearrange("p h (b m) -> p (h b) m", m=2 * m)
                        sub(dv, b, b[:, :, m - 1:m].to_broadcast([P, 1024 // (2 * m), 2 * m])).then_inc(sig("hg_diff"), 1)
                    else:
                        c4 = cum.rearrange("p h (c i) -> p (h c) i", i=64)
                        d4 = dtmp.rearrange("p h (c i) -> p (h c) i", i=64)
                        if n == 7:
                            v(copy(d4[:, 1::2, :], c4[:, 1::2, :]))
                            sub(d4[:, 0::2, :], c4[:, 0::2, :], c4[:, 0::2, 63:64].to_broadcast([P, 8, 64])).then_inc(sig("hg_diff"), 1)
                        else:
                            c5 = cum.rearrange("p h (c i) -> p h c i", i=64)
                            d5 = dtmp.rearrange("p h (c i) -> p h c i", i=64)
                            two = small[:, 472:476][:, :, None]
                            v(add(two, c5[:, :, 0, 63:64], c5[:, :, 1, 63:64]))
                            v(copy(d5[:, :, 2, :], c5[:, :, 2, :]))
                            v(add(d5[:, :, 3, :], c5[:, :, 3, :], c5[:, :, 2, 63:64].to_broadcast([P, NH, 64])))
                            v(sub(d5[:, :, 1, :], c5[:, :, 1, :], c5[:, :, 1, 63:64].to_broadcast([P, NH, 64])))
                            sub(d5[:, :, 0, :], c5[:, :, 0, :], two.to_broadcast([P, NH, 64])).then_inc(sig("hg_diff"), 1)
                    dve.wait_ge(sig("hg_exp"), 8 * l + n)
                    mm = min(m, P)

                    def half(z, right):
                        z2 = z.rearrange("p h (b m) -> p (h b) m", m=2 * mm)
                        return z2[:, :, mm:] if right else z2[:, :, 0:mm]
                    v(mul(half(k2, False), half(ks, False), half(etmp, False)))
                    mul(half(q2, True), half(qs, True), half(etmp, True)).then_inc(sig("hg_factors"), 1)
                    dve.wait_ge(sig("hg_factors"), 9 * l + n + 1)

                def collect(n):
                    for t in (range(TT) if n < 8 else (1,)):
                        st = s(f"hg{n}_{t}")
                        dve.wait_ge(*computed(st))
                        if n == 8:
                            evac(copy(hst_off, bank(st, NH, P)), st)
                            continue
                        mask = (ident if n == 0 else level[:, n - 1, :]).bitcast(mybir.dt.uint32)
                        evac(nc.vector.copy_predicated(hst[:, t], mask[:, None, :].to_broadcast([P, NH, P]), bank(st, NH, P)), st)
                factors(1)
                collect(0)
                factors(2)
                collect(1)
                factors(3)
                dve.wait_ge(*group_in("QA"))
                dve.wait_ge(*group_in("KA"))
                qk = region(R1["QA"], 32, DH_A)
                head_norm(qk, 32, DH_A, None, 1.0 / DH_A, 1e-6, sq.rearrange("p (n d) -> p n d", n=32))
                qk2 = region(R1["QA"], 2, 16, DH_A)
                v(mul(qk2, qk2, g_qk[:, l][:, :, None, :].to_broadcast([P, 2, 16, DH_A])))
                collect(2)
                factors(4)
                collect(3)
                qkr = region(R1["QA"], 4, NH_A, DH_A)
                x1, x2 = qkr[:, :, :, 0:ROT], qkr[:, :, :, ROT:2 * ROT]
                cosv, sinv = (rot[:, i][:, :, None, :].to_broadcast([P, 4, NH_A, ROT]) for i in range(2))
                ta, tb = (sq[:, 256 * i:256 * i + 256].rearrange("p (a h j) -> p a h j", a=4, h=NH_A) for i in range(2))
                v(mul(ta, x1, sinv))
                v(mul(tb, x2, sinv))
                v(mul(x1, x1, cosv))
                v(sub(x1, x1, tb))
                v(mul(x2, x2, cosv))
                add(x2, x2, ta).then_inc(sig("qk_rotated"), 1)
                factors(5)
                collect(4)
                for t in range(TT):
                    st = s(f"qaT{t}")
                    dve.wait_ge(*computed(st))
                    v(copy(QT[0:64, 0:8:2, t * P:t * P + P], bank(st, 4, P)[0:64]))
                    evac(copy(QT[64:128, 1:8:2, t * P:t * P + P], bank(st, 4, P)[64:128]), st)
                for t in range(TT):
                    dve.wait_ge(*computed(s(f"kaT{t}")))
                    evac(copy(KT[:, :, t * P:t * P + P], bank(s(f"kaT{t}"), 4, P)), s(f"kaT{t}"))

                def attn_scores(h0):
                    for h in range(h0, h0 + 4):
                        dve.wait_ge(*computed(s(f"sc{h}")))
                        evac(nc.vector.scalar_tensor_tensor(sco[:, h, :], bank(s(f"sc{h}"), 384), DH_A ** -0.5, C("causal"),
                                                            ALU.mult, ALU.add), s(f"sc{h}"))
                    v(nc.vector.tensor_reduce(small[:, 368 + h0:372 + h0], sco[:, h0:h0 + 4, 0:P], X, ALU.max, negate=True))
                    nc.vector.tensor_reduce(small[:, 376 + h0:380 + h0], sco[:, h0:h0 + 4, P:3 * P], X, ALU.max, negate=True)\
                        .then_inc(sig("attn_max"), 1)
                factors(6)
                collect(5)
                attn_scores(0)
                factors(7)
                collect(6)
                attn_scores(4)
                factors(8)
                collect(7)
                collect(8)
                for h in range(8):
                    dve.wait_ge(*computed(s(f"pt{h}")))
                    evac(copy(prT[:, h, :], bank(s(f"pt{h}"), 384)), s(f"pt{h}"))
                v(nc.vector.reciprocal(small[:, 384:400], small[:, 384:400]))

                def gate(j, o):
                    dve.wait_ge(sig("z_sig"), 3 * l + j + 1)
                    z = reg("A", f"Z{j}")
                    v(mul(z, z, region(a_memT, TT, G)))
                    mul(z, z, o).then_inc(sig("y_ready"), 1)
                    dve.wait_ge(sig("y_ready"), 3 * l + j + 1)
                for t in range(TT):
                    st = s(f"oa{t}")
                    dve.wait_ge(*computed(st))
                    evac(mul(o_tmp[:, t].rearrange("p (h d) -> p h d", h=NH_A), bank(st, NH_A, DH_A),
                             over(small[:, 384 + 8 * t:392 + 8 * t], NH_A, DH_A)), st)
                dve.wait_ge(*group_in("QM"))
                qm = heads(reg("A", "QM"))
                sq8 = region(a_B, 8, P)
                v(mul(sq8, qm, qm))
                v(nc.vector.tensor_reduce(small[:, 420:428], sq8, X, ALU.add))
                r = rstd(small[:, 420:428], 8, 1.0 / P, 1e-6)
                v(mul(qm, qm, over(r, 8, P)))
                mul(qm, qm, g_mq[:, l][:, None, :].to_broadcast([P, 8, P])).then_inc(sig("qm_normed"), 1)
                gate(0, o_tmp)
                for t in range(TT):
                    dve.wait_ge(*computed(s(f"qmT{t}")))
                    evac(copy(reg("A", "QM")[:, t, :], bank(s(f"qmT{t}"))), s(f"qmT{t}"))
                for h in range(NH):
                    dve.wait_ge(*computed(s(f"ms{h}")))
                    mxv = small[:, 400:408].rearrange("p (t h) -> p t h", t=2)[:, :, h:h + 1]
                    v(nc.vector.tensor_reduce(mxv, bank(s(f"ms{h}"), TT, MEM), X, ALU.max, negate=True))
                    nc.vector.tensor_scalar(mxv, mxv, P ** -0.5, None, ALU.mult).then_inc(sig("mem_max"), 1)
                for t in range(TT):
                    dve.wait_ge(*computed(s(f"hgo{t}")))
                    evac(copy(o_tmp[:, t, :], bank(s(f"hgo{t}"))), s(f"hgo{t}"))
                ov = heads(o_tmp)
                head_norm(ov, 8, P, g_ho[:, l][:, None, :].to_broadcast([P, 8, P]), 1.0 / P, 1e-6, sq8)
                gate(1, o_tmp)
                for h in range(NH):
                    dve.wait_ge(*computed(s(f"mpt{h}")))
                    evac(copy(mprT[:, h], bank(s(f"mpt{h}"), 4, P)), s(f"mpt{h}"))
                v(nc.vector.reciprocal(small[:, 408:416], small[:, 408:416]))
                for t in range(TT):
                    st = s(f"om{t}")
                    dve.wait_ge(*computed(st))
                    evac(mul(o_tmp[:, t].rearrange("p (h d) -> p h d", h=NH), bank(st, NH, P),
                             over(small[:, 408 + 4 * t:412 + 4 * t], NH, P)), st)
                gate(2, o_tmp)
                for i in range(6):
                    j, t = divmod(i, 2)
                    dve.wait_ge(*computed(s(f"yT{i}")))
                    evac(copy(reg("A", f"Z{j}")[:, t, :], bank(s(f"yT{i}"))), s(f"yT{i}"))
                if l == 0:
                    dd, e = small[:, 480:488], small[:, 488:496]
                    v(sub(dd[:, 0:4], col("lb", 1), col("lb", 0)))
                    v(sub(dd[:, 4:8], col("lb", 0), col("lb", 1)))
                    absolute(e, dd).then_inc(sig("lb_in"), 1)
                    scale_memory(l + 1)
                dve.wait_ge(*summed(s("O0")))
                add(x[:, :, 0:G], x[:, :, 0:G], group_banks(s("O0"))).then_inc(group_read[GROUP_NO[s("O0")] % 2], 1)
                dve.wait_ge(*taken(s("O0")))
                for t in range(TT):
                    dve.wait_ge(*((sig("first_tile"), l + 1) if t == 0 else summed(s("O1"))))
                    add(x[:, t, G:], x[:, t, G:], group_bank(s("O1"), t)).then_inc(sig("x_tile"), 1)
                    if t == TT - 1:
                        dve.wait_ge(sig("x_tile"), 2 * (l + 1))
                        nc.vector.memset(small[:, 476:477], 0.0).then_inc(group_read[GROUP_NO[s("O1")] % 2], 1)
                    norm_tile(l + 1, t, xs if l + 1 < DEPTH else xs2)
                if l == 0:
                    dve.wait_ge(sig("lb_ln"), 1)
                    v(nc.vector.scalar_tensor_tensor(lbs[:, 0:8], dd, 0.0, small[:, 496:504], ALU.min, ALU.subtract))
                    dve.wait_ge(sig("lb_sig"), 1)

            for l in range(DEPTH):
                s = lambda n: f"B{l}.{n}"

                def group_in(g):
                    n = GROUP_NO[s(g)]
                    return group_read[n % 2], n // 2 + 1

                def x_out(prefix, gain, i):
                    t, q = divmod(i, 2)
                    normed_T(s(f"{prefix}{i}"), col(gain, l)[:, 4 * q:4 * q + 4], hT[:, t, 4 * q:4 * q + 4, :])

                def add_result(names, gain, n, between, parts=0):
                    for t in range(TT):
                        if t == 1:
                            weight_rests(parts)
                        dve.wait_ge(sig("res_sq"), 2 * (n - DEPTH) + t + 1)
                        v(add(small[:, 420:421], small[:, 364 + t:365 + t], small[:, 366 + t:367 + t]))
                        r = rstd(small[:, 420:421], 1, 1.0 / D, 1e-6)
                        for j in range(2):
                            ins = nc.vector.scalar_tensor_tensor(mres[:, t, G * j:G * j + G], group_bank(names[j], t), r[:, 0:1],
                                                                 gain[:, G * j:G * j + G], ALU.mult, ALU.mult)
                            if t == TT - 1:
                                ins.then_inc(group_read[GROUP_NO[names[j]] % 2], 1)
                                dve.wait_ge(*taken(names[j]))
                            else:
                                v(ins)
                        add(x[:, t], x[:, t], mres[:, t]).then_inc(sig("x_tile"), 1)
                        if t == 1 and between is not None:
                            between()
                        if n + 1 < 3 * DEPTH:
                            norm_tile(n + 1, t, xs2)
                def rests_until(i):
                    weight_rests(parts_until(first_unit(s("Q")) + i))

                def split_mixer_h(t):
                    v(copy(mix_hT_hi[:, t], hT[:, t]))
                    sub(mix_hT_rest[:, t], hT[:, t], mix_hT_hi[:, t].bitcast(F)).then_inc(sig("h_split"), 1)
                if l == 0:
                    for i in range(2):
                        x_out("xT", "mix_pre", i)
                split_mixer_h(0)
                if l > 0:
                    rests_until(0)
                for i in range(2, 4):
                    x_out("xT", "mix_pre", i)
                split_mixer_h(1)
                rests_until(7)
                dve.wait_ge(*computed(s("ba")))
                ba = bank(s("ba"), 2, 8)
                v(copy(small[:, 24:32].rearrange("p (t h) -> p t h", t=2), ba[:, :, 0:4]))
                evac(add(small[:, 104:112].rearrange("p (t h) -> p t h", t=2), ba[:, :, 4:8],
                         dt_bias[:, l][:, None, :].to_broadcast([P, 2, 4])), s("ba"))
                absolute(small[:, 32:40], small[:, 104:112]).then_inc(sig("ba_in"), 1)
                dve.wait_ge(sig("gate_parts"), l + 1)
                gates = small[:, 0:8]
                gates2 = gates.rearrange("p (t h) -> p t h", t=2)
                v(nc.vector.scalar_tensor_tensor(gates, small[:, 104:112], 0.0, small[:, 40:48], ALU.max, ALU.add))
                v(nc.vector.scalar_tensor_tensor(gates2, gates2, -1.0, small[:, 48:52][:, None, :].to_broadcast([P, 2, 4]), ALU.mult, ALU.mult))
                copy(gbc, gates[:, :, None].to_broadcast([P, 8, P])).then_inc(sig("gates_ready"), 1)
                rests_until(8)
                taps = cols[:, COL_A_ROWS + 48 * l:COL_A_ROWS + 48 * (l + 1)].rearrange("p (w k) -> p w k", w=4)
                for j in range(3):
                    dve.wait_ge(*group_in("QKV"[j]))
                    for k in range(4 * j, 4 * j + 4):
                        ins = nc.vector.tensor_scalar(cT3[:, k, :], xT3[:, k, :], taps[:, 3, k:k + 1], None, ALU.mult)
                    for d in (1, 2, 3):
                        v(ins)
                        for k in range(4 * j, 4 * j + 4):
                            ins = nc.vector.scalar_tensor_tensor(cT3[:, k, d:], xT3[:, k, 0:S - d], taps[:, 3 - d, k:k + 1], cT3[:, k, d:],
                                                                 ALU.mult, ALU.add)
                    ins.then_inc(sig("conv_in"), 1)
                    rests_until(9 + j)
                for j in range(3):
                    dve.wait_ge(sig("conv_sig"), 3 * l + j + 1)
                    ins = mul(cT3s(j), cT3s(j), e3[:, 4 * j:4 * j + 4, :])
                ins.then_inc(sig("conv_done"), 1)
                dve.wait_ge(sig("conv_done"), l + 1)
                rests_until(12)
                dve.wait_ge(*computed(s("cg")))
                v(copy(small[:, 56:64], bank(s("cg"))[:, 0:8]))
                evac(sub(small[:, 64:72], bank(s("cg"))[:, 8:16], small[:, 56:64]), s("cg"))
                dve.wait_ge(*computed(s("gb0")))
                evac(sub(yl[:, 0], bank(s("gb0"), NH, P), over(small[:, 56:60], NH, P)), s("gb0"))
                dve.wait_ge(*computed(s("gb1")))
                v(sub(yl[:, 1], bank(s("gb1"), NH, P), over(small[:, 60:64], NH, P)))
                nc.vector.tensor_scalar(yl, yl, 0.0, None, ALU.min).then_inc(sig("decay_in"), 1)
                for j, g in enumerate("QKV"):
                    for t in range(TT):
                        dve.wait_ge(*computed(s(f"bT{j}{t}")))
                        evac(copy(reg("B", g)[:, t, :], bank(s(f"bT{j}{t}"))), s(f"bT{j}{t}"))
                rests_until(13)
                qk = region(R2["Q"], 16, P)
                qv, kv, vv = (heads(reg("B", g)) for g in "QKV")
                sq16 = sq2.rearrange("p (n d) -> p n d", n=16)
                v(mul(sq16, qk, qk))
                v(nc.vector.tensor_reduce(small[:, 420:436], sq16, X, ALU.add))
                r = rstd(small[:, 420:436], 16, 1.0, 1e-6)
                v(nc.vector.tensor_scalar(small[:, 420:428], r[:, 0:8], P ** -0.5, None, ALU.mult))
                v(mul(qv, qv, over(small[:, 420:428], 8, P)))
                v(mul(kv, kv, over(r[:, 8:16], 8, P)))
                dve.wait_ge(sig("beta_ready"), l + 1)
                kb8 = kb.rearrange("p t h d -> p (t h) d")
                v(mul(vv, vv, over(small[:, 16:24], 8, P)))
                mul(kb8, kv, over(small[:, 16:24], 8, P)).then_inc(sig("dn_normed"), 1)
                rests_until(14)
                dve.wait_ge(sig("decay_exp"), l + 1)
                v(mul(decT.rearrange("p t h i -> p (t h) i"), yl.rearrange("p t h i -> p (t h) i"), upper[:, None, :].to_broadcast([P, 8, P])))
                dve.wait_ge(*read_out(s("gb1")))
                v(mul(ktl, kv[:, 0:4, :], over(small[:, 88:92], NH, P)))
                for n, dst in (("kT", kT), ("qT", qT), ("kbT", kbT)):
                    for t in range(TT):
                        dve.wait_ge(*computed(s(f"{n}{t}")))
                        evac(copy(dst[:, t], bank(s(f"{n}{t}"), NH, P)), s(f"{n}{t}"))
                v(mul(kb[:, 1], kb[:, 1], over(small[:, 84:88], NH, P)))
                v(mul(qd, qT[:, 1], eg))
                for n, dst in (("mm", mT), ("at", atT)):
                    for t in range(TT):
                        dve.wait_ge(*computed(s(f"{n}{t}")))
                        evac(mul(dst[:, t], bank(s(f"{n}{t}"), NH, P), decT[:, t]), s(f"{n}{t}"))
                iv, ivT = (z.rearrange("p t h i -> p (t h) i") for z in (inv, invT))
                v(copy(iv, ident[:, None, :].to_broadcast([P, 8, P])))
                v(copy(ivT, ident[:, None, :].to_broadcast([P, 8, P])))

                def level_mask(n):
                    mul(ml.rearrange("p t h i -> p (t h) i"), mT.rearrange("p t h i -> p (t h) i"),
                        level[:, n, :][:, None, :].to_broadcast([P, 8, P])).then_inc(sig("inv_ready"), 1)
                    dve.wait_ge(sig("inv_ready"), len(LEVELS) * l + n + 1)
                level_mask(0)
                for n in range(len(LEVELS)):
                    rests_until(15 + 2 * n)
                    if n < len(LEVELS) - 1:
                        for t in range(TT):
                            st = s(f"Z{n}_{t}")
                            dve.wait_ge(*computed(st))
                            evac(sub(inv[:, t], inv[:, t], bank(st, NH, P)), st)
                    for t in range(TT):
                        st = s(f"W{n}_{t}")
                        dve.wait_ge(*computed(st))
                        evac(sub(invT[:, t], invT[:, t], bank(st, NH, P)), st)
                    if n < len(LEVELS) - 1:
                        level_mask(n + 1)
                    if n == 0:
                        rests_until(16)
                        dve.wait_ge(*group_in("RQ"))
                        dve.wait_ge(*group_in("RK"))
                        rr = region(R2["RQ"], 4, NH, P)
                        x1, x2 = rr[:, :, :, 0:64], rr[:, :, :, 64:P]
                        cosv, sinv = (C(n_).rearrange("p (a j) -> p a j", a=4)[:, :, None, :].to_broadcast([P, 4, NH, 64]) for n_ in ("cos", "sin"))
                        ta = region(R2["G0"], 4, NH, 64)
                        tb = region(R2["G1"], 4, NH, 64)
                        v(mul(ta, x1, sinv))
                        v(mul(tb, x2, sinv))
                        v(mul(x1, x1, cosv))
                        v(sub(x1, x1, tb))
                        v(mul(x2, x2, cosv))
                        add(x2, x2, ta).then_inc(sig("ret_rotated"), 1)
                rests_until(29)
                for t in range(TT):
                    dve.wait_ge(*computed(s(f"do{t}")))
                    evac(copy(reg("B", "Q")[:, t, :], bank(s(f"do{t}"))), s(f"do{t}"))
                for g, n in (("RQ", "rqT"), ("RK", "rkT")):
                    for t in range(TT):
                        dve.wait_ge(*computed(s(f"{n}{t}")))
                        evac(copy(reg("B", g)[:, t, :], bank(s(f"{n}{t}"))), s(f"{n}{t}"))
                for i in range(3):
                    dve.wait_ge(*computed(s(f"rs{i}")))
                    evac(mul(rst[:, i], bank(s(f"rs{i}"), NH, P), decay_c[:, i % 2]), s(f"rs{i}"))
                for t in range(TT):
                    dve.wait_ge(*computed(s(f"ro{t}")))
                    evac(copy(reg("B", "RQ")[:, t, :], bank(s(f"ro{t}"))), s(f"ro{t}"))
                for i in range(2):
                    dve.wait_ge(*computed(s(f"pm{i}")))
                    evac(copy(mx[:, 2 * i:2 * i + 2, :], bank(s(f"pm{i}"), 2, S)), s(f"pm{i}"))
                po = region(R2["PU"], 4, S)
                for i in range(2):
                    dve.wait_ge(*computed(s(f"py{i}")))
                    evac(mul(po[:, 2 * i:2 * i + 2, :], bank(s(f"py{i}"), 2, S),
                             col("pool_scale", l)[:, 2 * i:2 * i + 2][:, :, None].to_broadcast([P, 2, S])), s(f"py{i}"))
                dve.wait_ge(loaded["early"], 16 * 2 * (l + 1))
                dve.wait_ge(loaded["late"], 16 * 3 * (l + 1))
                ro = heads(reg("B", "RQ"))
                t8 = tmp.rearrange("p (n d) -> p n d", n=8)
                v(nc.vector.tensor_reduce(small[:, 420:428], ro, X, ALU.add))
                v(nc.vector.tensor_scalar(small[:, 420:428], small[:, 420:428], 1.0 / P, None, ALU.mult))
                v(sub(ro, ro, over(small[:, 420:428], 8, P)))
                v(mul(t8, ro, ro))
                v(nc.vector.tensor_reduce(small[:, 420:428], t8, X, ALU.add))
                r = rstd(small[:, 420:428], 8, 1.0 / P, 1e-5)
                v(mul(ro, ro, over(r, 8, P)))
                v(mul(reg("B", "RQ"), reg("B", "RQ"), g_ro[:, None, :].to_broadcast([P, TT, G])))
                dve.wait_ge(sig("out_sig"), l + 1)
                v(mul(reg("B", "RG"), reg("B", "RG"), region(b_x, TT, G)))
                mul(reg("B", "RQ"), reg("B", "RQ"), reg("B", "RG")).then_inc(sig("ret_out"), 1)
                for j in range(2):
                    n = s(f"BP{j}")
                    dve.wait_ge(*summed(n))
                    dve.wait_ge(*group_in(f"G{2 + j}"))
                    gt = reg("B", f"G{2 + j}")
                    mul(gt, gt, group_banks(n)).then_inc(group_read[GROUP_NO[n] % 2], 1)
                for t in range(TT):
                    dve.wait_ge(*computed(s(f"oT_r{t}")))
                    evac(copy(reg("B", "RQ")[:, t, :], bank(s(f"oT_r{t}"))), s(f"oT_r{t}"))
                od = heads(reg("B", "Q"))
                head_norm(od, 8, P, g_do[:, None, :].to_broadcast([P, 8, P]), 1.0 / P, 1e-6, sq2[:, 0:1024].rearrange("p (n d) -> p n d", n=8))
                v(mul(reg("B", "DZ"), reg("B", "DZ"), region(b_x + 1024, TT, G)))
                mul(reg("B", "Q"), reg("B", "Q"), reg("B", "DZ")).then_inc(sig("dn_out"), 1)

                def add_branch(b, g0, done):
                    for j in range(2):
                        n = s(f"{b}{j}")
                        dve.wait_ge(*summed(n))
                        gt = reg("B", f"G{g0 + j}")
                        mul(gt, gt, group_banks(n)).then_inc(group_read[GROUP_NO[n] % 2], 1)
                        dve.wait_ge(*taken(n))
                        acc = reg("B", f"G{2 + j}")
                        ins = add(acc, acc, gt)
                        if done:
                            ins.then_inc(sig("mix_sum"), 1)
                        else:
                            v(ins)
                add_branch("BR", 4, False)
                for t in range(TT):
                    dve.wait_ge(*computed(s(f"oT_d{t}")))
                    evac(copy(reg("B", "Q")[:, t, :], bank(s(f"oT_d{t}"))), s(f"oT_d{t}"))
                add_branch("BD", 0, True)
                for i in range(4):
                    j, t = divmod(i, 2)
                    dve.wait_ge(*computed(s(f"yT{i}")))
                    evac(copy(reg("B", f"G{2 + j}")[:, t, :], bank(s(f"yT{i}"))), s(f"yT{i}"))
                def first_tile_out(prefix, gain):
                    for i in range(2):
                        x_out(prefix, gain, i)
                add_result((s("M0"), s("M1")), g_mp, DEPTH + 2 * l, lambda: first_tile_out("fT", "ffn_pre"),
                           parts_until(last_unit(s("M1"))) + 2)

                def split_h(t):
                    v(copy(hT_hi[:, t], hT[:, t]))
                    sub(hT_rest[:, t], hT[:, t], hT_hi[:, t].bitcast(F)).then_inc(sig("h_split"), 1)
                split_h(0)
                for i in range(2, 4):
                    x_out("fT", "ffn_pre", i)
                split_h(1)
                for j in range(FF_G):
                    n = s(f"F{j}")
                    weight_rests(parts_until(last_unit(n) + AHEAD))
                    dve.wait_ge(sig("ff_sig"), FF_G * l + j + 1)
                    sgj = sg[:, j % 2].rearrange("p c s -> p (c s)")
                    v(mul(sgj, sgj, group_bank(n, 0)))
                    mul(sgj, sgj, group_bank(n, 1)).then_inc(group_read[GROUP_NO[n] % 2], 1)
                    dve.wait_ge(*taken(n))
                    v(copy(hid_hi[:, j], sg[:, j % 2]))
                    sub(hid_rest[:, j], sg[:, j % 2], hid_hi[:, j].bitcast(F)).then_inc(sig("hid_split"), 1)
                weight_rests(parts_until(last_unit(s("E1"))))

                def next_first_tile_out():
                    for i in range(2):
                        t, q = divmod(i, 2)
                        normed_T(f"B{l + 1}.xT{i}", col("mix_pre", l + 1)[:, 4 * q:4 * q + 4], hT[:, t, 4 * q:4 * q + 4, :])
                add_result((s("E0"), s("E1")), g_fp, DEPTH + 2 * l + 1, next_first_tile_out if l + 1 < DEPTH else None)

        @block.gpsimd
        def _(pool):
            for n, width in enumerate(pow_widths):
                pool.wait_ge(pow_asked, n + 1)
                nc.gpsimd.tensor_tensor(rs_out[:, 0:width], rs_in[:, 0:width], minus_half[:, 0:width], ALU.pow).then_inc(pow_given, 1)


INS = ["x", "mem", "positions", "norm_g", "w_in", "w_out", "moba_q_norm", "moba_k_norm", "hgrn_lb_logits",
       "hgrn_o_norm", "mem_norm_g", "w_mem_kv", "mem_q_norm", "mem_k_norm", "mix_pre_norm_2", "mix_post_norm_2",
       "w_in_2", "dn_conv_2", "dn_A_log_2", "dn_dt_bias_2", "dn_out_norm_2", "ret_out_norm_2", "pool_w_2",
       "pool_scale_2", "w_branch_dn_2", "w_branch_ret_2", "w_branch_pool_2", "w_out_2", "ffn_pre_norm_2",
       "ffn_post_norm_2", "ffn_gate_2", "ffn_up_2", "ffn_down_2"]


def kernel(**inputs):
    import concourse.bacc as bacc
    from concourse.bass_utils import run_bass_kernel_spmd as run

    nc = bacc.Bacc("TRN2", target_bir_lowering=False, num_devices=1, dynamic_dma_scratch_size=1024)
    arrays = {n: np.ascontiguousarray(inputs[n]) for n in INS}
    arrays["shape_constants"] = shape_constants()
    w = {n: nc.dram_tensor("in_" + n, a.shape, mybir.dt.from_np(a.dtype), kind="ExternalInput").ap() for n, a in arrays.items()}
    out = nc.dram_tensor("out", (1, S, D), mybir.dt.float32, kind="ExternalOutput").ap()
    mixer_program(nc, w, out)
    return run(nc, [{"in_" + n: a for n, a in arrays.items()}], core_ids=[0]).results[0]["out"]
```
